# Optimizing a Trainium2 kernel written in Bass

```python
import jax, jax.numpy as jnp
from jax import lax
import numpy as np

D_MODEL = 1024
BATCH = 1
SEQ = 256
DEPTH = 1

HEAD_DIM = 128
DN_HEADS = 4
DN_WIDTH = DN_HEADS * HEAD_DIM
DN_CONV = 4
DN_CHUNK = 64
MB_HEADS = 4
MB_WIDTH = MB_HEADS * HEAD_DIM
MB_BLOCK = 256
MB_TOPK = 3
MB_QCHUNK = 32
ROPE_THETA = 500000.0
ROPE_DIM = HEAD_DIM // 4
N_EXPERTS = 32
TOP_K = 4
D_FF = D_MODEL
SWIGLU_LIMIT = 7.0
SWIGLU_ALPHA = 1.702
MOE_ROWS = 256
NORM_EPS = 1e-6
IN_SPLITS = (DN_WIDTH, DN_WIDTH, DN_WIDTH, DN_WIDTH, DN_HEADS, DN_HEADS,
             MB_WIDTH, MB_WIDTH, MB_WIDTH, D_MODEL, D_MODEL)
IN_WIDTH = 4 * DN_WIDTH + 2 * DN_HEADS + 3 * MB_WIDTH + 2 * D_MODEL

kernel_name = 'hybrid_deltanet_moba_moe_block'

def rmsnorm(x, g):
    xf = x.astype(jnp.float32)
    y = xf * lax.rsqrt(jnp.mean(xf * xf, axis=-1, keepdims=True) + NORM_EPS)
    return (y * g.astype(jnp.float32)).astype(x.dtype)

def l2norm(x):
    return x * lax.rsqrt(jnp.sum(x * x, axis=-1, keepdims=True) + 1e-6)

def partial_rope(x):
    S = x.shape[1]
    half = ROPE_DIM // 2
    inv_freq = ROPE_THETA ** (-jnp.arange(half, dtype=jnp.float32) / half)
    ang = jnp.arange(S, dtype=jnp.float32)[:, None] * inv_freq[None, :]
    cos = jnp.cos(ang)[None, :, None, :]
    sin = jnp.sin(ang)[None, :, None, :]
    x1 = x[..., :half]
    x2 = x[..., half:ROPE_DIM]
    return jnp.concatenate([x1 * cos - x2 * sin, x2 * cos + x1 * sin, x[..., ROPE_DIM:]], axis=-1)

def causal_depthwise_conv(x, w):
    K, C = w.shape
    return lax.conv_general_dilated(x, w[:, None, :], window_strides=(1,), padding=[(K - 1, 0)],
                                    dimension_numbers=('NWC', 'WIO', 'NWC'), feature_group_count=C)

def gated_delta_rule(q, k, v, g, beta):
    B, S, H, dk = q.shape
    dv = v.shape[-1]
    C = DN_CHUNK
    N = S // C

    def chunks(t):
        t = t.reshape((B, N, C, H) + t.shape[3:])
        return jnp.moveaxis(t, [1, 0, 3, 2], [0, 1, 2, 3])

    q = chunks(q) * (dk ** -0.5)
    k = chunks(k)
    v = chunks(v)
    g = chunks(g)
    beta = chunks(beta)
    gc = jnp.cumsum(g, axis=-1)
    tril = jnp.tril(jnp.ones((C, C), dtype=bool))
    strict = jnp.tril(jnp.ones((C, C), dtype=bool), -1)
    decay = jnp.exp(jnp.where(tril, gc[..., :, None] - gc[..., None, :], -jnp.inf))
    kb = k * beta[..., None]
    L = jnp.where(strict, jnp.einsum('nbhcd,nbhmd->nbhcm', kb, k) * decay, 0.0)
    A = L + jnp.eye(C, dtype=L.dtype)
    u = lax.linalg.triangular_solve(A, v * beta[..., None], left_side=True, lower=True)
    w = lax.linalg.triangular_solve(A, kb * jnp.exp(gc)[..., None], left_side=True, lower=True)
    qk = jnp.einsum('nbhcd,nbhmd->nbhcm', q, k) * decay
    g_last = gc[..., -1]
    k_tail = k * jnp.exp(g_last[..., None] - gc)[..., None]
    q_dec = q * jnp.exp(gc)[..., None]

    def step(state, xs):
        q_n, qk_n, u_n, w_n, kt_n, gl_n = xs
        v_new = u_n - jnp.einsum('bhcd,bhde->bhce', w_n, state)
        o = jnp.einsum('bhcd,bhde->bhce', q_n, state) + jnp.einsum('bhcm,bhme->bhce', qk_n, v_new)
        state = state * jnp.exp(gl_n)[..., None, None] + jnp.einsum('bhcd,bhce->bhde', kt_n, v_new)
        return state, o

    s0 = jnp.zeros((B, H, dk, dv), jnp.float32)
    _, o = lax.scan(step, s0, (q_dec, qk, u, w, k_tail, g_last))
    return jnp.moveaxis(o, [1, 0, 3, 2], [0, 1, 2, 3]).reshape(B, S, H, dv)

def moba_attention(q, k, v):
    B, S, H, d = q.shape
    nb = -(-S // MB_BLOCK)
    Sp = nb * MB_BLOCK
    pad = ((0, 0), (0, Sp - S), (0, 0), (0, 0))
    q, k, v = [jnp.pad(t, pad).transpose(0, 2, 1, 3) for t in (q, k, v)]
    k_blk = k.reshape(B, H, nb, MB_BLOCK, d)
    v_blk = v.reshape(B, H, nb, MB_BLOCK, d)
    k_mean = jnp.mean(k_blk, axis=3)
    pos = jnp.arange(Sp, dtype=jnp.int32)
    q_blk = pos // MB_BLOCK
    past = jnp.arange(nb, dtype=jnp.int32)[None, :] < q_blk[:, None]
    scores = jnp.where(past, jnp.einsum('bhsd,bhnd->bhsn', q, k_mean), -jnp.inf)
    topk = min(MB_TOPK, nb)
    _, top_idx = lax.top_k(scores, topk)
    sel = jnp.concatenate([top_idx.astype(jnp.int32),
                           jnp.broadcast_to(q_blk[:, None], (B, H, Sp, 1))], axis=-1)
    sel_ok = jnp.concatenate([jnp.arange(topk, dtype=jnp.int32)[None, :] < q_blk[:, None],
                              jnp.ones((Sp, 1), dtype=bool)], axis=-1)
    K1 = topk + 1
    nq = Sp // MB_QCHUNK

    def to_chunks(t):
        t = t.reshape(t.shape[:2] + (nq, MB_QCHUNK) + t.shape[3:])
        return jnp.moveaxis(t, 2, 0)

    b_idx = jnp.arange(B)[:, None, None, None]
    h_idx = jnp.arange(H)[None, :, None, None]
    offs = jnp.arange(MB_BLOCK, dtype=jnp.int32)
    scale = d ** -0.5

    def attend(args):
        q_i, sel_i, pos_i, ok_i = args
        k_g = k_blk[b_idx, h_idx, sel_i]
        v_g = v_blk[b_idx, h_idx, sel_i]
        logits = jnp.einsum('bhqd,bhqjkd->bhqjk', q_i, k_g) * scale
        k_pos = sel_i[..., None] * MB_BLOCK + offs
        allowed = (k_pos <= pos_i[:, None, None]) & ok_i[:, :, None]
        logits = jnp.where(allowed, logits, -jnp.inf)
        p = jax.nn.softmax(logits.reshape(logits.shape[:3] + (-1,)), axis=-1).reshape(logits.shape)
        return jnp.einsum('bhqjk,bhqjkd->bhqd', p, v_g)

    o = lax.map(attend, (to_chunks(q), to_chunks(sel), pos.reshape(nq, MB_QCHUNK),
                         sel_ok.reshape(nq, MB_QCHUNK, K1)))
    o = jnp.moveaxis(o, 0, 2).reshape(B, H, Sp, d)[:, :, :S]
    return o.transpose(0, 2, 1, 3)

def hybrid_mixer(h, w_in, conv_w, a_log, dt_bias, g_dn_out, w_br_a, w_br_b, w_o):
    B, S, _ = h.shape
    f32 = jnp.float32
    proj = h @ w_in
    cuts = [int(i) for i in np.cumsum(IN_SPLITS)[:-1]]
    dn_q, dn_k, dn_v, dn_z, dn_b, dn_a, mb_q, mb_k, mb_v, gate_a, gate_b = jnp.split(proj, cuts, axis=-1)

    def heads(t, n):
        return t.reshape(B, S, n, HEAD_DIM)

    qkv = jax.nn.silu(causal_depthwise_conv(jnp.concatenate([dn_q, dn_k, dn_v], axis=-1), conv_w))
    q_a, k_a, v_a = jnp.split(qkv.astype(f32), 3, axis=-1)
    q_a = l2norm(heads(q_a, DN_HEADS))
    k_a = l2norm(heads(k_a, DN_HEADS))
    v_a = heads(v_a, DN_HEADS)
    beta = jax.nn.sigmoid(dn_b.astype(f32))
    g = -jnp.exp(a_log.astype(f32)) * jax.nn.softplus(dn_a.astype(f32) + dt_bias.astype(f32))
    o_a = gated_delta_rule(q_a, k_a, v_a, g, beta)
    o_a = rmsnorm(o_a, g_dn_out) * jax.nn.silu(heads(dn_z.astype(f32), DN_HEADS))
    y_a = o_a.reshape(B, S, DN_WIDTH).astype(h.dtype) @ w_br_a

    q_b = partial_rope(heads(mb_q.astype(f32), MB_HEADS))
    k_b = partial_rope(heads(mb_k.astype(f32), MB_HEADS))
    v_b = heads(mb_v.astype(f32), MB_HEADS)
    o_b = moba_attention(q_b, k_b, v_b)
    y_b = o_b.reshape(B, S, MB_WIDTH).astype(h.dtype) @ w_br_b

    merged = jax.nn.sigmoid(gate_a) * y_a + jax.nn.sigmoid(gate_b) * y_b
    return merged @ w_o

def routed_moe(h, w_router, b_router, w_gu, b_gu, w_down, b_down):
    B, S, D = h.shape
    T = B * S
    x = h.reshape(T, D)
    logits = (x @ w_router).astype(jnp.float32) + b_router.astype(jnp.float32)
    top_val, top_idx = lax.top_k(logits, TOP_K)
    top_w = jax.nn.softmax(top_val, axis=-1)
    A = T * TOP_K
    flat_e = top_idx.reshape(A)
    order = jnp.argsort(flat_e)
    e_sorted = flat_e[order]
    tok_sorted = (order // TOP_K).astype(jnp.int32)
    w_sorted = top_w.reshape(A)[order]
    counts = jnp.bincount(flat_e, length=N_EXPERTS)
    padded = (counts + MOE_ROWS - 1) // MOE_ROWS * MOE_ROWS
    pad_end = jnp.cumsum(padded)
    pad_start = pad_end - padded
    grp_start = jnp.cumsum(counts) - counts
    dest = pad_start[e_sorted] + jnp.arange(A) - grp_start[e_sorted]
    n_blocks = -(-A // MOE_ROWS) + N_EXPERTS
    n_rows = n_blocks * MOE_ROWS
    row_tok = jnp.zeros((n_rows,), jnp.int32).at[dest].set(tok_sorted)
    row_w = jnp.zeros((n_rows,), jnp.float32).at[dest].set(w_sorted)
    blk_exp = jnp.minimum(jnp.searchsorted(pad_end, jnp.arange(n_blocks) * MOE_ROWS, side='right'),
                          N_EXPERTS - 1)

    def expert_block(args):
        tok, e = args
        gu = x[tok] @ w_gu[e] + b_gu[e]
        gate = jnp.minimum(gu[:, :D_FF], SWIGLU_LIMIT)
        up = jnp.clip(gu[:, D_FF:], -SWIGLU_LIMIT, SWIGLU_LIMIT)
        act = (up + 1) * gate * jax.nn.sigmoid(SWIGLU_ALPHA * gate)
        return act @ w_down[e] + b_down[e]

    y_rows = lax.map(expert_block, (row_tok.reshape(n_blocks, MOE_ROWS), blk_exp))
    y_rows = y_rows.reshape(n_rows, D).astype(jnp.float32) * row_w[:, None]
    out = jax.ops.segment_sum(y_rows, row_tok, num_segments=T)
    return out.reshape(B, S, D).astype(h.dtype)

def setup_inputs(seed: int = 0) -> dict:
    key = jax.random.key(seed)
    ks = jax.random.split(key, 24)
    f32 = jnp.float32
    L, D = DEPTH, D_MODEL

    def nrm(k, shape, fan_in):
        return jax.random.normal(k, shape, f32) * (fan_in ** -0.5)

    def gain(k, shape):
        return 1.0 + 0.05 * jax.random.normal(k, shape, f32)

    dt = jnp.exp(jax.random.uniform(ks[12], (L, DN_HEADS), f32, np.log(1e-3), np.log(1e-1)))
    return {
        'x': jax.random.normal(ks[0], (BATCH, SEQ, D), f32),
        'c': jax.random.normal(ks[1], (BATCH, D), f32),
        'w_ada': nrm(ks[2], (L, D, 6 * D), D),
        'b_ada': 0.02 * jax.random.normal(ks[3], (L, 6 * D), f32),
        'g_pre_mix': gain(ks[4], (L, D)),
        'g_post_mix': gain(ks[5], (L, D)),
        'g_pre_ffn': gain(ks[6], (L, D)),
        'g_post_ffn': gain(ks[7], (L, D)),
        'w_in': nrm(ks[8], (L, D, IN_WIDTH), D),
        'conv_w': nrm(ks[9], (L, DN_CONV, 3 * DN_WIDTH), DN_CONV),
        'a_log': jnp.log(jax.random.uniform(ks[10], (L, DN_HEADS), f32, 1.0, 16.0)),
        'dt_bias': dt + jnp.log(-jnp.expm1(-dt)),
        'g_dn_out': gain(ks[11], (L, HEAD_DIM)),
        'w_br_a': nrm(ks[13], (L, DN_WIDTH, D), DN_WIDTH),
        'w_br_b': nrm(ks[14], (L, MB_WIDTH, D), MB_WIDTH),
        'w_o': nrm(ks[15], (L, D, D), D),
        'w_router': nrm(ks[16], (L, D, N_EXPERTS), D),
        'b_router': 0.01 * jax.random.normal(ks[17], (L, N_EXPERTS), f32),
        'w_gu': nrm(ks[18], (L, N_EXPERTS, D, 2 * D_FF), D),
        'b_gu': 0.01 * jax.random.normal(ks[19], (L, N_EXPERTS, 2 * D_FF), f32),
        'w_down': nrm(ks[20], (L, N_EXPERTS, D_FF, D), D_FF),
        'b_down': 0.01 * jax.random.normal(ks[21], (L, N_EXPERTS, D), f32),
    }

def reference(x, c, w_ada, b_ada, g_pre_mix, g_post_mix, g_pre_ffn, g_post_ffn, w_in, conv_w,
              a_log, dt_bias, g_dn_out, w_br_a, w_br_b, w_o, w_router, b_router, w_gu, b_gu,
              w_down, b_down):
    for l in range(DEPTH):
        mod = jax.nn.silu(c) @ w_ada[l] + b_ada[l]
        shift_m, scale_m, gate_m, shift_f, scale_f, gate_f = [m[:, None, :] for m in jnp.split(mod, 6, axis=-1)]
        h = rmsnorm(x, g_pre_mix[l]) * (1 + scale_m) + shift_m
        y = hybrid_mixer(h, w_in[l], conv_w[l], a_log[l], dt_bias[l], g_dn_out[l],
                         w_br_a[l], w_br_b[l], w_o[l])
        x = x + gate_m * rmsnorm(y, g_post_mix[l])
        h = rmsnorm(x, g_pre_ffn[l]) * (1 + scale_f) + shift_f
        y = routed_moe(h, w_router[l], b_router[l], w_gu[l], b_gu[l], w_down[l], b_down[l])
        x = x + gate_f * rmsnorm(y, g_post_ffn[l])
    return x


_drawn_inputs = setup_inputs


def setup_inputs(seed=0):
    import zlib

    import numpy as np

    out = dict(_drawn_inputs(seed))
    spreads = {}
    factors = {'b_gu': 8.0, 'b_down': 8.0}
    for name, (base, spread) in spreads.items():
        noise = np.random.default_rng([zlib.crc32(name.encode()), seed]).standard_normal(out[name].shape)
        drawn = base * np.exp(spread * noise) if base else spread * noise
        out[name] = __import__('jax').numpy.asarray(drawn.astype(out[name].dtype))
    for name, factor in factors.items():
        out[name] = (out[name] * factor).astype(out[name].dtype)
    return out
```

```python
import numpy as np
import concourse.bass as bass
from concourse import mybir
from contextlib import ExitStack

F32 = mybir.dt.float32
BF16 = mybir.dt.bfloat16
I32 = mybir.dt.int32
ALU = mybir.AluOpType
ACT = mybir.ActivationFunctionType
AX = mybir.AxisListType

P = 128
D = 1024
S = 256
NT = S // P
KD = D // P
HD = 128
H = 4
W = H * HD
CHUNK = 64
TAPS = 4
HALF_ROPE = HD // 8
NE = 32
TOPK = 4
F = 1024
KF = F // P
SLOTS = 64
MAXJ = NE + S * TOPK // SLOTS
JC = MAXJ + 1
EPS = 1e-6
LIMIT = 7.0
ALPHA = 1.702
NEG = -1e30

BLK = 256
UNIT = KD * BLK
RING = 12
MIX_RING = 6
GU_UNITS = KD
DN_UNITS = 4

CONST = {}
_at = 0
for _name, _n in (("ident", 128), ("ones", 128), ("tri", 128), ("blockones", 128), ("firsthalf", 128),
                  ("secondhalf", 128), ("decaymask", 128), ("strict", 128), ("level", 6 * 128), ("level1t", 128),
                  ("before", 128), ("causal", 128), ("iota", JC), ("slot", SLOTS), ("cos", S), ("sin", S),
                  ("tri32", 32), ("ntri32", 32), ("expert", 1)):
    CONST[_name] = (_at, _n)
    _at += _n
NCONST = _at


def shape_constants():
    c = np.zeros((P, NCONST), np.float32)

    def put(name, value):
        a, n = CONST[name]
        c[:value.shape[0], a:a + n] = value

    i, j = np.arange(P)[:, None], np.arange(P)[None, :]
    same = i // CHUNK == j // CHUNK
    put("ident", (i == j).astype(np.float32))
    put("ones", np.ones((P, P), np.float32))
    put("tri", ((i <= j) & same).astype(np.float32))
    put("blockones", same.astype(np.float32))
    put("firsthalf", (i + 0 * j < CHUNK).astype(np.float32))
    put("secondhalf", (i + 0 * j >= CHUNK).astype(np.float32))
    put("decaymask", np.where((i <= j) & same, 0.0, NEG).astype(np.float32))
    put("strict", ((i < j) & same).astype(np.float32))
    levels = []
    for s in (1, 2, 4, 8, 16, 32):
        m = (i // (2 * s) == j // (2 * s)) & (i // s % 2 == 1) & (j // s % 2 == 0)
        levels.append(-m.astype(np.float32))
    put("level", np.concatenate(levels, 1))
    put("level1t", levels[0].T)
    put("before", (i < j).astype(np.float32))
    put("causal", np.where(j <= i, 0.0, NEG).astype(np.float32))
    put("iota", np.broadcast_to(np.arange(JC, dtype=np.float32), (P, JC)))
    put("slot", np.broadcast_to(np.arange(SLOTS, dtype=np.float32), (P, SLOTS)))
    inv = np.float32(500000.0) ** (-np.arange(HALF_ROPE, dtype=np.float32) / np.float32(HALF_ROPE))
    ang = (np.arange(S, dtype=np.float32)[:, None] * inv[None, :]).astype(np.float32).astype(np.float64)
    cos, sin = np.cos(ang).T.astype(np.float32), np.sin(ang).T.astype(np.float32)
    put("cos", np.concatenate([cos, cos]))
    put("sin", np.concatenate([-sin, sin]))
    e = np.arange(NE)
    put("tri32", (e[:, None] <= e[None, :]).astype(np.float32))
    put("ntri32", (e[:, None] < e[None, :]).astype(np.float32))
    put("expert", e[:, None].astype(np.float32))
    return c


def build(nc, A, out):
    ctx = ExitStack()
    with ctx:
        def sb(name, shape, dt=F32):
            return ctx.enter_context(nc.sbuf_tensor(name, shape, dt))

        def sem(name):
            return ctx.enter_context(nc.semaphore(name))

        B = [ctx.enter_context(nc.psum_tensor(f"bank{i}", [P, 512], F32)) for i in range(8)]

        ring = sb("ring", [P, RING * UNIT])
        cst = sb("cst", [P, NCONST])
        hT = sb("hT", [P, KD * S])
        qkv = sb("qkv", [P, 3 * H * S])
        zT = sb("zT", [P, H * S])
        mbx = sb("mbx", [P, 3 * H * S])
        gates = sb("gates", [P, 2 * KD * S])
        oT = sb("oT", [P, 2 * H * S])
        rows = sb("rows", [P, 2 * D])
        xs = sb("xs", [P, NT * D])
        mod = sb("mod", [P, 4 * D])
        col = sb("col", [P, 8 + 16 + 48 + 1 + 8 + 8])
        wba = sb("wba", [P, KD * 8])
        wrt = sb("wrt", [P, KD * NE])
        sm = sb("sm", [P, 640])
        silc = sb("silc", [P, KD * 32])
        posj = sb("posj", [P, 2 * NT * JC])
        table = sb("table", [1, NE + JC + 1], I32)
        sgat = sb("sgat", [P, NT * SLOTS], BF16)

        def const(name):
            a, n = CONST[name]
            return cst[:, a:a + n]

        ident, ones = const("ident"), const("ones")
        gcol, bcol = col[:, 0:8], col[:, 8:24]
        convw = col[:, 24:72]
        gdn = col[:, 72:73]
        ccol = col[:, 73:81]
        hTk = hT[:, :].rearrange("p (k t) -> p k t", k=KD)
        qT, kT, vT = (qkv[:, i * H * S:(i + 1) * H * S] for i in range(3))
        gv = [gates[:, i * KD * S:(i + 1) * KD * S] for i in range(2)]
        oaT, obT = oT[:, 0:H * S], oT[:, H * S:2 * H * S]
        mq, mk, mv = (mbx[:, i * H * S:(i + 1) * H * S] for i in range(3))

        scr = MIX_RING * UNIT

        def scratch(at, n):
            return ring[:, scr + at:scr + at + n]

        TW = H * HD
        vb, kbg, ktl, DT, LT, QK, T, TT, M, qd = (scratch(1024 * i, 1024) for i in range(10))
        state = scratch(10240, TW)
        prob = scratch(10752, 1536)
        uu, wT, vn, otok = DT, LT, T, kbg
        squares, rnorm = scratch(1024 * 6, 2048), scratch(1024 * 3, 2048)
        egb = T

        def tile(buf, t):
            return buf[:, t * TW:(t + 1) * TW]

        def head(buf, t, h):
            return buf[:, t * TW + h * HD:t * TW + (h + 1) * HD]

        def small(a, n):
            return sm[:, a:a + n]

        shG = small(0, 16)
        ba = small(16, 16)
        beta, g, gc, eg, etail, bk, t8a, t8b = (small(32 + 8 * i, 8) for i in range(8))
        dec = small(96, 16)
        alog = small(112, 4)
        dtb = small(116, 4)
        ssum = small(120, 16)
        rsc = small(136, 16)
        mx = small(152, 16)
        baT = sm[0:8, 168:168 + S]
        rmsb = small(168, S)
        eps128 = small(424, 4)
        mstat = small(428, 8)
        rbr = small(436, NE)

        hb = qkv[:, :].bitcast(BF16).rearrange("p (s t d) -> p s t d", s=3, t=NT)
        acc = gv[0]
        ffn = gv[1]
        gus = ffn[:, 0:1024]
        ysb = ffn[:, 1024:1536]
        cab = ffn[:, 1536:2048]
        xg = oT[:, 0:512]
        actT = oT[:, 512:1024]
        tg, tu, ts = zT[:, 384:896], oT[:, 1024:1536], oT[:, 1536:2048]
        swt = zT[:, 0:2 * 192]
        bJ = mbx[:, 0:16 * JC]
        rt = zT[:, 384:1024]
        bgu = rows[0:NE, :]
        bdn = mbx[0:NE, 2048:3072]
        GM, SH2, G2, GF = (mod[:, i * D:(i + 1) * D] for i in range(4))
        gpm, gpf, gqf = (mbx[:, i * D:(i + 1) * D] for i in range(3))

        names = """const_in x_in small_in wba_in x2_in rows_in modb_in bdn_in silu_c zeros sq_x ss_x ssx_e rt_x xn col_ps shg
            h_ok unit_used proj conv ract a_read sq_k ss_ps ss_e rtn qk_n ba_ps ba_sb bat_ps ax axe g_ok
            cum_ps cum_a cum_v tr_ps ktok gcb_ps dt_v dt_a egb_a bb_ps kk_ps lt_v qk_v l_ps t1_v a_ps m_v x_ps
            tt_v uw_ps uw_a ws_ps vn_v o_ps o_a st_ps s_v ro_a ro_v ot_ps oa_v rope_v sc_ps mx_v p_a pn_v
            pt_ps pt_a ob_ps ob_a mod_a mod_ps mod_v ya_ps ya_v mix_ps mix_a xss xsr x1 hss hsr h2 hb1 h2t_ps
            h2t lg_ps lg_v ex_a sel_v pos_ps pos_v cnt_v jt_ps oh_v job_ps bj_ps bj_a tab_v y0_ps y0_v selg
            gat xg_a gu gu_a gu_v trn g_rdy sg_rdy act_v ctr c_a yd y_a sc accd fss fsr fo out_d vch ach
            scratch_dead expert_rows selw ktv vz""".split()
        s = {n: sem(n) for n in names}
        landed = [sem(f"landed{i}") for i in range(RING)]
        used = [sem(f"used{i}") for i in range(RING)]

        units = [("ada", i * BLK) for i in range(8)]
        units += [("in", c) for c in (512, 768, 0, 256, 1024, 1280, 1536, 1792)]
        units += [("in", 2056 + i * BLK) for i in range(6)]
        units += [("in", 3592 + i * BLK) for i in range(8)]
        units += [("ada", 2048 + i * BLK) for i in range(16)]
        units += [("bra", 0), ("brb", 0), ("bra", 512), ("brb", 512)]
        units += [("o", i * BLK) for i in range(4)]
        NU = len(units)
        assert NU % MIX_RING == 0
        ROUNDS = NU // MIX_RING

        def slot(i):
            return ring[:, i * UNIT:(i + 1) * UNIT]

        def unit_source(i):
            kind, c = units[i]
            if kind in ("bra", "brb"):
                return A["w_br_a" if kind == "bra" else "w_br_b"][:, c:c + 512].rearrange("(k p) n -> p k n", p=P)
            w = A[{"ada": "w_ada", "in": "w_in", "o": "w_o"}[kind]]
            return w[:, c:c + BLK].rearrange("(k p) n -> p k n", p=P)

        readers = "aaaa" + "vvvvvv" + "aa" + "aaaa" + "aa"
        readers += "aaaaaaaa" + "aaaaaaaa"

        def reads(kind, use):
            return readers[:use + 1].count(kind)

        Q0, Z0, MB0, MV0, GA0, AD0 = 4, 10, 12, 16, 18, 26

        block = ctx.enter_context(nc.Block())

        @block.sync
        def _(sp):
            for i in range(NU):
                if i >= MIX_RING:
                    sp.wait_ge(s["unit_used"], i - MIX_RING + 1)
                v = slot(i % MIX_RING).rearrange("p (k n) -> p k n", k=4 if units[i][0][:2] == "br" else KD)
                sp.dma_start(v, unit_source(i)).then_inc(landed[i % MIX_RING], 16)
                if i == 0:
                    sp.dma_start(wba[:, :].rearrange("p (k n) -> p k n", k=KD),
                                 A["w_in"][:, 2048:2056].rearrange("(k p) n -> p k n", p=P)).then_inc(s["wba_in"], 16)

            def expert_units(wait, e):
                for u in range(RING):
                    wait(u)
                    if u < GU_UNITS:
                        src = A["w_gu"][bass.ds(e, 1), u * P:(u + 1) * P, :].rearrange("e p n -> p (e n)")
                        sp.dma_start(slot(u), src).then_inc(landed[u], 16)
                    else:
                        v = u - GU_UNITS
                        src = A["w_down"][bass.ds(e, 1), v * 2 * P:(v + 1) * 2 * P, :].rearrange(
                            "e (f p) n -> p (e f) n", p=P)
                        sp.dma_start(slot(u).rearrange("p (f n) -> p f n", f=2), src).then_inc(landed[u], 16)

            def first_wait(u):
                if u < MIX_RING:
                    sp.wait_ge(s["unit_used"], NU - MIX_RING + u + 1)
                elif u == MIX_RING:
                    sp.wait_ge(s["scratch_dead"], 1)

            expert_units(first_wait, 0)
            sp.wait_ge(s["tab_v"], 1)
            with sp.Fori(1, NE) as e:
                first = sp.value_load(table[0:1, bass.ds(e, 1)], min_val=1, max_val=MAXJ)
                expert_units(lambda u: sp.wait_ge(used[u], first), e)
            for t in range(NT):
                sp.wait_ge(s["fo"], t + 1)
                sp.dma_start(out[t * P:(t + 1) * P, :], xs[:, t * D:(t + 1) * D]).then_inc(s["out_d"], 16)
            sp.wait_ge(s["out_d"], 16 * NT)

        @block.gpsimd
        def _(pool):
            pool.memset(silc[:, :], 0.0).then_inc(s["zeros"], 1)
            for i, c in enumerate((2048, 3072, 4096, 5120)):
                pool.dma_start(mod[:, i * D:(i + 1) * D], A["b_ada"][0:1, c:c + D].partition_broadcast(P)).then_inc(s["modb_in"], 16)
            for t in range(NT):
                pool.dma_start(xs[:, t * D:(t + 1) * D], A["x"][t * P:(t + 1) * P, :]).then_inc(s["x2_in"], 16)
            pool.dma_start(rbr, A["b_router"][0:1, :].partition_broadcast(P)).then_inc(s["x2_in"], 16)
            pool.dma_start(wrt[:, :].rearrange("p (k n) -> p k n", k=KD),
                           A["w_router"].rearrange("(k p) n -> p k n", p=P)).then_inc(s["x2_in"], 16)
            pool.wait_ge(s["ob_a"], H)
            for i, n in enumerate(("g_post_mix", "g_pre_ffn", "g_post_ffn")):
                pool.dma_start(mbx[:, i * D:(i + 1) * D], A[n][0:1, :].partition_broadcast(P)).then_inc(s["rows_in"], 16)
            pool.wait_ge(s["mod_v"], 4)
            pool.dma_start(bdn, A["b_down"]).then_inc(s["bdn_in"], 16)
            pool.wait_ge(s["x1"], 2)
            pool.dma_start(bgu, A["b_gu"]).then_inc(s["expert_rows"], 16)

        @block.scalar
        def _(act):
            act.dma_start(cst[:, :], A["cst"]).then_inc(s["const_in"], 16)
            act.dma_start(hTk, A["xT"].rearrange("(k p) t -> p k t", p=P)).then_inc(s["x_in"], 16)
            act.dma_start(col[:, 0:8], A["g_pre_col"]).then_inc(s["small_in"], 16)
            act.dma_start(col[:, 8:24], A["b_ada_col"]).then_inc(s["small_in"], 16)
            act.dma_start(col[:, 24:72], A["conv_col"]).then_inc(s["small_in"], 16)
            act.dma_start(col[:, 72:73], A["g_dn_col"]).then_inc(s["small_in"], 16)
            act.dma_start(col[:, 73:81], A["c_col"]).then_inc(s["small_in"], 16)
            act.dma_start(alog, A["a_log"][0:1, :].partition_broadcast(P)).then_inc(s["small_in"], 16)
            act.dma_start(dtb, A["dt_bias"][0:1, :].partition_broadcast(P)).then_inc(s["small_in"], 16)
            act.wait_ge(s["small_in"], 16 * 7)
            act.wait_ge(s["zeros"], 1)
            act.activation(silc[:, :].rearrange("p (k n) -> p k n", n=32)[:, :, 0], ccol, ACT.Silu).then_inc(s["silu_c"], 1)
            act.wait_ge(s["x_in"], 16)
            act.activation(rows[:, :], hT[:, :], ACT.Square).then_inc(s["sq_x"], 1)
            act.wait_ge(s["ssx_e"], 1)
            act.activation(rmsb, rmsb, ACT.Sqrt).then_inc(s["rt_x"], 1)
            act.activation(alog, alog, ACT.Exp).then_inc(s["ach"], 1)
            act.wait_ge(s["ss_x"], 1)
            for q in range(4):
                act.wait_ge(s["proj"], q + 1)
                act.activation(rows[:, q * 512:(q + 1) * 512], B[q % 2][:, :], ACT.Copy).then_inc(s["a_read"], 1)

            def silu_conv(n):
                dst = (kT, kT, qT, qT, vT, vT)[n][:, (n % 2) * 512:(n % 2) * 512 + 512]
                act.wait_ge(s["conv"], n + 1)
                act.activation(dst, dst, ACT.Silu).then_inc(s["ract"], 1)

            def square_norm(which):
                src = kT if which == 0 else qT
                if which == 1:
                    act.wait_ge(s["ss_ps"], 1)
                act.wait_ge(s["ract"], 2 * which + 2)
                act.activation(squares[:, 0:1024], src, ACT.Square).then_inc(s["sq_k"], 1)

            def root_norm(which):
                r = rnorm[:, which * 1024:(which + 1) * 1024]
                act.wait_ge(s["ss_e"], which + 1)
                act.activation(r, r, ACT.Sqrt).then_inc(s["rtn"], 1)

            silu_conv(0)
            act.wait_ge(s["ba_ps"], 1)
            act.activation(baT, B[7][0:8, 0:S], ACT.Copy).then_inc(s["ba_sb"], 1)
            silu_conv(1)
            square_norm(0)
            act.wait_ge(s["ax"], 1)
            act.activation(beta.rearrange("p (t h) -> p t h", t=NT),
                           B[7][:, 256:272].rearrange("p (t h) -> p t h", t=NT)[:, :, 0:H], ACT.Sigmoid).then_inc(s["ach"], 1)
            act.activation(t8b, t8b, ACT.Exp).then_inc(s["ach"], 1)
            act.wait_ge(s["ach"], 3)
            act.activation(t8b, t8b, ACT.Ln, bias=1.0).then_inc(s["axe"], 1)
            silu_conv(2)
            root_norm(0)
            silu_conv(3)
            square_norm(1)
            act.wait_ge(s["cum_v"], 1)
            act.activation(eg, B[7][:, 0:8], ACT.Exp).then_inc(s["cum_a"], 1)
            act.activation(dec, B[7][:, 16:32], ACT.Exp).then_inc(s["cum_a"], 1)
            act.activation(etail, t8a, ACT.Exp).then_inc(s["cum_a"], 1)
            silu_conv(4)
            root_norm(1)
            silu_conv(5)

            for n in range(2):
                act.wait_ge(s["proj"], Z0 + n + 1)
                act.activation(zT[:, n * 512:(n + 1) * 512], B[(Z0 + n) % 2][:, :], ACT.Silu).then_inc(s["a_read"], 1)

            def decay_exp(t):
                act.wait_ge(s["dt_v"], t + 1)
                if t == 0:
                    act.wait_ge(s["ss_ps"], 2)
                act.activation(tile(egb, t), B[6][:, :], ACT.Exp).then_inc(s["egb_a"], 1)
                act.activation(tile(DT, t), tile(DT, t), ACT.Exp).then_inc(s["dt_a"], 1)

            for t in range(NT):
                act.wait_ge(s["ktv"], H * (t + 1))
                act.wait_ge(s["cum_a"], 3)
                for h in range(H):
                    c = t * H + h
                    act.activation(head(ktl, t, h), B[2 + t][:, h * HD:(h + 1) * HD], ACT.Copy,
                                   scale=etail[:, c:c + 1]).then_inc(s["ktok"], 1)
            for t in range(NT):
                act.wait_ge(s["tr_ps"], NT + t + 1)
                for h in range(H):
                    c = t * H + h
                    act.activation(head(vb, t, h), B[4 + t][:, h * HD:(h + 1) * HD], ACT.Copy,
                                   scale=beta[:, c:c + 1]).then_inc(s["ktok"], 1)
            decay_exp(0)

            def copy_rotary(n):
                act.wait_ge(s["proj"], MB0 + n + 1)
                dst = (mq, mk)[n // 2][:, (n % 2) * 512:(n % 2) * 512 + 512]
                act.activation(dst, B[(MB0 + n) % 2][:, :], ACT.Copy).then_inc(s["a_read"], 1)

            def copy_v(n):
                act.wait_ge(s["proj"], MV0 + n + 1)
                for t in range(NT):
                    ins = act.activation(mv[:, t * TW + n * BLK:t * TW + (n + 1) * BLK],
                                         B[(MV0 + n) % 2][:, t * BLK:(t + 1) * BLK], ACT.Copy)
                ins.then_inc(s["a_read"], 1)

            def gate_sig(n):
                act.wait_ge(s["proj"], GA0 + n + 1)
                act.activation(gv[n // 4][:, (n % 4) * 512:(n % 4) * 512 + 512], B[(GA0 + n) % 2][:, :],
                               ACT.Sigmoid).then_inc(s["a_read"], 1)

            copy_rotary(0)
            decay_exp(1)
            copy_rotary(1)
            copy_rotary(2)
            copy_rotary(3)
            copy_v(0)
            copy_v(1)
            for n in range(8):
                gate_sig(n)

            def mod_row(q):
                if q >= 4:
                    act.wait_ge(s["mod_ps"], q // 2 - 1)
                act.wait_ge(s["proj"], AD0 + q + 1)
                act.activation(rows[:, (q % 4) * 512:(q % 4) * 512 + 512], B[(AD0 + q) % 2][:, :], ACT.Copy).then_inc(s["a_read"], 1)

            act.wait_ge(s["col_ps"], 1)
            for q in range(8):
                mod_row(q)
            for t in range(NT):
                act.wait_ge(s["uw_ps"], t + 1)
                act.activation(tile(uu, t), B[2 + t][:, :], ACT.Copy).then_inc(s["uw_a"], 1)
                act.activation(tile(wT, t), B[6 + t][:, :], ACT.Copy).then_inc(s["uw_a"], 1)

            def softmax_exp(h):
                p = prob[:, (h % 2) * 768:(h % 2) * 768 + 384]
                act.wait_ge(s["mx_v"], h + 1)
                act.activation(p[:, 0:128], p[:, 0:128], ACT.Exp, bias=mstat[:, 0:1], scale=HD ** -0.5, accum_out=mstat[:, 2:3]).then_inc(s["p_a"], 1)
                act.activation(p[:, 128:384], p[:, 128:384], ACT.Exp, bias=mstat[:, 1:2], scale=HD ** -0.5, accum_out=mstat[:, 3:4]).then_inc(s["p_a"], 1)

            def softmax_copies(h):
                pt = prob[:, (h % 2) * 768 + 384:(h % 2) * 768 + 768]
                act.wait_ge(s["pt_ps"], h + 1)
                act.activation(pt, B[1][:, 0:384], ACT.Copy).then_inc(s["pt_a"], 1)
                act.wait_ge(s["ob_ps"], h + 1)
                act.activation(obT[:, h * S:(h + 1) * S], B[0][:, 0:S], ACT.Copy).then_inc(s["ob_a"], 1)

            def out_copy(n):
                t, r0 = n // 2, CHUNK * (n % 2)
                act.wait_ge(s["o_ps"], n + 1)
                act.activation(tile(otok, t)[r0:r0 + CHUNK, :], B[2 + t][r0:r0 + CHUNK, :], ACT.Copy).then_inc(s["o_a"], 1)

            for n in range(4):
                softmax_exp(n)
                out_copy(n)
                softmax_copies(n)

            for t in range(NT):
                act.wait_ge(s["o_a"], 2 * t + 2)
                act.activation(tile(qd, t), tile(otok, t), ACT.Square).then_inc(s["ro_a"], 1)
            act.wait_ge(s["ro_v"], 1)
            act.activation(rsc[:, 0:8], ssum[:, 0:8], ACT.Sqrt).then_inc(s["ro_a"], 1)

            for n in range(4):
                act.wait_ge(s["mix_ps"], n + 1)
                for t in range(NT):
                    ins = act.activation(rows[:, t * D + n * BLK:t * D + (n + 1) * BLK],
                                         B[n % 2][:, t * BLK:(t + 1) * BLK], ACT.Copy)
                ins.then_inc(s["mix_a"], 1)
            act.wait_ge(s["mix_a"], 4)
            act.wait_ge(s["ya_v"], KD)
            for t in range(NT):
                act.activation(gv[0][:, t * D:(t + 1) * D], rows[:, t * D:(t + 1) * D], ACT.Square,
                               accum_out=ssum[:, t:t + 1]).then_inc(s["xss"], 1)
            act.wait_ge(s["xsr"], 1)
            act.activation(rsc[:, 0:2], ssum[:, 2:4], ACT.Sqrt).then_inc(s["xss"], 1)
            for t in range(NT):
                act.wait_ge(s["x1"], t + 1)
                act.activation(gv[1][:, t * D:(t + 1) * D], xs[:, t * D:(t + 1) * D], ACT.Square,
                               accum_out=ssum[:, 4 + t:5 + t]).then_inc(s["hss"], 1)
            act.wait_ge(s["hsr"], 1)
            act.activation(rsc[:, 4:6], ssum[:, 6:8], ACT.Sqrt).then_inc(s["hss"], 1)
            for n in range(4):
                act.wait_ge(s["h2t_ps"], n + 1)
                act.activation(hT[:, n * 512:(n + 1) * 512], B[n][:, :], ACT.Copy).then_inc(s["h2t"], 1)
            act.wait_ge(s["lg_v"], 1)
            for t in range(NT):
                act.activation(rt[:, 64 + t * NE:64 + (t + 1) * NE], rt[:, t * NE:(t + 1) * NE], ACT.Exp,
                               bias=mx[:, 8 * t + 1:8 * t + 2]).then_inc(s["ex_a"], 1)
            for n in range(2):
                act.wait_ge(s["bj_ps"], n + 1)
                act.activation(bJ[:, n * 8 * JC:(n + 1) * 8 * JC], B[n][:, 0:8 * JC], ACT.Copy).then_inc(s["bj_a"], 1)

            act.wait_ge(s["gat"], 1)
            act.activation(xg, B[3][:, :], ACT.Copy).then_inc(s["xg_a"], 1)
            act.wait_ge(s["tab_v"], 1)
            J = act.value_load(table[0:1, NE + JC:NE + JC + 1], min_val=NE, max_val=MAXJ)
            act.sem_inc(s["gu_a"], 1)
            act.sem_inc(s["c_a"], 1)
            act.sem_inc(s["y_a"], 1)
            act.sem_inc(s["sg_rdy"], 2)
            with act.Fori(0, J) as j:
                act.wait_ge(s["gu"], j + 1)
                act.activation(gus[:, 0:512], B[0][:, :], ACT.Copy).then_inc(s["gu_a"], 1)
                act.wait_ge(s["gat"], j + 2)
                act.activation(xg, B[3][:, :], ACT.Copy).then_inc(s["xg_a"], 1)
                for q in range(2):
                    act.wait_ge(s["g_rdy"], 2 * j + q + 1)
                    act.activation(ts[:, q * 256:(q + 1) * 256], tg[:, q * 256:(q + 1) * 256], ACT.Sigmoid, scale=ALPHA).then_inc(s["sg_rdy"], 1)
                act.wait_ge(s["ctr"], j + 2)
                act.activation(cab, B[3][:, :], ACT.Copy).then_inc(s["c_a"], 1)
                act.wait_ge(s["yd"], j + 2)
                act.activation(ysb, B[4][:, :], ACT.Copy).then_inc(s["y_a"], 1)

            act.wait_ge(s["accd"], 4 * J + 8)
            for t in range(NT):
                act.activation(ffn[:, 0:D] if t == 0 else ffn[:, D:2 * D], acc[:, t * D:(t + 1) * D], ACT.Square,
                               accum_out=ssum[:, 8 + t:9 + t]).then_inc(s["fss"], 1)
            act.wait_ge(s["fsr"], 1)
            act.activation(rsc[:, 8:10], ssum[:, 10:12], ACT.Sqrt).then_inc(s["fss"], 1)

        @block.vector
        def _(dve):
            v = nc.vector
            done = [0]

            def chain(ins):
                done[0] += 1
                ins.then_inc(s["vch"], 1)

            def settle():
                dve.wait_ge(s["vch"], done[0])

            def heads4(ap):
                return ap.rearrange("p (h d) -> p h d", h=H)

            def over_heads(ap):
                return ap.rearrange("p (a d) -> p a d", a=1).broadcast_to([P, H, ap.shape[1]])

            def root_arg(dst, src, scale, eps):
                return v.tensor_scalar(dst, src, scale, eps, ALU.mult, ALU.add)

            dve.wait_ge(s["ss_x"], 1)
            root_arg(rmsb, B[7][:, 0:S], 1.0 / D, EPS).then_inc(s["ssx_e"], 1)
            dve.wait_ge(s["rt_x"], 1)
            chain(v.reciprocal(rmsb, rmsb))
            settle()
            v.tensor_tensor(hTk, hTk, rmsb.rearrange("p (a t) -> p a t", a=1).broadcast_to([P, KD, S]), ALU.mult).then_inc(s["xn"], 1)
            dve.wait_ge(s["col_ps"], 1)
            dve.wait_ge(s["small_in"], 16 * 7)
            chain(v.tensor_tensor(shG, B[6][:, 0:16], bcol, ALU.add))
            settle()
            v.scalar_tensor_tensor(out=shG[:, 8:16], in0=shG[:, 8:16], scalar=1.0, in1=gcol, op0=ALU.add, op1=ALU.mult).then_inc(s["shg"], 1)
            dve.wait_ge(s["shg"], 1)
            dve.wait_ge(s["xn"], 1)
            for k in range(KD):
                v.tensor_scalar(hTk[:, k, :], hTk[:, k, :], shG[:, 8 + k:9 + k], shG[:, k:k + 1], ALU.mult, ALU.add).then_inc(s["h_ok"], 1)

            def conv(n):
                base = (kT, kT, qT, qT, vT, vT)[n]
                first = (4, 6, 0, 2, 8, 10)[n]
                dve.wait_ge(s["proj"], Q0 + n + 1)
                for j in range(TAPS):
                    if j:
                        settle()
                    for c in range(2):
                        x = B[(Q0 + n) % 2][:, c * S:(c + 1) * S]
                        y = base[:, (n % 2) * 512 + c * S:(n % 2) * 512 + (c + 1) * S]
                        w = convw[:, (first + c) * TAPS + TAPS - 1 - j:(first + c) * TAPS + TAPS - j]
                        if j == 0:
                            ins = v.tensor_scalar(y, x, w, None, ALU.mult)
                        else:
                            ins = v.scalar_tensor_tensor(out=y[:, j:], in0=x[:, 0:S - j], scalar=w, in1=y[:, j:], op0=ALU.mult, op1=ALU.add)
                        if j < TAPS - 1 or c == 0:
                            chain(ins)
                        else:
                            ins.then_inc(s["conv"], 1)

            def norm_arg(which):
                dve.wait_ge(s["ss_ps"], which + 1)
                for i in range(2):
                    ins = v.tensor_scalar(rnorm[:, which * 1024 + i * 512:which * 1024 + (i + 1) * 512],
                                          B[2 + 2 * which + i][:, :], 1e-6, None, ALU.add)
                    if i == 0:
                        chain(ins)
                ins.then_inc(s["ss_e"], 1)

            def normalise(which):
                r = rnorm[:, which * 1024:(which + 1) * 1024]
                dve.wait_ge(s["rtn"], which + 1)
                chain(v.reciprocal(r, r))
                settle()
                if which == 0:
                    v.tensor_tensor(kT, kT, r, ALU.mult).then_inc(s["qk_n"], 1)
                else:
                    v.scalar_tensor_tensor(out=qT, in0=qT, scalar=HD ** -0.5, in1=r, op0=ALU.mult, op1=ALU.mult).then_inc(s["qk_n"], 1)

            conv(0)
            conv(1)
            dve.wait_ge(s["bat_ps"], 1)
            chain(v.tensor_tensor(t8a.rearrange("p (t h) -> p t h", t=NT), B[7][:, 256:272].rearrange("p (t h) -> p t h", t=NT)[:, :, H:2 * H],
                                  dtb.rearrange("p (a h) -> p a h", a=1).broadcast_to([P, NT, H]), ALU.add))
            settle()
            chain(v.tensor_scalar(gc, t8a, -1.0, None, ALU.mult))
            settle()
            v.tensor_tensor(t8b, t8a, gc, ALU.min).then_inc(s["ax"], 1)
            conv(2)
            norm_arg(0)
            dve.wait_ge(s["axe"], 1)
            chain(v.scalar_tensor_tensor(out=g, in0=t8a, scalar=0.0, in1=t8b, op0=ALU.max, op1=ALU.add))
            settle()
            v.scalar_tensor_tensor(out=g.rearrange("p (t h) -> p t h", t=NT), in0=g.rearrange("p (t h) -> p t h", t=NT), scalar=-1.0,
                                   in1=alog.rearrange("p (a h) -> p a h", a=1).broadcast_to([P, NT, H]),
                                   op0=ALU.mult, op1=ALU.mult).then_inc(s["g_ok"], 1)
            conv(3)
            normalise(0)
            dve.wait_ge(s["cum_ps"], 1)
            chain(v.tensor_copy(gc, B[7][:, 0:8]))
            settle()
            v.tensor_tensor(t8a, B[7][:, 8:16], gc, ALU.subtract).then_inc(s["cum_v"], 1)
            dve.wait_ge(s["cum_a"], 1)
            v.tensor_tensor(bk, beta, eg, ALU.mult).then_inc(s["cum_v"], 1)
            conv(4)
            norm_arg(1)
            conv(5)
            normalise(1)
            dve.wait_ge(s["cum_v"], 2)
            for t in range(NT):
                dve.wait_ge(s["tr_ps"], t + 1)
                for h in range(H):
                    c = t * H + h
                    v.tensor_scalar(head(kbg, t, h), B[2 + t][:, h * HD:(h + 1) * HD], bk[:, c:c + 1], None, ALU.mult).then_inc(s["ktv"], 1)

            def decay_arg(t):
                dve.wait_ge(s["gcb_ps"], t + 1)
                for h in range(H):
                    ins = v.scalar_tensor_tensor(out=head(DT, t, h), in0=B[6][:, h * HD:(h + 1) * HD], scalar=gc[:, t * H + h:t * H + h + 1],
                                                 in1=const("decaymask"), op0=ALU.subtract, op1=ALU.add)
                    if h < H - 1:
                        chain(ins)
                ins.then_inc(s["dt_v"], 1)

            def lower(t):
                dve.wait_ge(s["dt_a"], t + 1)
                chain(v.tensor_tensor(heads4(tile(LT, t)), heads4(tile(DT, t)), over_heads(const("strict")), ALU.mult))
                dve.wait_ge(s["kk_ps"], t + 1)
                dve.wait_ge(s["bb_ps"], t + 1)
                settle()
                chain(v.tensor_tensor(tile(LT, t), tile(LT, t), B[7][:, :], ALU.mult))
                settle()
                v.tensor_tensor(tile(LT, t), tile(LT, t), B[2 + t][:, :], ALU.mult).then_inc(s["lt_v"], 1)
                v.tensor_tensor(tile(QK, t), tile(DT, t), B[4 + t][:, :], ALU.mult).then_inc(s["qk_v"], 1)
                dve.wait_ge(s["egb_a"], t + 1)
                chain(v.tensor_tensor(heads4(tile(qd, t)), heads4(qT)[:, :, t * P:(t + 1) * P], heads4(tile(egb, t)), ALU.mult))

            decay_arg(0)
            lower(0)
            decay_arg(1)
            lower(1)

            def level(l):
                a = const("level")[:, l * P:(l + 1) * P]
                return over_heads(a)

            for t in range(NT):
                dve.wait_ge(s["l_ps"], t + 1)
                settle()
                chain(v.tensor_tensor(heads4(tile(T, t)), heads4(B[2 + t][:, :]), level(0), ALU.mult))
                chain(v.tensor_tensor(heads4(tile(TT, t)), heads4(tile(LT, t)), over_heads(const("level1t")), ALU.mult))
                settle()
                v.tensor_tensor(heads4(tile(T, t)), heads4(tile(T, t)), over_heads(ident), ALU.add).then_inc(s["t1_v"], 1)
                v.tensor_tensor(heads4(tile(TT, t)), heads4(tile(TT, t)), over_heads(ident), ALU.add).then_inc(s["t1_v"], 1)
            dve.wait_ge(s["a_read"], reads("a", MB0 + 3))
            swap = [(i + HALF_ROPE) % (2 * HALF_ROPE) for i in range(2 * HALF_ROPE)]
            for i, m in enumerate((mq, mk)):
                R = 2 * HALF_ROPE
                tmp = prob[0:R, 0:H * S]
                rows32 = m[0:R, :].rearrange("p (h t) -> p h t", h=H)
                c4 = const("cos")[0:R, :].rearrange("p (a t) -> p a t", a=1).broadcast_to([R, H, S])
                s4 = const("sin")[0:R, :].rearrange("p (a t) -> p a t", a=1).broadcast_to([R, H, S])
                settle()
                chain(v.stream_shuffle(tmp, m[0:R, :], swap))
                settle()
                chain(v.tensor_tensor(tmp.rearrange("p (h t) -> p h t", h=H), tmp.rearrange("p (h t) -> p h t", h=H), s4, ALU.mult))
                chain(v.tensor_tensor(rows32, rows32, c4, ALU.mult))
                settle()
                v.tensor_tensor(m[0:R, :], m[0:R, :], tmp, ALU.add).then_inc(s["rope_v"], 1)
                dve.wait_ge(s["rope_v"], i + 1)

            for l in range(1, 6):
                for t in range(NT):
                    i = (l - 1) * NT + t
                    dve.wait_ge(s["a_ps"], i + 1)
                    v.tensor_tensor(heads4(tile(M, t)), heads4(B[2 + t][:, :]), level(l), ALU.mult).then_inc(s["m_v"], 1)
                for t in range(NT):
                    i = (l - 1) * NT + t
                    dve.wait_ge(s["x_ps"], i + 1)
                    if l < 5:
                        chain(v.tensor_tensor(tile(T, t), tile(T, t), B[4 + t][:, :], ALU.add))
                    v.tensor_tensor(tile(TT, t), tile(TT, t), B[6 + t][:, :], ALU.add).then_inc(s["tt_v"], 1)
            settle()
            v.memset(vn, 0.0).then_inc(s["vz"], 1)

            for i in range(4):
                dve.wait_ge(s["mod_ps"], i + 1)
                dve.wait_ge(s["modb_in"], 64)
                for n in range(2):
                    ins = v.tensor_tensor(mod[:, i * D + n * 512:i * D + (n + 1) * 512], mod[:, i * D + n * 512:i * D + (n + 1) * 512],
                                          B[4 + n][:, :], ALU.add)
                    if n == 0:
                        chain(ins)
                ins.then_inc(s["mod_a"], 1)

            for n in range(4):
                t, hf = n // 2, n % 2
                r = slice(CHUNK * hf, CHUNK * hf + CHUNK)
                vnb = vn[:, hf * TW:(hf + 1) * TW]
                dve.wait_ge(s["uw_a"], 2 * t + 1)
                dve.wait_ge(s["vz"], 1)
                if n == 0:
                    v.tensor_copy(vnb[r, :], tile(uu, t)[r, :]).then_inc(s["vn_v"], 1)
                else:
                    dve.wait_ge(s["ws_ps"], n)
                    v.tensor_tensor(vnb[r, :], tile(uu, t)[r, :], B[6][r, :], ALU.subtract).then_inc(s["vn_v"], 1)
                p = prob[:, (n % 2) * 768:(n % 2) * 768 + 384]
                dve.wait_ge(s["sc_ps"], n + 1)
                if n:
                    dve.wait_ge(s["pn_v"], 2 * n)
                if n >= 2:
                    dve.wait_ge(s["pt_ps"], n - 1)
                chain(v.tensor_tensor(p[:, 0:128], B[0][:, 0:128], const("causal"), ALU.add))
                chain(v.tensor_copy(p[:, 128:256], B[0][:, 128:256]))
                chain(v.tensor_tensor(p[:, 256:384], B[0][:, 256:384], const("causal"), ALU.add))
                settle()
                chain(v.tensor_reduce(mstat[:, 0:1], p[:, 0:128], AX.X, ALU.max))
                chain(v.tensor_reduce(mstat[:, 1:2], p[:, 128:384], AX.X, ALU.max))
                settle()
                v.tensor_scalar(mstat[:, 0:2], mstat[:, 0:2], -HD ** -0.5, None, ALU.mult).then_inc(s["mx_v"], 1)
                if n < 3:
                    dve.wait_ge(s["st_ps"], n + 1)
                    if n == 0:
                        v.tensor_copy(state, B[7][:, :]).then_inc(s["s_v"], 1)
                    else:
                        for h in range(H):
                            c = hf * 8 + t * H + h
                            st = state[:, h * HD:(h + 1) * HD]
                            ins = v.scalar_tensor_tensor(out=st, in0=st, scalar=dec[:, c:c + 1], in1=B[7][:, h * HD:(h + 1) * HD],
                                                         op0=ALU.mult, op1=ALU.add)
                            if h < H - 1:
                                chain(ins)
                        ins.then_inc(s["s_v"], 1)
                    dve.wait_ge(s["s_v"], n + 1)
                dve.wait_ge(s["p_a"], 2 * n + 2)
                chain(v.reciprocal(mstat[:, 4:6], mstat[:, 2:4]))
                settle()
                v.tensor_scalar(p[:, 0:128], p[:, 0:128], mstat[:, 4:5], None, ALU.mult).then_inc(s["pn_v"], 1)
                v.tensor_scalar(p[:, 128:384], p[:, 128:384], mstat[:, 5:6], None, ALU.mult).then_inc(s["pn_v"], 1)

            for t in range(NT):
                dve.wait_ge(s["ro_a"], t + 1)
                chain(v.tensor_reduce(ssum[:, t * H:(t + 1) * H], heads4(tile(qd, t)), AX.X, ALU.add))
            settle()
            root_arg(ssum[:, 0:8], ssum[:, 0:8], 1.0 / HD, EPS).then_inc(s["ro_v"], 1)
            dve.wait_ge(s["ro_a"], 3)
            chain(v.reciprocal(rsc[:, 0:8], rsc[:, 0:8]))
            settle()
            for t in range(NT):
                for h in range(H):
                    v.tensor_scalar(head(otok, t, h), head(otok, t, h), rsc[:, t * H + h:t * H + h + 1], None, ALU.mult).then_inc(s["ro_v"], 1)
            for t in range(NT):
                dve.wait_ge(s["ot_ps"], t + 1)
                v.scalar_tensor_tensor(out=heads4(oaT)[:, :, t * P:(t + 1) * P], in0=heads4(B[4 + t][:, :]), scalar=gdn,
                                       in1=heads4(zT)[:, :, t * P:(t + 1) * P], op0=ALU.mult, op1=ALU.mult).then_inc(s["oa_v"], 1)
            dve.wait_ge(s["rows_in"], 48)
            dve.wait_ge(s["mod_a"], 4)
            v.tensor_tensor(GM, GM, gpm, ALU.mult).then_inc(s["mod_v"], 1)
            v.scalar_tensor_tensor(out=G2, in0=G2, scalar=1.0, in1=gpf, op0=ALU.add, op1=ALU.mult).then_inc(s["mod_v"], 1)
            v.tensor_tensor(GF, GF, gqf, ALU.mult).then_inc(s["mod_v"], 2)
            for j in range(KD):
                b = B[2 + j % 2]
                ga, gb = (gv[i][:, j * S:(j + 1) * S] for i in range(2))
                dve.wait_ge(s["ya_ps"], j + 1)
                if j == 0:
                    dve.wait_ge(s["a_read"], reads("a", len(readers) - 1))
                chain(v.tensor_tensor(ga, ga, b[:, 0:S], ALU.mult))
                chain(v.tensor_tensor(gb, gb, b[:, S:2 * S], ALU.mult))
                settle()
                v.tensor_tensor(hTk[:, j, :], ga, gb, ALU.add).then_inc(s["ya_v"], 1)

            dve.wait_ge(s["xss"], 2)
            root_arg(ssum[:, 2:4], ssum[:, 0:2], 1.0 / D, EPS).then_inc(s["xsr"], 1)
            dve.wait_ge(s["xss"], 3)
            chain(v.reciprocal(rsc[:, 2:4], rsc[:, 0:2]))
            settle()
            dve.wait_ge(s["mod_v"], 4)
            dve.wait_ge(s["x2_in"], 64)
            for t in range(NT):
                a = slice(t * D, (t + 1) * D)
                chain(v.scalar_tensor_tensor(out=gv[0][:, a], in0=rows[:, a], scalar=rsc[:, 2 + t:3 + t], in1=GM, op0=ALU.mult, op1=ALU.mult))
                settle()
                v.tensor_tensor(xs[:, a], xs[:, a], gv[0][:, a], ALU.add).then_inc(s["x1"], 1)
            dve.wait_ge(s["hss"], 2)
            root_arg(ssum[:, 6:8], ssum[:, 4:6], 1.0 / D, EPS).then_inc(s["hsr"], 1)
            dve.wait_ge(s["hss"], 3)
            chain(v.reciprocal(rsc[:, 6:8], rsc[:, 4:6]))
            settle()
            dve.wait_ge(s["x1"], 2)
            for t in range(NT):
                a = slice(t * D, (t + 1) * D)
                chain(v.scalar_tensor_tensor(out=gv[0][:, a], in0=xs[:, a], scalar=rsc[:, 6 + t:7 + t], in1=G2, op0=ALU.mult, op1=ALU.mult))
                settle()
                v.tensor_tensor(gv[0][:, a], gv[0][:, a], SH2, ALU.add).then_inc(s["h2"], 1)
            dve.wait_ge(s["h2"], 2)
            for t in range(NT):
                a = slice(t * D, (t + 1) * D)
                chain(v.tensor_copy(hb[:, 0, t, :], gv[0][:, a]))
            settle()
            for t in range(NT):
                a = slice(t * D, (t + 1) * D)
                chain(v.tensor_tensor(gv[1][:, a], gv[0][:, a], hb[:, 0, t, :], ALU.subtract))
            settle()
            for t in range(NT):
                a = slice(t * D, (t + 1) * D)
                chain(v.tensor_copy(hb[:, 1, t, :], gv[1][:, a]))
            settle()
            for t in range(NT):
                a = slice(t * D, (t + 1) * D)
                v.tensor_tensor(hb[:, 2, t, :], gv[1][:, a], hb[:, 1, t, :], ALU.subtract).then_inc(s["hb1"], 1)

            rt_ = rt
            lgt, ex, selt, eqt, tmp, posm, wts = (rt_[:, i * 64:(i + 1) * 64] for i in range(7))
            cum, misc = rt_[:, 448:512], rt_[:, 512:640]
            dve.wait_ge(s["lg_ps"], 1)
            for t in range(NT):
                chain(v.tensor_tensor(lgt[:, t * NE:(t + 1) * NE], B[4][:, t * NE:(t + 1) * NE], rbr, ALU.add))
            settle()
            for t in range(NT):
                chain(v.max(mx[:, t * 8:(t + 1) * 8], lgt[:, t * NE:(t + 1) * NE]))
            settle()
            for t in range(NT):
                e = slice(t * NE, (t + 1) * NE)
                chain(v.tensor_scalar(selt[:, e], lgt[:, e], mx[:, 8 * t + TOPK - 1:8 * t + TOPK], None, ALU.is_gt))
                chain(v.tensor_scalar(eqt[:, e], lgt[:, e], mx[:, 8 * t + TOPK - 1:8 * t + TOPK], None, ALU.is_equal))
                ins = v.tensor_scalar(mx[:, 8 * t + 1:8 * t + 2], mx[:, 8 * t:8 * t + 1], -1.0, None, ALU.mult)
                if t == 0:
                    chain(ins)
                else:
                    ins.then_inc(s["lg_v"], 1)
            settle()
            for t in range(NT):
                e = slice(t * NE, (t + 1) * NE)
                chain(v.tensor_reduce(misc[:, t:t + 1], selt[:, e], AX.X, ALU.add))
                chain(v.tensor_tensor_scan(cum[:, e], ones[:, 0:NE], eqt[:, e], 0.0, ALU.mult, ALU.add))
            settle()
            chain(v.tensor_scalar(misc[:, 0:2], misc[:, 0:2], -1.0, float(TOPK), ALU.mult, ALU.add))
            settle()
            for t in range(NT):
                e = slice(t * NE, (t + 1) * NE)
                chain(v.scalar_tensor_tensor(out=tmp[:, e], in0=cum[:, e], scalar=misc[:, t:t + 1], in1=eqt[:, e], op0=ALU.is_le, op1=ALU.mult))
            settle()
            v.tensor_tensor(selt, selt, tmp, ALU.add).then_inc(s["sel_v"], 1)
            dve.wait_ge(s["sel_v"], 1)
            dve.wait_ge(s["ex_a"], 2)
            chain(v.tensor_tensor(ex, ex, selt, ALU.mult))
            settle()
            chain(v.tensor_reduce(misc[:, 2:4], ex.rearrange("p (t e) -> p t e", t=NT), AX.X, ALU.add))
            settle()
            chain(v.reciprocal(misc[:, 2:4], misc[:, 2:4]))
            settle()
            for t in range(NT):
                e = slice(t * NE, (t + 1) * NE)
                chain(v.tensor_scalar(wts[:, e], ex[:, e], misc[:, 2 + t:3 + t], None, ALU.mult))
            dve.wait_ge(s["pos_ps"], 1)
            chain(v.scalar_tensor_tensor(out=posm, in0=B[5][:, 0:2 * NE], scalar=1.0, in1=selt, op0=ALU.add, op1=ALU.mult))
            nrow, jend, ncol = misc[:, 32:64], misc[:, 64:96], misc[0:NE, 8:9]
            chain(v.tensor_scalar(nrow, B[5][:, 64:64 + NE], float(SLOTS), 1.0, ALU.is_gt, ALU.add))
            chain(v.tensor_scalar(ncol, B[5][0:NE, 96:97], float(SLOTS), 1.0, ALU.is_gt, ALU.add))
            settle()
            chain(v.tensor_scalar(posm, posm, -1.0, None, ALU.add))
            for m in range(2, S // SLOTS):
                chain(v.scalar_tensor_tensor(out=nrow, in0=B[5][:, 64:64 + NE], scalar=float(SLOTS * m), in1=nrow, op0=ALU.is_gt, op1=ALU.add))
                chain(v.scalar_tensor_tensor(out=ncol, in0=B[5][0:NE, 96:97], scalar=float(SLOTS * m), in1=ncol, op0=ALU.is_gt, op1=ALU.add))
                settle()
            v.tensor_copy(misc[0:1, 16:17], ones[0:1, 0:1]).then_inc(s["pos_v"], 1)
            chain(v.tensor_tensor_scan(jend, ones[:, 0:NE], nrow, 0.0, ALU.mult, ALU.add))
            settle()
            chain(v.tensor_tensor(nrow, jend, nrow, ALU.subtract))
            settle()
            chain(v.tensor_copy(table[0:1, 0:NE], nrow[0:1, :]))
            chain(v.tensor_copy(table[0:1, NE + JC:NE + JC + 1], jend[0:1, NE - 1:NE]))
            jst, jen, jst64 = misc[0:NE, 9:10], misc[0:NE, 10:11], misc[0:NE, 11:12]
            pqw = ffn[0:NE, 0:512]
            oh, oh1 = ffn[0:NE, 512:512 + JC], ffn[0:NE, 576:576 + JC]
            dve.wait_ge(s["jt_ps"], 1)
            settle()
            chain(v.tensor_copy(misc[0:NE, 9:11], B[7][0:NE, 0:2]))
            settle()
            chain(v.tensor_scalar(jst64, jst, float(SLOTS), None, ALU.mult))
            chain(v.tensor_scalar(oh1, const("iota")[0:NE, :], jst, None, ALU.is_ge))
            settle()
            dve.wait_ge(s["hb1"], 2)
            chain(v.scalar_tensor_tensor(out=oh, in0=const("iota")[0:NE, :], scalar=jen, in1=oh1, op0=ALU.is_lt, op1=ALU.mult))
            chain(v.tensor_scalar(pqw[:, 0:S], B[6][0:NE, 0:S], jst64, None, ALU.add))
            v.tensor_copy(pqw[:, S:2 * S], B[6][0:NE, S:2 * S]).then_inc(s["oh_v"], 1)
            dve.wait_ge(s["job_ps"], 1)
            for t in range(NT):
                chain(v.scalar_tensor_tensor(out=posj[:, t * JC:(t + 1) * JC], in0=const("iota"), scalar=-float(SLOTS),
                                             in1=B[7][:, 128 + t * JC:128 + (t + 1) * JC], op0=ALU.mult, op1=ALU.add))
            chain(v.tensor_copy(posj[:, 2 * JC:4 * JC], B[7][:, 128 + 2 * JC:128 + 4 * JC]))
            v.tensor_copy(table[0:1, NE:NE + JC], B[7][0:1, 128 + 4 * JC:128 + 5 * JC]).then_inc(s["tab_v"], 1)
            dve.wait_ge(s["y0_ps"], 1)
            dve.wait_ge(s["h2t_ps"], 4)
            for i in range(4):
                v.tensor_copy(acc[:, i * 512:(i + 1) * 512], B[2 + i][:, :]).then_inc(s["y0_v"], 1)
            chain(v.memset(swt, 0.0))
            chain(v.memset(ysb, 0.0))
            v.memset(cab, 0.0).then_inc(s["cnt_v"], 1)
            slot_row = const("slot")
            settle()

            def gather_select(j):
                for t in range(NT):
                    ins = v.tensor_scalar(sgat[:, t * SLOTS:(t + 1) * SLOTS], slot_row, posj[:, bass.ds(j + t * JC, 1)], None, ALU.is_equal)
                    if t == 0:
                        chain(ins)
                ins.then_inc(s["selg"], 1)

            gather_select(0)
            J = dve.value_load(table[0:1, NE + JC:NE + JC + 1], min_val=NE, max_val=MAXJ)
            before_loop = done[0]
            PER = 12
            dve.sem_inc(s["gu_v"], 1)
            dve.sem_inc(s["act_v"], 2)
            dve.sem_inc(s["accd"], 4)
            with dve.Fori(0, J) as j:
                done[0] = 0

                def settle_j():
                    dve.wait_ge(s["vch"], j * PER + (before_loop + done[0]))

                def chain_j(ins):
                    done[0] += 1
                    ins.then_inc(s["vch"], 1)

                dve.wait_ge(s["gat"], j + 1)
                for t in range(NT):
                    ins = v.tensor_scalar(sgat[:, t * SLOTS:(t + 1) * SLOTS], slot_row, posj[:, bass.ds(j + (t * JC + 1), 1)], None, ALU.is_equal)
                    if t == 0:
                        chain_j(ins)
                ins.then_inc(s["selg"], 1)
                dve.wait_ge(s["ctr"], j + 1)
                for t in range(NT):
                    ins = v.tensor_scalar(swt[:, t * 192 + SLOTS:t * 192 + 2 * SLOTS], slot_row, posj[:, bass.ds(j + t * JC, 1)],
                                          posj[:, bass.ds(j + (2 + t) * JC, 1)], ALU.is_equal, ALU.mult)
                    if t == 0:
                        chain_j(ins)
                ins.then_inc(s["selw"], 1)
                dve.wait_ge(s["gu"], j + 1)
                v.tensor_copy(gus[:, 512:1024], B[1][:, :]).then_inc(s["gu_v"], 1)
                bj3 = bJ.rearrange("p (c j) -> p c j", j=JC)
                for q in range(2):
                    bt = B[(2, 5)[q]][:, :].rearrange("p (c x) -> p c x", c=4)
                    gq, uq, sq = (x[:, q * 256:(q + 1) * 256] for x in (tg, tu, ts))
                    g3, u3 = (x.rearrange("p (c x) -> p c x", c=4) for x in (gq, uq))
                    dve.wait_ge(s["trn"], 2 * j + q + 1)
                    if q == 0:
                        dve.wait_ge(s["sg_rdy"], 2 * j + 2)
                    chain_j(v.tensor_tensor(g3, bt[:, :, 0:64], bj3[:, 4 * q:4 * q + 4, bass.ds(j, 1)].broadcast_to([P, 4, 64]), ALU.add))
                    chain_j(v.tensor_tensor(u3, bt[:, :, 64:128], bj3[:, 8 + 4 * q:12 + 4 * q, bass.ds(j, 1)].broadcast_to([P, 4, 64]), ALU.add))
                    settle_j()
                    v.tensor_scalar(gq, gq, LIMIT, None, ALU.min).then_inc(s["g_rdy"], 1)
                    chain_j(v.tensor_scalar(uq, uq, LIMIT, -LIMIT, ALU.min, ALU.max))
                    settle_j()
                    dve.wait_ge(s["g_rdy"], 2 * j + q + 1)
                    chain_j(v.scalar_tensor_tensor(out=uq, in0=uq, scalar=1.0, in1=gq, op0=ALU.add, op1=ALU.mult))
                    settle_j()
                    dve.wait_ge(s["sg_rdy"], 2 * j + q + 3)
                    if q == 0:
                        dve.wait_ge(s["yd"], j + 1)
                    v.tensor_tensor(actT[:, q * 256:(q + 1) * 256], uq, sq, ALU.mult).then_inc(s["act_v"], 1)
                    for i in (2 * q, 2 * q + 1):
                        dve.wait_ge(s["sc"], 4 * j + i + 1)
                        dve.wait_ge(s["accd"], 4 * j + i + 4)
                        a = acc[:, i * 512:(i + 1) * 512]
                        v.tensor_tensor(a, a, B[6 + i % 2][:, :], ALU.add).then_inc(s["accd"], 1)
                for _ in range(PER - done[0]):
                    chain_j(v.engine_nop())
            for i in range(4):
                dve.wait_ge(s["sc"], 4 * J + (i + 1))
                a = acc[:, i * 512:(i + 1) * 512]
                v.tensor_tensor(a, a, B[6 + i % 2][:, :], ALU.add).then_inc(s["accd"], 1)
            dve.wait_ge(s["fss"], 2)
            root_arg(ssum[:, 10:12], ssum[:, 8:10], 1.0 / D, EPS).then_inc(s["fsr"], 1)
            dve.wait_ge(s["fss"], 3)
            v.reciprocal(rsc[:, 10:12], rsc[:, 8:10]).then_inc(s["fsr"], 1)
            dve.wait_ge(s["fsr"], 2)
            for t in range(NT):
                a = slice(t * D, (t + 1) * D)
                v.scalar_tensor_tensor(out=gv[1][:, a], in0=acc[:, a], scalar=rsc[:, 10 + t:11 + t], in1=GF, op0=ALU.mult, op1=ALU.mult).then_inc(s["fsr"], 1)
                dve.wait_ge(s["fsr"], 3 + t)
                v.tensor_tensor(xs[:, a], xs[:, a], gv[1][:, a], ALU.add).then_inc(s["fo"], 1)

        @block.tensor
        def _(pe):
            def sum8(out_ap, lhs, rhs):
                for k in range(KD):
                    ins = pe.matmul(out_ap, lhs(k), rhs(k), start=(k == 0), stop=(k == KD - 1))
                return ins

            def free_bank(use):
                if use >= 2:
                    kind = readers[use - 2]
                    if kind == "a":
                        pe.wait_ge(s["a_read"], reads("a", use - 2))
                    else:
                        pe.wait_ge(s["conv"], reads("v", use - 2))

            def unit(i, k=KD):
                pe.wait_ge(landed[i % MIX_RING], 16 * (i // MIX_RING + 1))
                return slot(i % MIX_RING).rearrange("p (k n) -> p k n", k=k)

            pe.wait_ge(s["const_in"], 16)
            pe.wait_ge(s["sq_x"], 1)
            sum8(B[7][:, 0:S], lambda k: ones, lambda k: rows[:, k * S:(k + 1) * S]).then_inc(s["ss_x"], 1)
            sil3 = silc[:, :].rearrange("p (k n) -> p k n", n=32)

            def ada_pair(first, use):
                free_bank(use)
                for n in range(2):
                    w = unit(first + n)
                    for k in range(KD):
                        q = k % 4
                        ins = pe.matmul(B[use % 2][32 * q:32 * q + 32, n * BLK:(n + 1) * BLK], sil3[:, k, :], w[:, k, :],
                                        start=(k < 4), stop=(k >= 4), tile_position=(0, 32 * q))
                    if n == 0:
                        ins.then_inc(s["unit_used"], 1)
                ins.then_inc(s["proj"], 1)
                pe.wait_ge(s["proj"], use + 1)
                pe.sem_inc(s["unit_used"], 1)

            pe.wait_ge(s["silu_c"], 1)
            for q in range(4):
                ada_pair(2 * q, q)
            pe.wait_ge(s["a_read"], 4)
            for j in range(16):
                ins = pe.matmul(B[6][:, j:j + 1], rows[:, j * P:(j + 1) * P], ones[:, 0:1], start=True, stop=True)
            ins.then_inc(s["col_ps"], 1)
            pe.wait_ge(s["wba_in"], 16)
            pe.wait_ge(s["h_ok"], 8)
            w8 = wba[:, :].rearrange("p (k n) -> p k n", k=KD)
            sum8(B[7][0:8, 0:S], lambda k: w8[:, k, :], lambda k: hTk[:, k, :]).then_inc(s["ba_ps"], 1)

            def project(i, use):
                free_bank(use)
                w = unit(i)
                for c in range(2):
                    ins = sum8(B[use % 2][:, c * S:(c + 1) * S], lambda k: w[:, k, c * P:(c + 1) * P], lambda k: hTk[:, k, :])
                ins.then_inc(s["proj"], 1)
                pe.wait_ge(s["proj"], use + 1)
                pe.sem_inc(s["unit_used"], 1)

            def project_v(i, use):
                free_bank(use)
                w = unit(i)
                for t in range(NT):
                    ins = sum8(B[use % 2][:, t * BLK:(t + 1) * BLK], lambda k: hTk[:, k, t * P:(t + 1) * P], lambda k: w[:, k, :])
                ins.then_inc(s["proj"], 1)
                pe.wait_ge(s["proj"], use + 1)
                pe.sem_inc(s["unit_used"], 1)

            def norm_sums(which):
                pe.wait_ge(s["sq_k"], which + 1)
                for h in range(H):
                    ins = pe.matmul(B[2 + 2 * which + h // 2][:, (h % 2) * S:(h % 2) * S + S], ones, squares[:, h * S:(h + 1) * S],
                                    start=True, stop=True)
                ins.then_inc(s["ss_ps"], 1)

            project(8, Q0)
            pe.wait_ge(s["ba_sb"], 1)
            for t in range(NT):
                ins = pe.matmul(B[7][:, 256 + 8 * t:264 + 8 * t], baT[:, t * P:(t + 1) * P], ident[0:8, 0:8], start=True, stop=True)
            ins.then_inc(s["bat_ps"], 1)
            project(9, Q0 + 1)
            project(10, Q0 + 2)
            norm_sums(0)
            pe.wait_ge(s["g_ok"], 1)
            for i, n in enumerate(("tri", "blockones", "firsthalf", "secondhalf")):
                ins = pe.matmul(B[7][:, 8 * i:8 * i + 8], const(n), g, start=True, stop=True)
            ins.then_inc(s["cum_ps"], 1)
            project(11, Q0 + 3)
            project(12, Q0 + 4)
            norm_sums(1)
            project(13, Q0 + 5)

            def token_layout(src, t, bank):
                for h in range(H):
                    ins = pe.transpose(bank[:, h * HD:(h + 1) * HD], src[:, h * S + t * P:h * S + (t + 1) * P], ident)
                ins.then_inc(s["tr_ps"], 1)

            project(14, Z0)
            pe.wait_ge(s["qk_n"], 1)
            pe.wait_ge(s["ss_e"], 1)
            for t in range(NT):
                token_layout(kT, t, B[2 + t])
            project(15, Z0 + 1)
            pe.wait_ge(s["ract"], 6)
            pe.wait_ge(s["ss_e"], 2)
            for t in range(NT):
                token_layout(vT, t, B[4 + t])

            def decay_rows(t):
                if t == 1:
                    pe.wait_ge(s["dt_v"], 1)
                    pe.wait_ge(s["egb_a"], 1)
                for h in range(H):
                    c = t * H + h
                    ins = pe.matmul(B[6][:, h * HD:(h + 1) * HD], g[:, c:c + 1].broadcast_to([P, P]), const("tri"), start=True, stop=True)
                ins.then_inc(s["gcb_ps"], 1)
                if t == 1:
                    pe.wait_ge(s["lt_v"], 1)
                else:
                    pe.wait_ge(s["cum_a"], 2)
                    pe.wait_ge(s["cum_v"], 1)
                for h in range(H):
                    c = t * H + h
                    ins = pe.matmul(B[7][:, h * HD:(h + 1) * HD], beta[:, c:c + 1].broadcast_to([P, P]), ident, start=True, stop=True)
                ins.then_inc(s["bb_ps"], 1)

            def products(t):
                if t == 0:
                    pe.wait_ge(s["ktok"], 2 * NT * H)
                    pe.wait_ge(s["ktv"], NT * H)
                    pe.wait_ge(s["qk_n"], 2)
                for i, x in enumerate((kT, qT)):
                    for h in range(H):
                        a = slice(h * S + t * P, h * S + (t + 1) * P)
                        ins = pe.matmul(B[2 + 2 * i + t][:, h * HD:(h + 1) * HD], kT[:, a], x[:, a], start=True, stop=True)
                ins.then_inc(s["kk_ps"], 1)

            decay_rows(0)
            project(16, MB0)
            products(0)
            project(17, MB0 + 1)
            decay_rows(1)
            products(1)
            project(18, MB0 + 2)
            for t in range(NT):
                pe.wait_ge(s["lt_v"], t + 1)
                for h in range(H):
                    ins = pe.transpose(B[2 + t][:, h * HD:(h + 1) * HD], head(LT, t, h), ident)
                ins.then_inc(s["l_ps"], 1)
            project(19, MB0 + 3)

            def double_a(l, t):
                pe.wait_ge(s["t1_v"], 2 * NT) if l == 1 else pe.wait_ge(s["tt_v"], (l - 2) * NT + t + 1)
                for h in range(H):
                    ins = pe.matmul(B[2 + t][:, h * HD:(h + 1) * HD], head(LT, t, h), head(T, t, h), start=True, stop=True)
                ins.then_inc(s["a_ps"], 1)

            def double_x(l, t):
                pe.wait_ge(s["m_v"], (l - 1) * NT + t + 1)
                if l == 1:
                    pe.wait_ge(s["qk_v"], t + 1)
                if l < 5:
                    for h in range(H):
                        pe.matmul(B[4 + t][:, h * HD:(h + 1) * HD], head(TT, t, h), head(M, t, h), start=True, stop=True)
                for h in range(H):
                    ins = pe.matmul(B[6 + t][:, h * HD:(h + 1) * HD], head(M, t, h), head(TT, t, h), start=True, stop=True)
                ins.then_inc(s["x_ps"], 1)

            def filler(n):
                if n < 2:
                    project_v(20 + n, MV0 + n)
                elif n < 10:
                    project(22 + n - 2, GA0 + n - 2)

            for l in range(1, 6):
                for t in range(NT):
                    double_a(l, t)
                filler(2 * l - 2)
                for t in range(NT):
                    double_x(l, t)
                filler(2 * l - 1)

            def mod_rows(v):
                ada_pair(30 + 4 * v, AD0 + 2 * v)
                ada_pair(32 + 4 * v, AD0 + 2 * v + 1)
                pe.wait_ge(s["a_read"], reads("a", AD0 + 2 * v + 1))
                if v == 0:
                    pe.wait_ge(s["tt_v"], 5 * NT)
                else:
                    pe.wait_ge(s["mod_a"], v)
                for n in range(2):
                    a = (v % 2) * D + n * 512
                    ins = pe.matmul(B[4 + n][:, :], ones, rows[:, a:a + 512], start=True, stop=True)
                ins.then_inc(s["mod_ps"], 1)

            mod_rows(0)
            mod_rows(1)
            for t in range(NT):
                pe.wait_ge(s["tt_v"], 4 * NT + t + 1)
                for h in range(H):
                    pe.matmul(B[2 + t][:, h * HD:(h + 1) * HD], head(TT, t, h), head(vb, t, h), start=True, stop=True)
                for h in range(H):
                    ins = pe.matmul(B[6 + t][:, h * HD:(h + 1) * HD], head(kbg, t, h), head(TT, t, h), start=True, stop=True)
                ins.then_inc(s["uw_ps"], 1)
            mod_rows(2)
            mod_rows(3)

            for n in range(4):
                t, hf = n // 2, n % 2
                r = slice(CHUNK * hf, CHUNK * hf + CHUNK)
                at = (0, CHUNK * hf)
                vnb = vn[:, hf * TW:(hf + 1) * TW]
                if n == 0:
                    pe.wait_ge(s["uw_a"], 4)
                else:
                    pe.wait_ge(s["s_v"], n)
                    for h in range(H):
                        ins = pe.matmul(B[6][r, h * HD:(h + 1) * HD], head(wT, t, h)[:, r], state[:, h * HD:(h + 1) * HD],
                                        start=True, stop=True, tile_position=at)
                    ins.then_inc(s["ws_ps"], 1)
                if n == 0:
                    pe.wait_ge(s["rope_v"], 2)
                    pe.wait_ge(s["a_read"], reads("a", len(readers) - 1))
                else:
                    pe.wait_ge(s["ob_a"], n)
                q0 = n * S
                pe.matmul(B[0][:, 0:P], mq[:, q0:q0 + P], mk[:, q0:q0 + P], start=True, stop=True)
                pe.matmul(B[0][:, P:3 * P], mq[:, q0 + P:q0 + 2 * P], mk[:, q0:q0 + S], start=True, stop=True).then_inc(s["sc_ps"], 1)
                pe.wait_ge(s["vn_v"], n + 1)
                for h in range(H):
                    o = B[2 + t][r, h * HD:(h + 1) * HD]
                    if n:
                        pe.matmul(o, head(qd, t, h)[:, r], state[:, h * HD:(h + 1) * HD], start=True, stop=False, tile_position=at)
                    ins = pe.matmul(o, head(QK, t, h)[:, r], vnb[:, h * HD:(h + 1) * HD], start=(n == 0), stop=True, tile_position=at)
                ins.then_inc(s["o_ps"], 1)
                if n < 3:
                    for h in range(H):
                        ins = pe.matmul(B[7][:, h * HD:(h + 1) * HD], head(ktl, t, h), vnb[:, h * HD:(h + 1) * HD], start=True, stop=True)
                    ins.then_inc(s["st_ps"], 1)
                p = prob[:, (n % 2) * 768:(n % 2) * 768 + 384]
                pt = prob[:, (n % 2) * 768 + 384:(n % 2) * 768 + 768]
                pe.wait_ge(s["pn_v"], 2 * n + 2)
                if n:
                    pe.wait_ge(s["pt_a"], n)
                for i in range(3):
                    ins = pe.transpose(B[1][:, i * P:(i + 1) * P], p[:, i * P:(i + 1) * P], ident)
                ins.then_inc(s["pt_ps"], 1)
                pe.wait_ge(s["pt_a"], n + 1)
                pe.matmul(B[0][:, 0:P], head(mv, 0, n), pt[:, 0:P], start=True, stop=True)
                pe.matmul(B[0][:, P:S], head(mv, 0, n), pt[:, P:2 * P], start=True, stop=False)
                pe.matmul(B[0][:, P:S], head(mv, 1, n), pt[:, 2 * P:3 * P], start=False, stop=True).then_inc(s["ob_ps"], 1)

            pe.wait_ge(s["mod_a"], 4)
            for t in range(NT):
                pe.wait_ge(s["ro_v"], 1 + H * (t + 1))
                for h in range(H):
                    ins = pe.transpose(B[4 + t][:, h * HD:(h + 1) * HD], head(otok, t, h), ident)
                ins.then_inc(s["ot_ps"], 1)
            pe.wait_ge(s["ot_ps"], 2)
            pe.sem_inc(s["scratch_dead"], 1)
            pe.wait_ge(s["oa_v"], 2)
            pe.wait_ge(s["ob_a"], H)
            pe.wait_ge(s["o_a"], 4)
            for j in range(KD):
                wa, wb = unit(46 + 2 * (j // 4), H), unit(47 + 2 * (j // 4), H)
                if j >= 2:
                    pe.wait_ge(s["ya_v"], j - 1)
                for i, (w, o) in enumerate(((wa, oaT), (wb, obT))):
                    for k in range(H):
                        ins = pe.matmul(B[2 + j % 2][:, i * S:(i + 1) * S], w[:, k, (j % 4) * P:(j % 4 + 1) * P],
                                        o[:, k * S:(k + 1) * S], start=(k == 0), stop=(k == H - 1))
                ins.then_inc(s["ya_ps"], 1)
                if j % 4 == 3:
                    pe.wait_ge(s["ya_ps"], j + 1)
                    pe.sem_inc(s["unit_used"], 2)
            pe.wait_ge(s["ya_v"], KD)
            for n in range(4):
                w = unit(50 + n)
                if n >= 2:
                    pe.wait_ge(s["mix_a"], n - 1)
                for t in range(NT):
                    ins = sum8(B[n % 2][:, t * BLK:(t + 1) * BLK], lambda k: hTk[:, k, t * P:(t + 1) * P], lambda k: w[:, k, :])
                ins.then_inc(s["mix_ps"], 1)
                pe.wait_ge(s["mix_ps"], n + 1)
                pe.sem_inc(s["unit_used"], 1)

            pe.wait_ge(s["h2"], 2)
            pe.wait_ge(s["mix_a"], 4)
            for n in range(4):
                for kk in range(2):
                    for t in range(NT):
                        k = 2 * n + kk
                        ins = pe.transpose(B[n][:, kk * S + t * P:kk * S + (t + 1) * P], gv[0][:, t * D + k * P:t * D + (k + 1) * P], ident)
                ins.then_inc(s["h2t_ps"], 1)
            pe.wait_ge(s["h2t"], 4)
            pe.wait_ge(s["x2_in"], 64)
            w3 = wrt[:, :].rearrange("p (k n) -> p k n", k=KD)
            for t in range(NT):
                ins = sum8(B[4][:, t * NE:(t + 1) * NE], lambda k: hTk[:, k, t * P:(t + 1) * P], lambda k: w3[:, k, :])
            ins.then_inc(s["lg_ps"], 1)
            selt, posm, wts = rt[:, 128:192], rt[:, 320:384], rt[:, 384:448]
            pe.wait_ge(s["sel_v"], 1)
            pe.matmul(B[5][:, 0:NE], const("before"), selt[:, 0:NE], start=True, stop=True)
            pe.matmul(B[5][:, NE:2 * NE], const("before"), selt[:, NE:2 * NE], start=True, stop=False)
            pe.matmul(B[5][:, NE:2 * NE], ones, selt[:, 0:NE], start=False, stop=True)
            for t in range(NT):
                pe.matmul(B[5][:, 2 * NE:3 * NE], ones, selt[:, t * NE:(t + 1) * NE], start=(t == 0), stop=(t == 1))
            for t in range(NT):
                ins = pe.matmul(B[5][0:NE, 96:97], selt[:, t * NE:(t + 1) * NE], ones[:, 0:1], start=(t == 0), stop=(t == 1))
            ins.then_inc(s["pos_ps"], 1)
            pe.wait_ge(s["pos_v"], 1)
            ncol = rt[0:NE, 520:521]
            pe.matmul(B[7][0:NE, 0:1], const("ntri32")[0:NE, :], ncol, start=True, stop=True)
            pe.matmul(B[7][0:NE, 1:2], const("tri32")[0:NE, :], ncol, start=True, stop=True)
            for i, x in enumerate((posm, wts)):
                for t in range(NT):
                    ins = pe.transpose(B[6][0:NE, (2 * i + t) * P:(2 * i + t + 1) * P], x[:, t * NE:(t + 1) * NE], ident)
            ins.then_inc(s["jt_ps"], 1)
            pe.wait_ge(s["oh_v"], 1)
            pqw, oh = ffn[0:NE, 0:512], ffn[0:NE, 512:512 + JC]
            for i in range(4):
                pe.matmul(B[7][:, 128 + i * JC:128 + (i + 1) * JC], pqw[:, i * P:(i + 1) * P], oh, start=True, stop=True)
            pe.matmul(B[7][0:1, 128 + 4 * JC:128 + 5 * JC], const("expert")[0:NE, :], oh, start=True, stop=True).then_inc(s["job_ps"], 1)
            pe.wait_ge(s["bdn_in"], 16)
            for t in range(NT):
                for n in range(2):
                    ins = pe.matmul(B[2 + 2 * t + n][:, :], pqw[:, S + t * P:S + (t + 1) * P], bdn[:, n * 512:(n + 1) * 512], start=True, stop=True)
            ins.then_inc(s["y0_ps"], 1)
            pe.wait_ge(s["expert_rows"], 16)
            for n in range(2):
                for c in range(8):
                    ins = pe.matmul(B[n][:, c * JC:(c + 1) * JC], bgu[:, (8 * n + c) * P:(8 * n + c + 1) * P], oh, start=True, stop=True)
                ins.then_inc(s["bj_ps"], 1)
            pe.wait_ge(s["y0_v"], 4)

            def gather():
                for c in range(KD):
                    for i in range(3):
                        for t in range(NT):
                            ins = pe.matmul(B[3][:, c * SLOTS:(c + 1) * SLOTS], hb[:, i, t, c * P:(c + 1) * P],
                                            sgat[:, t * SLOTS:(t + 1) * SLOTS], start=(i == 0 and t == 0), stop=(i == 2 and t == 1))
                ins.then_inc(s["gat"], 1)

            pe.wait_ge(s["hb1"], 2)
            pe.wait_ge(s["selg"], 1)
            gather()
            pe.wait_ge(s["bj_a"], 2)
            pe.wait_ge(s["cnt_v"], 1)
            pe.wait_ge(s["tab_v"], 1)
            J = pe.value_load(table[0:1, NE + JC:NE + JC + 1], min_val=NE, max_val=MAXJ)
            pe.sem_inc(s["ctr"], 1)
            pe.sem_inc(s["yd"], 1)
            with pe.Fori(0, J) as j:
                e = pe.value_load(table[0:1, bass.ds(j + NE, 1)], min_val=0, max_val=NE - 1)

                def weights(u):
                    pe.wait_ge(landed[u], e * 16 + (16 * (ROUNDS + 1) if u < MIX_RING else 16))
                    return slot(u)

                pe.wait_ge(s["xg_a"], j + 1)
                pe.wait_ge(s["gu_a"], j + 1)
                pe.wait_ge(s["gu_v"], j + 1)
                for u in range(GU_UNITS):
                    w = weights(u)
                    for n in range(2):
                        for half in range(2):
                            ins = pe.matmul(B[n][64 * half:64 * half + 64, :], xg[:, u * SLOTS:(u + 1) * SLOTS],
                                            w[:, half * F + n * 512:half * F + (n + 1) * 512], start=(u == 0), stop=(u == GU_UNITS - 1),
                                            tile_position=(0, 64 * half))
                    ins.then_inc(used[u], 1)
                pe.wait_ge(used[GU_UNITS - 1], j + 1)
                pe.sem_inc(s["gu"], 1)
                pe.wait_ge(s["selg"], j + 2)
                pe.wait_ge(s["c_a"], j + 1)
                gather()
                for q in range(2):
                    if q == 0:
                        pe.wait_ge(s["gu_a"], j + 2)
                        pe.wait_ge(s["act_v"], 2 * j + 2)
                    else:
                        pe.wait_ge(s["gu_v"], j + 2)
                    for c in range(4):
                        ins = pe.transpose(B[(2, 5)[q]][:, c * P:(c + 1) * P], gus[:, (4 * q + c) * P:(4 * q + c + 1) * P], ident)
                    ins.then_inc(s["trn"], 1)
                pe.wait_ge(s["y_a"], j + 1)
                pe.wait_ge(s["c_a"], j + 1)
                for i in range(4):
                    if i >= 2:
                        pe.wait_ge(s["accd"], 4 * j + (i + 3))
                    else:
                        pe.wait_ge(s["accd"], 4 * j + 4)
                    pe.matmul(B[6 + i % 2][:, :], cab[:, i * P:(i + 1) * P], ysb, start=True, stop=True).then_inc(s["sc"], 1)
                pe.wait_ge(s["selw"], j + 1)
                pe.wait_ge(s["xg_a"], j + 2)
                for t in range(NT):
                    for half in range(2):
                        ins = pe.transpose(B[3][:, (2 * t + half) * P:(2 * t + half + 1) * P],
                                           swt[:, t * 192 + 64 - 64 * half:t * 192 + 192 - 64 * half], ident)
                ins.then_inc(s["ctr"], 1)
                for f in range(KF):
                    u = GU_UNITS + f // 2
                    if f == 0:
                        pe.wait_ge(s["act_v"], 2 * j + 3)
                    if f == 4:
                        pe.wait_ge(s["act_v"], 2 * j + 4)
                    w = weights(u) if f % 2 == 0 else slot(u)
                    for half in range(2):
                        ins = pe.matmul(B[4][64 * half:64 * half + 64, :], actT[:, f * SLOTS:(f + 1) * SLOTS],
                                        w[:, (f % 2) * D + half * 512:(f % 2) * D + (half + 1) * 512], start=(f == 0), stop=(f == KF - 1),
                                        tile_position=(0, 64 * half))
                    if f % 2:
                        ins.then_inc(used[u], 1)
                pe.wait_ge(used[RING - 1], j + 1)
                pe.sem_inc(s["yd"], 1)
            pe.wait_ge(s["y_a"], J + 1)
            pe.wait_ge(s["c_a"], J + 1)
            for i in range(4):
                pe.wait_ge(s["accd"], 4 * J + (4 if i < 2 else i + 3))
                pe.matmul(B[6 + i % 2][:, :], cab[:, i * P:(i + 1) * P], ysb, start=True, stop=True).then_inc(s["sc"], 1)


def kernel(**inputs):
    import concourse.bacc as bacc
    from concourse.bass_utils import run_bass_kernel_spmd

    def arr(n):
        return np.asarray(inputs[n])

    def columns(v, n):
        return np.ascontiguousarray(v.reshape(n, P).T)

    x = arr("x")[0]
    data = {
        "x": x, "xT": np.ascontiguousarray(x.T), "c_col": columns(arr("c")[0], KD),
        "w_ada": arr("w_ada")[0], "b_ada": arr("b_ada"), "b_ada_col": columns(arr("b_ada")[0][:2 * D], 16),
        "g_pre_col": columns(arr("g_pre_mix")[0], KD), "w_in": arr("w_in")[0],
        "g_post_mix": arr("g_post_mix"), "g_pre_ffn": arr("g_pre_ffn"), "g_post_ffn": arr("g_post_ffn"),
        "conv_col": np.ascontiguousarray(arr("conv_w")[0].reshape(TAPS, 12, P).transpose(2, 1, 0).reshape(P, 12 * TAPS)),
        "a_log": arr("a_log"), "dt_bias": arr("dt_bias"), "g_dn_col": columns(arr("g_dn_out")[0], 1),
        "w_br_a": arr("w_br_a")[0], "w_br_b": arr("w_br_b")[0], "w_o": arr("w_o")[0],
        "w_router": arr("w_router")[0], "b_router": arr("b_router"),
        "w_gu": arr("w_gu")[0], "b_gu": arr("b_gu")[0], "w_down": arr("w_down")[0], "b_down": arr("b_down")[0],
        "cst": shape_constants(),
    }
    nc = bacc.Bacc("TRN2", target_bir_lowering=False, num_devices=1)
    arrays, A = {}, {}
    for n, a in data.items():
        a = np.ascontiguousarray(a)
        arrays[f"in_{n}"] = a
        A[n] = nc.dram_tensor(f"in_{n}", a.shape, mybir.dt.from_np(a.dtype), kind="ExternalInput").ap()
    out = nc.dram_tensor("out_0", (S, D), F32, kind="ExternalOutput").ap()
    build(nc, A, out)
    r = run_bass_kernel_spmd(nc, [arrays], core_ids=[0])
    return r.results[0]["out_0"].reshape(1, S, D)
```

```python
import numpy as np
import concourse.bass as bass
from concourse import mybir
from contextlib import ExitStack

F32 = mybir.dt.float32
BF16 = mybir.dt.bfloat16
I32 = mybir.dt.int32
ALU = mybir.AluOpType
ACT = mybir.ActivationFunctionType
AX = mybir.AxisListType

P = 128
D = 1024
S = 256
NT = S // P
KD = D // P
HD = 128
H = 4
W = H * HD
CHUNK = 64
TAPS = 4
HALF_ROPE = HD // 8
NE = 32
TOPK = 4
F = 1024
KF = F // P
SLOTS = 64
MAXJ = NE + S * TOPK // SLOTS
JC = MAXJ + 1
EPS = 1e-6
LIMIT = 7.0
ALPHA = 1.702
NEG = -1e30

BLK = 256
UNIT = KD * BLK
GU_UNITS = KD
DN_UNITS = KF // 2
UPE = GU_UNITS + DN_UNITS
RING = 16
ROW_BANK = (6, 7, 0, 1)
GROUP = 4
LAPS = GROUP * UPE // RING
OWN = 12
MIX_RING = 6

CONST = {}
_at = 0
for _name, _n in (("ident", 128), ("ones", 128), ("tri", 128), ("blockones", 128), ("firsthalf", 128),
                  ("secondhalf", 128), ("decaymask", 128), ("strict", 128), ("level", 6 * 128), ("level1t", 128),
                  ("before", 128), ("causal", 128), ("iota", JC), ("slot", SLOTS), ("cos", S), ("sin", S),
                  ("tri32", 32), ("ntri32", 32)):
    CONST[_name] = (_at, _n)
    _at += _n
NCONST = _at


def shape_constants():
    c = np.zeros((P, NCONST), np.float32)

    def put(name, value):
        a, n = CONST[name]
        c[:value.shape[0], a:a + n] = value

    i, j = np.arange(P)[:, None], np.arange(P)[None, :]
    same = i // CHUNK == j // CHUNK
    put("ident", (i == j).astype(np.float32))
    put("ones", np.ones((P, P), np.float32))
    put("tri", ((i <= j) & same).astype(np.float32))
    put("blockones", same.astype(np.float32))
    put("firsthalf", (i + 0 * j < CHUNK).astype(np.float32))
    put("secondhalf", (i + 0 * j >= CHUNK).astype(np.float32))
    put("decaymask", np.where((i <= j) & same, 0.0, NEG).astype(np.float32))
    put("strict", ((i < j) & same).astype(np.float32))
    levels = []
    for s in (1, 2, 4, 8, 16, 32):
        m = (i // (2 * s) == j // (2 * s)) & (i // s % 2 == 1) & (j // s % 2 == 0)
        levels.append(-m.astype(np.float32))
    put("level", np.concatenate(levels, 1))
    put("level1t", levels[0].T)
    put("before", (i < j).astype(np.float32))
    put("causal", np.where(j <= i, 0.0, NEG).astype(np.float32))
    put("iota", np.broadcast_to(np.arange(JC, dtype=np.float32), (P, JC)))
    put("slot", np.broadcast_to(np.arange(SLOTS, dtype=np.float32), (P, SLOTS)))
    inv = np.float32(500000.0) ** (-np.arange(HALF_ROPE, dtype=np.float32) / np.float32(HALF_ROPE))
    ang = (np.arange(S, dtype=np.float32)[:, None] * inv[None, :]).astype(np.float32).astype(np.float64)
    cos, sin = np.cos(ang).T.astype(np.float32), np.sin(ang).T.astype(np.float32)
    put("cos", np.concatenate([cos, cos]))
    put("sin", np.concatenate([-sin, sin]))
    e = np.arange(NE)
    put("tri32", (e[:, None] <= e[None, :]).astype(np.float32))
    put("ntri32", (e[:, None] < e[None, :]).astype(np.float32))
    return c


def build(nc, A, out):
    ctx = ExitStack()
    with ctx:
        def sb(name, shape, dt=F32):
            return ctx.enter_context(nc.sbuf_tensor(name, shape, dt))

        def sem(name):
            return ctx.enter_context(nc.semaphore(name))

        B = [ctx.enter_context(nc.psum_tensor(f"bank{i}", [P, 512], F32)) for i in range(8)]

        ring = sb("ring", [P, OWN * UNIT])
        cst = sb("cst", [P, NCONST])
        hT = sb("hT", [P, KD * S])
        qkv = sb("qkv", [P, 3 * H * S])
        zT = sb("zT", [P, H * S])
        mbx = sb("mbx", [P, 3 * H * S])
        gates = sb("gates", [P, 2 * KD * S])
        oT = sb("oT", [P, 2 * H * S])
        rows = sb("rows", [P, 2 * D])
        xs = sb("xs", [P, NT * D])
        mod = sb("mod", [P, 5 * D])
        col = sb("col", [P, 8 + 16 + 48 + 1 + 8 + 8])
        wba = sb("wba", [P, KD * 8])
        wrt = sb("wrt", [P, KD * NE])
        sm = sb("sm", [P, 640])
        table = sb("table", [1, NE + 1], I32)

        def const(name):
            a, n = CONST[name]
            return cst[:, a:a + n]

        ident, ones = const("ident"), const("ones")
        gcol, bcol = col[:, 0:8], col[:, 8:24]
        convw = col[:, 24:72]
        gdn = col[:, 72:73]
        ccol = col[:, 73:81]
        hTk = hT[:, :].rearrange("p (k t) -> p k t", k=KD)
        qT, kT, vT = (qkv[:, i * H * S:(i + 1) * H * S] for i in range(3))
        gv = [gates[:, i * KD * S:(i + 1) * KD * S] for i in range(2)]
        oaT, obT = oT[:, 0:H * S], oT[:, H * S:2 * H * S]
        mq, mk, mv = (mbx[:, i * H * S:(i + 1) * H * S] for i in range(3))

        scr = MIX_RING * UNIT

        def scratch(at, n):
            return ring[:, scr + at:scr + at + n]

        TW = H * HD
        vb, kbg, ktl, DT, LT, QK, T, TT, M, qd = (scratch(1024 * i, 1024) for i in range(10))
        state = scratch(10240, TW)
        prob = scratch(10752, 1536)
        silc = prob[:, 1280:1536]
        uu, wT, vn, otok = DT, LT, T, kbg
        squares, rnorm = scratch(1024 * 6, 2048), scratch(1024 * 3, 2048)
        egb = T

        def tile(buf, t):
            return buf[:, t * TW:(t + 1) * TW]

        def head(buf, t, h):
            return buf[:, t * TW + h * HD:t * TW + (h + 1) * HD]

        def small(a, n):
            return sm[:, a:a + n]

        shG = small(0, 16)
        ba = small(16, 16)
        beta, g, gc, eg, etail, bk, t8a, t8b = (small(32 + 8 * i, 8) for i in range(8))
        dec = small(96, 16)
        alog = small(112, 4)
        dtb = small(116, 4)
        ssum = small(120, 16)
        rsc = small(136, 16)
        mx = small(152, 16)
        baT = sm[0:8, 168:168 + S]
        rmsb = small(168, S)
        eps128 = small(424, 4)
        mstat = small(428, 8)
        rbr = small(436, NE)

        hb = qkv[:, :].bitcast(BF16).rearrange("p (s t d) -> p s t d", s=3, t=NT)
        acc = gv[0]
        ffn = gv[1]
        gus = ffn[:, 0:1024]
        ysb = ffn[:, 1024:1536]
        cab = ffn[:, 1536:2048]
        xg = oT[:, 0:512]
        actT = oT[:, 512:1024]
        tg, tu, ts = zT[:, 384:896], oT[:, 1024:1536], oT[:, 1536:2048]
        swt = zT[:, 0:2 * 192]
        bJ = mbx[:, 0:16 * JC]
        rt = zT[:, 384:1024]
        bgu = oT[0:NE, :]
        bdn = mbx[0:NE, 2048:3072]
        lv = const("level")
        posj = lv[:, 0:2 * NT * JC]
        sgat = lv[:, 256:256 + NT * SLOTS // 2].bitcast(BF16)
        GF, GM, SH2, G2 = (mod[:, i * D:(i + 1) * D] for i in range(4))
        gpm, gpf, gqf = (mbx[:, i * D:(i + 1) * D] for i in range(3))

        names = """const_in x_in small_in wba_in x2_in rows_in modb_in bdn_in silu_c zeros sq_x ss_x ssx_e rt_x col_ps h_ok
            unit_used proj conv ract a_read sq_k ss_ps ss_e rtn qk_n ba_ps ba_sb bat_ps ax axe g_ok cum_ps
            cum_a cum_v tr_ps ktok gcb_ps dt_v dt_a egb_a bb_ps kk_ps lt_v qk_v l_ps t1_v a_ps m_v x_ps tt_v
            uw_ps uw_a ws_ps vn_v o_ps o_a st_ps s_v ro_a ro_v ot_ps oa_v rope_v sc_ps mx_v p_a pn_v pt_ps
            pt_a ob_ps ob_a mod_a mod_v ya_ps ya_v mix_ps mix_a xss xsr x1 h2 hb1 h2t_ps h2t lg_ps lg_v ex_a
            sel_v pos_ps pos_v cnt_v jt_ps oh_v job_ps bj_ps bj_a tab_v y0_ps y0_v selg gat xg_a gu_a gu_v
            trn g_rdy sg_rdy act_v ctr c_a y_a sc accd fss fsr fo out_d vch ach scratch_dead expert_rows
            const2_in selw ktv""".split()
        s = {n: sem(n) for n in names}
        landed = [sem(f"landed{i}") for i in range(RING)]
        used = [sem(f"used{i}") for i in range(UPE)]

        plan = "c0 c1 c2 c3 k0 k1 q0 q1 v0 v1 z0 z1 mq0 mq1 mk0 mk1 r0 r1 mv0 M0 M1 r2 r3 mv1 M2 M3 r4 g0 r5 M4 M5 g1"
        plan += " r6 r7 g2 M6 M7 g3 s0 g4 t0 o0 s1 g5 t1 o1 s2 g6 t2 o2 s3 g7 t3 o3"
        plan = plan.split()
        USE = {name: i for i, name in enumerate(plan)}
        IN_COLS = {"q": 0, "k": 512, "v": 1024, "z": 1536, "mq": 2056, "mk": 2568, "mv": 3080, "g": 3592}
        units, UNIT_OF = [], {}
        for name in plan:
            kind, n = name[:-1], int(name[-1])
            if kind in IN_COLS or kind in "cr":
                UNIT_OF[name] = len(units)
            if kind in IN_COLS:
                units.append(("in", IN_COLS[kind] + n * BLK))
            elif kind in "cr":
                first = (2 * D if kind == "r" else 0) + 2 * n * BLK
                units += [("ada", first), ("ada", first + BLK)]
        BR0 = len(units)
        units += [("bra", 0), ("brb", 0), ("bra", 512), ("brb", 512)]
        O0 = len(units)
        units += [("o", i * BLK) for i in range(4)]
        NU = len(units)
        assert NU % MIX_RING == 0
        ROUNDS = NU // MIX_RING

        def reader(name):
            kind = name[:-1]
            if kind in ("q", "k", "v"):
                return "conv"
            return {"M": "mod_a", "s": "mx_v", "t": "pt_a", "o": "ob_a"}.get(kind, "a_read")

        def read_count(use):
            return sum(reader(n) == reader(plan[use]) for n in plan[:use + 1])

        def slot(i):
            if i < OWN:
                return ring[:, i * UNIT:(i + 1) * UNIT]
            return (hT[:, :], rows[:, :], mod[:, D:3 * D], mod[:, 3 * D:5 * D])[i - OWN]

        def landed_count(g):
            return 16 * (g // RING + 1) + (16 * ROUNDS if g % RING < MIX_RING else 0)

        def unit_source(i):
            kind, c = units[i]
            if kind in ("bra", "brb"):
                return A["w_br_a" if kind == "bra" else "w_br_b"][:, c:c + 512].rearrange("(k p) n -> p k n", p=P)
            w = A[{"ada": "w_ada", "in": "w_in", "o": "w_o"}[kind]]
            return w[:, c:c + BLK].rearrange("(k p) n -> p k n", p=P)

        block = ctx.enter_context(nc.Block())

        @block.sync
        def _(sp):
            for i in range(NU):
                if i >= MIX_RING:
                    sp.wait_ge(s["unit_used"], i - MIX_RING + 1)
                v = slot(i % MIX_RING).rearrange("p (k n) -> p k n", k=4 if units[i][0][:2] == "br" else KD)
                sp.dma_start(v, unit_source(i)).then_inc(landed[i % MIX_RING], 16)
                if i == 0:
                    sp.dma_start(wba[:, :].rearrange("p (k n) -> p k n", k=KD),
                                 A["w_in"][:, 2048:2056].rearrange("(k p) n -> p k n", p=P)).then_inc(s["wba_in"], 16)

            def load(e, g):
                u, dst = g % UPE, slot(g % RING)
                if u < GU_UNITS:
                    src = A["w_gu"][bass.ds(e, 1), u * P:(u + 1) * P, :].rearrange("e p n -> p (e n)")
                else:
                    v = u - GU_UNITS
                    src = A["w_down"][bass.ds(e, 1), v * 2 * P:(v + 1) * 2 * P, :].rearrange("e (f p) n -> p (e f) n", p=P)
                    dst = dst.rearrange("p (f n) -> p f n", f=2)
                sp.dma_start(dst, src).then_inc(landed[g % RING], 16)

            def group(e0, g0):
                last = None
                for g in range(g0, GROUP * UPE):
                    before = g - RING
                    de, u = before // UPE, before % UPE
                    if de != last:
                        jobs = sp.value_load(table[0:1, bass.ds(e0 + (de + 1), 1)], min_val=1, max_val=MAXJ)
                        last = de
                    sp.wait_ge(used[u], jobs)
                    load(e0 + g // UPE, g)

            for g in range(RING):
                if g < MIX_RING:
                    sp.wait_ge(s["unit_used"], NU - MIX_RING + g + 1)
                elif g == MIX_RING:
                    sp.wait_ge(s["scratch_dead"], 1)
                elif g == OWN:
                    sp.wait_ge(s["lg_ps"], 1)
                elif g == OWN + 1:
                    sp.wait_ge(s["x1"], 2)
                elif g == OWN + 2:
                    sp.wait_ge(s["h2"], 2)
                load(g // UPE, g)
            sp.wait_ge(s["tab_v"], 1)
            group(0, RING)
            with sp.Fori(1, NE // GROUP) as n:
                group(n * GROUP, 0)
            for t in range(NT):
                sp.wait_ge(s["fo"], t + 1)
                sp.dma_start(out[t * P:(t + 1) * P, :], xs[:, t * D:(t + 1) * D]).then_inc(s["out_d"], 16)
            sp.wait_ge(s["out_d"], 16 * NT)

        @block.gpsimd
        def _(pool):
            pool.memset(silc, 0.0).then_inc(s["zeros"], 1)
            pool.wait_ge(s["proj"], 4)
            pool.dma_start(cst[:, 2 * P:], A["cst"][:, 2 * P:]).then_inc(s["const2_in"], 16)
            for i, c in enumerate((2048, 3072, 4096, 5120)):
                pool.dma_start(mod[:, (i + 1) % 4 * D:((i + 1) % 4 + 1) * D], A["b_ada"][0:1, c:c + D].partition_broadcast(P)).then_inc(s["modb_in"], 16)
            for t in range(NT):
                pool.dma_start(xs[:, t * D:(t + 1) * D], A["x"][t * P:(t + 1) * P, :]).then_inc(s["x2_in"], 16)
            pool.dma_start(rbr, A["b_router"][0:1, :].partition_broadcast(P)).then_inc(s["x2_in"], 16)
            pool.dma_start(wrt[:, :].rearrange("p (k n) -> p k n", k=KD),
                           A["w_router"].rearrange("(k p) n -> p k n", p=P)).then_inc(s["x2_in"], 16)
            pool.wait_ge(s["ob_a"], H)
            for i, n in enumerate(("g_post_mix", "g_pre_ffn", "g_post_ffn")):
                pool.dma_start(mbx[:, i * D:(i + 1) * D], A[n][0:1, :].partition_broadcast(P)).then_inc(s["rows_in"], 16)
            pool.wait_ge(s["mod_v"], 4)
            pool.dma_start(bdn, A["b_down"]).then_inc(s["bdn_in"], 16)
            pool.wait_ge(s["ya_v"], KD)
            pool.dma_start(bgu, A["b_gu"]).then_inc(s["expert_rows"], 16)

        def bank(kind, n):
            return B[USE[f"{kind}{n}"] % 2][:, :]

        def turns(name):
            return sum(n[:-1] not in ("s", "t", "o") for n in plan[:USE[name] + 1])

        @block.scalar
        def _(act):
            def turn_done(kind, n):
                act.wait_ge(s["proj"], turns(f"{kind}{n}"))

            act.dma_start(hTk, A["xT"].rearrange("(k p) t -> p k t", p=P)).then_inc(s["x_in"], 16)
            act.dma_start(col[:, 0:81], A["columns"]).then_inc(s["small_in"], 16)
            act.dma_start(cst[:, 0:2 * P], A["cst"][:, 0:2 * P]).then_inc(s["const_in"], 16)
            act.dma_start(alog, A["a_log"][0:1, :].partition_broadcast(P)).then_inc(s["small_in"], 16)
            act.dma_start(dtb, A["dt_bias"][0:1, :].partition_broadcast(P)).then_inc(s["small_in"], 16)
            act.wait_ge(s["small_in"], 16 * 3)
            act.wait_ge(s["zeros"], 1)
            act.activation(silc.rearrange("p (k n) -> p k n", n=32)[:, :, 0], ccol, ACT.Silu).then_inc(s["silu_c"], 1)
            act.wait_ge(s["x_in"], 16)
            act.activation(rows[:, :], hT[:, :], ACT.Square).then_inc(s["sq_x"], 1)
            act.wait_ge(s["ssx_e"], 1)
            act.activation(rmsb, rmsb, ACT.Sqrt).then_inc(s["rt_x"], 1)
            act.activation(alog, alog, ACT.Exp).then_inc(s["ach"], 1)
            act.wait_ge(s["ss_x"], 1)
            for q in range(4):
                turn_done("c", q)
                act.activation(rows[:, q * 512:(q + 1) * 512], bank("c", q), ACT.Copy).then_inc(s["a_read"], 1)

            def silu_conv(n):
                dst = (kT, kT, qT, qT, vT, vT)[n][:, (n % 2) * 512:(n % 2) * 512 + 512]
                act.wait_ge(s["conv"], n + 1)
                act.activation(dst, dst, ACT.Silu).then_inc(s["ract"], 1)

            def square_norm(which):
                src = kT if which == 0 else qT
                if which == 1:
                    act.wait_ge(s["ss_ps"], 1)
                act.wait_ge(s["ract"], 2 * which + 2)
                act.activation(squares[:, 0:1024], src, ACT.Square).then_inc(s["sq_k"], 1)

            def root_norm(which):
                r = rnorm[:, which * 1024:(which + 1) * 1024]
                act.wait_ge(s["ss_e"], which + 1)
                act.activation(r, r, ACT.Sqrt).then_inc(s["rtn"], 1)

            silu_conv(0)
            act.wait_ge(s["ba_ps"], 1)
            act.activation(baT, B[7][0:8, 0:S], ACT.Copy).then_inc(s["ba_sb"], 1)
            silu_conv(1)
            square_norm(0)
            act.wait_ge(s["ax"], 1)
            act.activation(beta.rearrange("p (t h) -> p t h", t=NT),
                           B[7][:, 256:272].rearrange("p (t h) -> p t h", t=NT)[:, :, 0:H], ACT.Sigmoid).then_inc(s["ach"], 1)
            act.activation(t8b, t8b, ACT.Exp).then_inc(s["ach"], 1)
            act.wait_ge(s["ach"], 3)
            act.activation(t8b, t8b, ACT.Ln, bias=1.0).then_inc(s["axe"], 1)
            silu_conv(2)
            root_norm(0)
            silu_conv(3)
            square_norm(1)
            act.wait_ge(s["cum_v"], 1)
            act.activation(eg, B[7][:, 0:8], ACT.Exp).then_inc(s["cum_a"], 1)
            act.activation(dec, B[7][:, 16:32], ACT.Exp).then_inc(s["cum_a"], 1)
            act.activation(etail, t8a, ACT.Exp).then_inc(s["cum_a"], 1)
            silu_conv(4)
            root_norm(1)
            silu_conv(5)

            for n in range(2):
                turn_done("z", n)
                act.activation(zT[:, n * 512:(n + 1) * 512], bank("z", n), ACT.Silu).then_inc(s["a_read"], 1)

            def decay_exp(t):
                act.wait_ge(s["dt_v"], t + 1)
                if t == 0:
                    act.wait_ge(s["ss_ps"], 2)
                act.activation(tile(egb, t), B[6][:, :], ACT.Exp).then_inc(s["egb_a"], 1)
                act.activation(tile(DT, t), tile(DT, t), ACT.Exp).then_inc(s["dt_a"], 1)

            for t in range(NT):
                act.wait_ge(s["ktv"], H * (t + 1))
                act.wait_ge(s["cum_a"], 3)
                for h in range(H):
                    c = t * H + h
                    act.activation(head(ktl, t, h), B[2 + t][:, h * HD:(h + 1) * HD], ACT.Copy,
                                   scale=etail[:, c:c + 1]).then_inc(s["ktok"], 1)
            for t in range(NT):
                act.wait_ge(s["tr_ps"], NT + t + 1)
                for h in range(H):
                    c = t * H + h
                    act.activation(head(vb, t, h), B[4 + t][:, h * HD:(h + 1) * HD], ACT.Copy,
                                   scale=beta[:, c:c + 1]).then_inc(s["ktok"], 1)
            decay_exp(0)

            def copy_rotary(n):
                kind = ("mq", "mk")[n // 2]
                turn_done(kind, n % 2)
                dst = (mq, mk)[n // 2][:, (n % 2) * 512:(n % 2) * 512 + 512]
                act.activation(dst, bank(kind, n % 2), ACT.Copy).then_inc(s["a_read"], 1)

            def copy_v(n):
                turn_done("mv", n)
                for t in range(NT):
                    ins = act.activation(mv[:, t * TW + n * BLK:t * TW + (n + 1) * BLK],
                                         bank("mv", n)[:, t * BLK:(t + 1) * BLK], ACT.Copy)
                ins.then_inc(s["a_read"], 1)

            def gate_sig(n):
                turn_done("g", n)
                act.activation(gv[n // 4][:, (n % 4) * 512:(n % 4) * 512 + 512], bank("g", n),
                               ACT.Sigmoid).then_inc(s["a_read"], 1)

            copy_rotary(0)
            decay_exp(1)
            copy_rotary(1)
            copy_rotary(2)
            copy_rotary(3)

            def mod_row(q):
                if q >= 4:
                    turn_done("M", q - 3 if q % 2 == 0 else q - 4)
                turn_done("r", q)
                act.activation(rows[:, (q % 4) * 512:(q % 4) * 512 + 512], bank("r", q), ACT.Copy).then_inc(s["a_read"], 1)

            act.wait_ge(s["col_ps"], 1)
            after = {name: i for i, name in enumerate(plan)}
            for name in sorted(["r0", "r1", "mv0", "r2", "r3", "mv1", "r4", "g0", "r5", "g1", "r6", "r7", "g2"], key=after.get):
                {"r": mod_row, "mv": copy_v, "g": gate_sig}[name[:-1]](int(name[-1]))
            for t in range(NT):
                act.wait_ge(s["uw_ps"], t + 1)
                act.activation(tile(uu, t), B[2 + t][:, :], ACT.Copy).then_inc(s["uw_a"], 1)
                act.activation(tile(wT, t), B[6 + t][:, :], ACT.Copy).then_inc(s["uw_a"], 1)
            gate_sig(3)

            def softmax_exp(h):
                p = prob[:, (h % 2) * 768:(h % 2) * 768 + 384]
                act.wait_ge(s["mx_v"], h + 1)
                act.activation(p[:, 0:128], p[:, 0:128], ACT.Exp, bias=mstat[:, 0:1], scale=HD ** -0.5, accum_out=mstat[:, 2:3]).then_inc(s["p_a"], 1)
                act.activation(p[:, 128:384], p[:, 128:384], ACT.Exp, bias=mstat[:, 1:2], scale=HD ** -0.5, accum_out=mstat[:, 3:4]).then_inc(s["p_a"], 1)

            def softmax_copies(h):
                pt = prob[:, (h % 2) * 768 + 384:(h % 2) * 768 + 768]
                act.wait_ge(s["pt_ps"], h + 1)
                act.activation(pt, bank("t", h)[:, 0:384], ACT.Copy).then_inc(s["pt_a"], 1)
                act.wait_ge(s["ob_ps"], h + 1)
                act.activation(obT[:, h * S:(h + 1) * S], bank("o", h)[:, 0:S], ACT.Copy).then_inc(s["ob_a"], 1)

            def out_copy(n):
                t, r0 = n // 2, CHUNK * (n % 2)
                act.wait_ge(s["o_ps"], n + 1)
                act.activation(tile(otok, t)[r0:r0 + CHUNK, :], B[2 + t][r0:r0 + CHUNK, :], ACT.Copy).then_inc(s["o_a"], 1)

            for n in range(4):
                softmax_exp(n)
                gate_sig(4 + n)
                out_copy(n)
                softmax_copies(n)

            for t in range(NT):
                act.wait_ge(s["o_a"], 2 * t + 2)
                act.activation(tile(qd, t), tile(otok, t), ACT.Square).then_inc(s["ro_a"], 1)
            act.wait_ge(s["ro_v"], 1)
            act.activation(rsc[:, 0:8], ssum[:, 0:8], ACT.Sqrt).then_inc(s["ro_a"], 1)

            for n in range(4):
                act.wait_ge(s["mix_ps"], n + 1)
                for t in range(NT):
                    ins = act.activation(rows[:, t * D + n * BLK:t * D + (n + 1) * BLK],
                                         B[n % 2][:, t * BLK:(t + 1) * BLK], ACT.Copy)
                ins.then_inc(s["mix_a"], 1)
            act.wait_ge(s["mix_a"], 4)
            act.wait_ge(s["ya_v"], KD)
            for t in range(NT):
                act.activation(gv[0][:, t * D:(t + 1) * D], rows[:, t * D:(t + 1) * D], ACT.Square,
                               accum_out=ssum[:, t:t + 1]).then_inc(s["xss"], 1)
            act.wait_ge(s["xsr"], 1)
            act.activation(rsc[:, 0:2], ssum[:, 2:4], ACT.Sqrt).then_inc(s["xss"], 1)
            for t in range(NT):
                act.wait_ge(s["x1"], t + 1)
                act.activation(gv[1][:, t * D:(t + 1) * D], xs[:, t * D:(t + 1) * D], ACT.Square,
                               accum_out=ssum[:, 4 + t:5 + t]).then_inc(s["xss"], 1)
            act.wait_ge(s["xsr"], 2)
            act.activation(rsc[:, 4:6], ssum[:, 6:8], ACT.Sqrt).then_inc(s["xss"], 1)
            for n in range(4):
                act.wait_ge(s["h2t_ps"], n + 1)
                act.activation(hT[:, n * 512:(n + 1) * 512], B[n][:, :], ACT.Copy).then_inc(s["h2t"], 1)
            act.wait_ge(s["lg_v"], 1)
            for t in range(NT):
                act.activation(rt[:, 64 + t * NE:64 + (t + 1) * NE], rt[:, t * NE:(t + 1) * NE], ACT.Exp,
                               bias=mx[:, 8 * t + 1:8 * t + 2]).then_inc(s["ex_a"], 1)
            for n in range(2):
                act.wait_ge(s["bj_ps"], n + 1)
                act.activation(bJ[:, n * 8 * JC:(n + 1) * 8 * JC], B[n][:, 0:8 * JC], ACT.Copy).then_inc(s["bj_a"], 1)

            act.wait_ge(s["gat"], 1)
            act.activation(xg, B[3][:, :], ACT.Copy).then_inc(s["xg_a"], 1)
            act.wait_ge(s["tab_v"], 1)
            J = act.value_load(table[0:1, NE:NE + 1], min_val=NE, max_val=MAXJ)
            act.sem_inc(s["gu_a"], 1)
            act.sem_inc(s["c_a"], 1)
            act.sem_inc(s["y_a"], 1)
            act.sem_inc(s["sg_rdy"], 2)
            with act.Fori(0, J) as j:
                act.wait_ge(used[GU_UNITS - 1], j + 1)
                act.activation(gus[:, 0:512], B[0][:, :], ACT.Copy).then_inc(s["gu_a"], 1)
                act.wait_ge(s["gat"], j + 2)
                act.activation(xg, B[3][:, :], ACT.Copy).then_inc(s["xg_a"], 1)
                for q in range(2):
                    act.wait_ge(s["g_rdy"], 2 * j + q + 1)
                    act.activation(ts[:, q * 256:(q + 1) * 256], tg[:, q * 256:(q + 1) * 256], ACT.Sigmoid, scale=ALPHA).then_inc(s["sg_rdy"], 1)
                act.wait_ge(s["ctr"], j + 2)
                act.activation(cab, B[3][:, :], ACT.Copy).then_inc(s["c_a"], 1)
                act.wait_ge(used[UPE - 1], j + 1)
                act.activation(ysb, B[4][:, :], ACT.Copy).then_inc(s["y_a"], 1)

            act.wait_ge(s["accd"], 4 * J + 8)
            for t in range(NT):
                act.activation(ffn[:, 0:D] if t == 0 else ffn[:, D:2 * D], acc[:, t * D:(t + 1) * D], ACT.Square,
                               accum_out=ssum[:, 8 + t:9 + t]).then_inc(s["fss"], 1)
            act.wait_ge(s["fsr"], 1)
            act.activation(rsc[:, 8:10], ssum[:, 10:12], ACT.Sqrt).then_inc(s["fss"], 1)

        @block.vector
        def _(dve):
            v = nc.vector
            done = [0]

            def chain(ins):
                done[0] += 1
                ins.then_inc(s["vch"], 1)

            def settle():
                dve.wait_ge(s["vch"], done[0])

            def heads4(ap):
                return ap.rearrange("p (h d) -> p h d", h=H)

            def over_heads(ap):
                return ap.rearrange("p (a d) -> p a d", a=1).broadcast_to([P, H, ap.shape[1]])

            def root_arg(dst, src, scale, eps):
                return v.tensor_scalar(dst, src, scale, eps, ALU.mult, ALU.add)

            dve.wait_ge(s["ss_x"], 1)
            root_arg(rmsb, B[7][:, 0:S], 1.0 / D, EPS).then_inc(s["ssx_e"], 1)
            dve.wait_ge(s["rt_x"], 1)
            chain(v.reciprocal(rmsb, rmsb))
            settle()
            chain(v.tensor_tensor(hTk, hTk, rmsb.rearrange("p (a t) -> p a t", a=1).broadcast_to([P, KD, S]), ALU.mult))
            dve.wait_ge(s["col_ps"], 1)
            dve.wait_ge(s["small_in"], 16 * 3)
            chain(v.tensor_tensor(shG, B[6][:, 0:16], bcol, ALU.add))
            settle()
            chain(v.scalar_tensor_tensor(out=shG[:, 8:16], in0=shG[:, 8:16], scalar=1.0, in1=gcol, op0=ALU.add, op1=ALU.mult))
            settle()
            for k in range(KD):
                v.tensor_scalar(hTk[:, k, :], hTk[:, k, :], shG[:, 8 + k:9 + k], shG[:, k:k + 1], ALU.mult, ALU.add).then_inc(s["h_ok"], 1)

            def conv(n):
                base = (kT, kT, qT, qT, vT, vT)[n]
                first = (4, 6, 0, 2, 8, 10)[n]
                name = ("k0", "k1", "q0", "q1", "v0", "v1")[n]
                dve.wait_ge(s["proj"], turns(name))
                for j in range(TAPS):
                    if j:
                        settle()
                    for c in range(2):
                        x = B[USE[name] % 2][:, c * S:(c + 1) * S]
                        y = base[:, (n % 2) * 512 + c * S:(n % 2) * 512 + (c + 1) * S]
                        w = convw[:, (first + c) * TAPS + TAPS - 1 - j:(first + c) * TAPS + TAPS - j]
                        if j == 0:
                            ins = v.tensor_scalar(y, x, w, None, ALU.mult)
                        else:
                            ins = v.scalar_tensor_tensor(out=y[:, j:], in0=x[:, 0:S - j], scalar=w, in1=y[:, j:], op0=ALU.mult, op1=ALU.add)
                        if j < TAPS - 1 or c == 0:
                            chain(ins)
                        else:
                            ins.then_inc(s["conv"], 1)

            def norm_arg(which):
                dve.wait_ge(s["ss_ps"], which + 1)
                for i in range(2):
                    ins = v.tensor_scalar(rnorm[:, which * 1024 + i * 512:which * 1024 + (i + 1) * 512],
                                          B[2 + 2 * which + i][:, :], 1e-6, None, ALU.add)
                    if i == 0:
                        chain(ins)
                ins.then_inc(s["ss_e"], 1)

            def normalise(which):
                r = rnorm[:, which * 1024:(which + 1) * 1024]
                dve.wait_ge(s["rtn"], which + 1)
                chain(v.reciprocal(r, r))
                settle()
                if which == 0:
                    v.tensor_tensor(kT, kT, r, ALU.mult).then_inc(s["qk_n"], 1)
                else:
                    v.scalar_tensor_tensor(out=qT, in0=qT, scalar=HD ** -0.5, in1=r, op0=ALU.mult, op1=ALU.mult).then_inc(s["qk_n"], 1)

            conv(0)
            conv(1)
            dve.wait_ge(s["bat_ps"], 1)
            chain(v.tensor_tensor(t8a.rearrange("p (t h) -> p t h", t=NT), B[7][:, 256:272].rearrange("p (t h) -> p t h", t=NT)[:, :, H:2 * H],
                                  dtb.rearrange("p (a h) -> p a h", a=1).broadcast_to([P, NT, H]), ALU.add))
            settle()
            chain(v.tensor_scalar(gc, t8a, -1.0, None, ALU.mult))
            settle()
            v.tensor_tensor(t8b, t8a, gc, ALU.min).then_inc(s["ax"], 1)
            conv(2)
            norm_arg(0)
            dve.wait_ge(s["axe"], 1)
            chain(v.scalar_tensor_tensor(out=g, in0=t8a, scalar=0.0, in1=t8b, op0=ALU.max, op1=ALU.add))
            settle()
            v.scalar_tensor_tensor(out=g.rearrange("p (t h) -> p t h", t=NT), in0=g.rearrange("p (t h) -> p t h", t=NT), scalar=-1.0,
                                   in1=alog.rearrange("p (a h) -> p a h", a=1).broadcast_to([P, NT, H]),
                                   op0=ALU.mult, op1=ALU.mult).then_inc(s["g_ok"], 1)
            conv(3)
            normalise(0)
            dve.wait_ge(s["cum_ps"], 1)
            chain(v.tensor_copy(gc, B[7][:, 0:8]))
            settle()
            v.tensor_tensor(t8a, B[7][:, 8:16], gc, ALU.subtract).then_inc(s["cum_v"], 1)
            dve.wait_ge(s["cum_a"], 1)
            v.tensor_tensor(bk, beta, eg, ALU.mult).then_inc(s["cum_v"], 1)
            conv(4)
            norm_arg(1)
            conv(5)
            normalise(1)
            dve.wait_ge(s["cum_v"], 2)
            for t in range(NT):
                dve.wait_ge(s["tr_ps"], t + 1)
                for h in range(H):
                    c = t * H + h
                    v.tensor_scalar(head(kbg, t, h), B[2 + t][:, h * HD:(h + 1) * HD], bk[:, c:c + 1], None, ALU.mult).then_inc(s["ktv"], 1)

            def decay_arg(t):
                dve.wait_ge(s["gcb_ps"], t + 1)
                for h in range(H):
                    ins = v.scalar_tensor_tensor(out=head(DT, t, h), in0=B[6][:, h * HD:(h + 1) * HD], scalar=gc[:, t * H + h:t * H + h + 1],
                                                 in1=const("decaymask"), op0=ALU.subtract, op1=ALU.add)
                    if h < H - 1:
                        chain(ins)
                ins.then_inc(s["dt_v"], 1)

            def lower(t):
                dve.wait_ge(s["dt_a"], t + 1)
                chain(v.tensor_tensor(heads4(tile(LT, t)), heads4(tile(DT, t)), over_heads(const("strict")), ALU.mult))
                dve.wait_ge(s["kk_ps"], t + 1)
                dve.wait_ge(s["bb_ps"], t + 1)
                settle()
                chain(v.tensor_tensor(tile(LT, t), tile(LT, t), B[7][:, :], ALU.mult))
                settle()
                v.tensor_tensor(tile(LT, t), tile(LT, t), B[2 + t][:, :], ALU.mult).then_inc(s["lt_v"], 1)
                v.tensor_tensor(tile(QK, t), tile(DT, t), B[4 + t][:, :], ALU.mult).then_inc(s["qk_v"], 1)
                dve.wait_ge(s["egb_a"], t + 1)
                chain(v.tensor_tensor(heads4(tile(qd, t)), heads4(qT)[:, :, t * P:(t + 1) * P], heads4(tile(egb, t)), ALU.mult))

            decay_arg(0)
            lower(0)
            decay_arg(1)
            lower(1)

            def level(l):
                a = const("level")[:, l * P:(l + 1) * P]
                return over_heads(a)

            for t in range(NT):
                dve.wait_ge(s["l_ps"], t + 1)
                settle()
                chain(v.tensor_tensor(heads4(tile(T, t)), heads4(B[2 + t][:, :]), level(0), ALU.mult))
                chain(v.tensor_tensor(heads4(tile(TT, t)), heads4(tile(LT, t)), over_heads(const("level1t")), ALU.mult))
                settle()
                v.tensor_tensor(heads4(tile(T, t)), heads4(tile(T, t)), over_heads(ident), ALU.add).then_inc(s["t1_v"], 1)
                v.tensor_tensor(heads4(tile(TT, t)), heads4(tile(TT, t)), over_heads(ident), ALU.add).then_inc(s["t1_v"], 1)
            dve.wait_ge(s["a_read"], read_count(USE["mk1"]))
            swap = [(i + HALF_ROPE) % (2 * HALF_ROPE) for i in range(2 * HALF_ROPE)]
            for i, m in enumerate((mq, mk)):
                R = 2 * HALF_ROPE
                tmp = prob[0:R, 0:H * S]
                rows32 = m[0:R, :].rearrange("p (h t) -> p h t", h=H)
                c4 = const("cos")[0:R, :].rearrange("p (a t) -> p a t", a=1).broadcast_to([R, H, S])
                s4 = const("sin")[0:R, :].rearrange("p (a t) -> p a t", a=1).broadcast_to([R, H, S])
                settle()
                chain(v.stream_shuffle(tmp, m[0:R, :], swap))
                settle()
                chain(v.tensor_tensor(tmp.rearrange("p (h t) -> p h t", h=H), tmp.rearrange("p (h t) -> p h t", h=H), s4, ALU.mult))
                chain(v.tensor_tensor(rows32, rows32, c4, ALU.mult))
                settle()
                v.tensor_tensor(m[0:R, :], m[0:R, :], tmp, ALU.add).then_inc(s["rope_v"], 1)
                dve.wait_ge(s["rope_v"], i + 1)

            def mod_sum(i):
                dve.wait_ge(s["proj"], turns(f"M{i}"))
                dve.wait_ge(s["modb_in"], 64)
                row = (i // 2 + 1) % 4 * D + i % 2 * 512
                v.tensor_tensor(mod[:, row:row + 512], mod[:, row:row + 512], bank("M", i), ALU.add).then_inc(s["mod_a"], 1)

            dve.wait_ge(s["const2_in"], 16)
            for l in range(1, 6):
                for t in range(NT):
                    i = (l - 1) * NT + t
                    dve.wait_ge(s["a_ps"], i + 1)
                    v.tensor_tensor(heads4(tile(M, t)), heads4(B[2 + t][:, :]), level(l), ALU.mult).then_inc(s["m_v"], 1)
                for i in {2: (0, 1), 3: (2, 3), 4: (4, 5)}.get(l, ()):
                    mod_sum(i)
                for t in range(NT):
                    i = (l - 1) * NT + t
                    dve.wait_ge(s["x_ps"], i + 1)
                    if l < 5:
                        chain(v.tensor_tensor(tile(T, t), tile(T, t), B[4 + t][:, :], ALU.add))
                    v.tensor_tensor(tile(TT, t), tile(TT, t), B[6 + t][:, :], ALU.add).then_inc(s["tt_v"], 1)
            settle()
            chain(v.memset(vn, 0.0))
            mod_sum(6)
            mod_sum(7)

            for n in range(4):
                t, hf = n // 2, n % 2
                r = slice(CHUNK * hf, CHUNK * hf + CHUNK)
                vnb = vn[:, hf * TW:(hf + 1) * TW]
                dve.wait_ge(s["uw_a"], 2 * t + 1)
                settle()
                if n == 0:
                    v.tensor_copy(vnb[r, :], tile(uu, t)[r, :]).then_inc(s["vn_v"], 1)
                else:
                    dve.wait_ge(s["ws_ps"], n)
                    v.tensor_tensor(vnb[r, :], tile(uu, t)[r, :], B[6][r, :], ALU.subtract).then_inc(s["vn_v"], 1)
                p = prob[:, (n % 2) * 768:(n % 2) * 768 + 384]
                dve.wait_ge(s["sc_ps"], n + 1)
                if n:
                    dve.wait_ge(s["pn_v"], 2 * n)
                if n >= 2:
                    dve.wait_ge(s["pt_ps"], n - 1)
                chain(v.tensor_tensor(p[:, 0:128], bank("s", n)[:, 0:128], const("causal"), ALU.add))
                chain(v.tensor_copy(p[:, 128:256], bank("s", n)[:, 128:256]))
                chain(v.tensor_tensor(p[:, 256:384], bank("s", n)[:, 256:384], const("causal"), ALU.add))
                settle()
                chain(v.tensor_reduce(mstat[:, 0:1], p[:, 0:128], AX.X, ALU.max))
                chain(v.tensor_reduce(mstat[:, 1:2], p[:, 128:384], AX.X, ALU.max))
                settle()
                v.tensor_scalar(mstat[:, 0:2], mstat[:, 0:2], -HD ** -0.5, None, ALU.mult).then_inc(s["mx_v"], 1)
                if n < 3:
                    dve.wait_ge(s["st_ps"], n + 1)
                    if n == 0:
                        v.tensor_copy(state, B[7][:, :]).then_inc(s["s_v"], 1)
                    else:
                        for h in range(H):
                            c = hf * 8 + t * H + h
                            st = state[:, h * HD:(h + 1) * HD]
                            ins = v.scalar_tensor_tensor(out=st, in0=st, scalar=dec[:, c:c + 1], in1=B[7][:, h * HD:(h + 1) * HD],
                                                         op0=ALU.mult, op1=ALU.add)
                            if h < H - 1:
                                chain(ins)
                        ins.then_inc(s["s_v"], 1)
                    dve.wait_ge(s["s_v"], n + 1)
                dve.wait_ge(s["p_a"], 2 * n + 2)
                chain(v.reciprocal(mstat[:, 4:6], mstat[:, 2:4]))
                settle()
                v.tensor_scalar(p[:, 0:128], p[:, 0:128], mstat[:, 4:5], None, ALU.mult).then_inc(s["pn_v"], 1)
                v.tensor_scalar(p[:, 128:384], p[:, 128:384], mstat[:, 5:6], None, ALU.mult).then_inc(s["pn_v"], 1)

            for t in range(NT):
                dve.wait_ge(s["ro_a"], t + 1)
                chain(v.tensor_reduce(ssum[:, t * H:(t + 1) * H], heads4(tile(qd, t)), AX.X, ALU.add))
            settle()
            root_arg(ssum[:, 0:8], ssum[:, 0:8], 1.0 / HD, EPS).then_inc(s["ro_v"], 1)
            dve.wait_ge(s["ro_a"], 3)
            chain(v.reciprocal(rsc[:, 0:8], rsc[:, 0:8]))
            settle()
            for t in range(NT):
                for h in range(H):
                    v.tensor_scalar(head(otok, t, h), head(otok, t, h), rsc[:, t * H + h:t * H + h + 1], None, ALU.mult).then_inc(s["ro_v"], 1)
            for t in range(NT):
                dve.wait_ge(s["ot_ps"], t + 1)
                v.scalar_tensor_tensor(out=heads4(oaT)[:, :, t * P:(t + 1) * P], in0=heads4(B[4 + t][:, :]), scalar=gdn,
                                       in1=heads4(zT)[:, :, t * P:(t + 1) * P], op0=ALU.mult, op1=ALU.mult).then_inc(s["oa_v"], 1)
            dve.wait_ge(s["rows_in"], 48)
            dve.wait_ge(s["mod_a"], 8)
            v.tensor_tensor(GM, GM, gpm, ALU.mult).then_inc(s["mod_v"], 1)
            v.scalar_tensor_tensor(out=G2, in0=G2, scalar=1.0, in1=gpf, op0=ALU.add, op1=ALU.mult).then_inc(s["mod_v"], 1)
            v.tensor_tensor(GF, GF, gqf, ALU.mult).then_inc(s["mod_v"], 2)
            for j in range(KD):
                b = B[2 + j % 2]
                ga, gb = (gv[i][:, j * S:(j + 1) * S] for i in range(2))
                dve.wait_ge(s["ya_ps"], j + 1)
                if j == 0:
                    dve.wait_ge(s["a_read"], read_count(USE["g7"]))
                chain(v.tensor_tensor(ga, ga, b[:, 0:S], ALU.mult))
                chain(v.tensor_tensor(gb, gb, b[:, S:2 * S], ALU.mult))
                settle()
                v.tensor_tensor(hTk[:, j, :], ga, gb, ALU.add).then_inc(s["ya_v"], 1)

            dve.wait_ge(s["xss"], 2)
            root_arg(ssum[:, 2:4], ssum[:, 0:2], 1.0 / D, EPS).then_inc(s["xsr"], 1)
            dve.wait_ge(s["xss"], 3)
            chain(v.reciprocal(rsc[:, 2:4], rsc[:, 0:2]))
            settle()
            dve.wait_ge(s["mod_v"], 4)
            dve.wait_ge(s["x2_in"], 64)
            for t in range(NT):
                a = slice(t * D, (t + 1) * D)
                chain(v.scalar_tensor_tensor(out=gv[0][:, a], in0=rows[:, a], scalar=rsc[:, 2 + t:3 + t], in1=GM, op0=ALU.mult, op1=ALU.mult))
                settle()
                v.tensor_tensor(xs[:, a], xs[:, a], gv[0][:, a], ALU.add).then_inc(s["x1"], 1)
            dve.wait_ge(s["xss"], 5)
            root_arg(ssum[:, 6:8], ssum[:, 4:6], 1.0 / D, EPS).then_inc(s["xsr"], 1)
            dve.wait_ge(s["xss"], 6)
            chain(v.reciprocal(rsc[:, 6:8], rsc[:, 4:6]))
            settle()
            dve.wait_ge(s["x1"], 2)
            for t in range(NT):
                a = slice(t * D, (t + 1) * D)
                chain(v.scalar_tensor_tensor(out=gv[0][:, a], in0=xs[:, a], scalar=rsc[:, 6 + t:7 + t], in1=G2, op0=ALU.mult, op1=ALU.mult))
                settle()
                v.tensor_tensor(gv[0][:, a], gv[0][:, a], SH2, ALU.add).then_inc(s["h2"], 1)
            dve.wait_ge(s["h2"], 2)
            for t in range(NT):
                a = slice(t * D, (t + 1) * D)
                chain(v.tensor_copy(hb[:, 0, t, :], gv[0][:, a]))
            settle()
            for t in range(NT):
                a = slice(t * D, (t + 1) * D)
                chain(v.tensor_tensor(gv[1][:, a], gv[0][:, a], hb[:, 0, t, :], ALU.subtract))
            settle()
            for t in range(NT):
                a = slice(t * D, (t + 1) * D)
                chain(v.tensor_copy(hb[:, 1, t, :], gv[1][:, a]))
            settle()
            for t in range(NT):
                a = slice(t * D, (t + 1) * D)
                v.tensor_tensor(hb[:, 2, t, :], gv[1][:, a], hb[:, 1, t, :], ALU.subtract).then_inc(s["hb1"], 1)

            rt_ = rt
            lgt, ex, selt, eqt, tmp, posm, wts = (rt_[:, i * 64:(i + 1) * 64] for i in range(7))
            cum, misc = rt_[:, 448:512], rt_[:, 512:640]
            dve.wait_ge(s["lg_ps"], 1)
            for t in range(NT):
                chain(v.tensor_tensor(lgt[:, t * NE:(t + 1) * NE], B[4][:, t * NE:(t + 1) * NE], rbr, ALU.add))
            settle()
            for t in range(NT):
                chain(v.max(mx[:, t * 8:(t + 1) * 8], lgt[:, t * NE:(t + 1) * NE]))
            settle()
            for t in range(NT):
                e = slice(t * NE, (t + 1) * NE)
                chain(v.tensor_scalar(selt[:, e], lgt[:, e], mx[:, 8 * t + TOPK - 1:8 * t + TOPK], None, ALU.is_gt))
                chain(v.tensor_scalar(eqt[:, e], lgt[:, e], mx[:, 8 * t + TOPK - 1:8 * t + TOPK], None, ALU.is_equal))
                ins = v.tensor_scalar(mx[:, 8 * t + 1:8 * t + 2], mx[:, 8 * t:8 * t + 1], -1.0, None, ALU.mult)
                if t == 0:
                    chain(ins)
                else:
                    ins.then_inc(s["lg_v"], 1)
            settle()
            for t in range(NT):
                e = slice(t * NE, (t + 1) * NE)
                chain(v.tensor_reduce(misc[:, t:t + 1], selt[:, e], AX.X, ALU.add))
                chain(v.tensor_tensor_scan(cum[:, e], ones[:, 0:NE], eqt[:, e], 0.0, ALU.mult, ALU.add))
            settle()
            chain(v.tensor_scalar(misc[:, 0:2], misc[:, 0:2], -1.0, float(TOPK), ALU.mult, ALU.add))
            settle()
            for t in range(NT):
                e = slice(t * NE, (t + 1) * NE)
                chain(v.scalar_tensor_tensor(out=tmp[:, e], in0=cum[:, e], scalar=misc[:, t:t + 1], in1=eqt[:, e], op0=ALU.is_le, op1=ALU.mult))
            settle()
            v.tensor_tensor(selt, selt, tmp, ALU.add).then_inc(s["sel_v"], 1)
            dve.wait_ge(s["sel_v"], 1)
            dve.wait_ge(s["ex_a"], 2)
            chain(v.tensor_tensor(ex, ex, selt, ALU.mult))
            settle()
            chain(v.tensor_reduce(misc[:, 2:4], ex.rearrange("p (t e) -> p t e", t=NT), AX.X, ALU.add))
            settle()
            chain(v.reciprocal(misc[:, 2:4], misc[:, 2:4]))
            settle()
            for t in range(NT):
                e = slice(t * NE, (t + 1) * NE)
                chain(v.tensor_scalar(wts[:, e], ex[:, e], misc[:, 2 + t:3 + t], None, ALU.mult))
            dve.wait_ge(s["pos_ps"], 1)
            chain(v.scalar_tensor_tensor(out=posm, in0=B[5][:, 0:2 * NE], scalar=1.0, in1=selt, op0=ALU.add, op1=ALU.mult))
            nrow, jend, ncol = misc[:, 32:64], misc[:, 64:96], misc[0:NE, 8:9]
            chain(v.tensor_scalar(nrow, B[5][:, 64:64 + NE], float(SLOTS), 1.0, ALU.is_gt, ALU.add))
            chain(v.tensor_scalar(ncol, B[5][0:NE, 96:97], float(SLOTS), 1.0, ALU.is_gt, ALU.add))
            settle()
            chain(v.tensor_scalar(posm, posm, -1.0, None, ALU.add))
            for m in range(2, S // SLOTS):
                chain(v.scalar_tensor_tensor(out=nrow, in0=B[5][:, 64:64 + NE], scalar=float(SLOTS * m), in1=nrow, op0=ALU.is_gt, op1=ALU.add))
                chain(v.scalar_tensor_tensor(out=ncol, in0=B[5][0:NE, 96:97], scalar=float(SLOTS * m), in1=ncol, op0=ALU.is_gt, op1=ALU.add))
                settle()
            v.tensor_copy(misc[0:1, 16:17], ones[0:1, 0:1]).then_inc(s["pos_v"], 1)
            chain(v.tensor_tensor_scan(jend, ones[:, 0:NE], nrow, 0.0, ALU.mult, ALU.add))
            settle()
            chain(v.tensor_tensor(nrow, jend, nrow, ALU.subtract))
            settle()
            chain(v.tensor_copy(table[0:1, 0:NE], nrow[0:1, :]))
            v.tensor_copy(table[0:1, NE:NE + 1], jend[0:1, NE - 1:NE]).then_inc(s["tab_v"], 1)
            jst, jen, jst64 = misc[0:NE, 9:10], misc[0:NE, 10:11], misc[0:NE, 11:12]
            pqw = ffn[0:NE, 0:512]
            oh, oh1 = ffn[0:NE, 512:512 + JC], ffn[0:NE, 576:576 + JC]
            dve.wait_ge(s["jt_ps"], 1)
            settle()
            chain(v.tensor_copy(misc[0:NE, 9:11], B[7][0:NE, 0:2]))
            settle()
            chain(v.tensor_scalar(jst64, jst, float(SLOTS), None, ALU.mult))
            chain(v.tensor_scalar(oh1, const("iota")[0:NE, :], jst, None, ALU.is_ge))
            settle()
            dve.wait_ge(s["hb1"], 2)
            chain(v.scalar_tensor_tensor(out=oh, in0=const("iota")[0:NE, :], scalar=jen, in1=oh1, op0=ALU.is_lt, op1=ALU.mult))
            chain(v.tensor_scalar(pqw[:, 0:S], B[6][0:NE, 0:S], jst64, None, ALU.add))
            v.tensor_copy(pqw[:, S:2 * S], B[6][0:NE, S:2 * S]).then_inc(s["oh_v"], 1)
            dve.wait_ge(s["job_ps"], 1)
            for t in range(NT):
                chain(v.scalar_tensor_tensor(out=posj[:, t * JC:(t + 1) * JC], in0=const("iota"), scalar=-float(SLOTS),
                                             in1=B[7][:, 128 + t * JC:128 + (t + 1) * JC], op0=ALU.mult, op1=ALU.add))
            chain(v.tensor_copy(posj[:, 2 * JC:4 * JC], B[7][:, 128 + 2 * JC:128 + 4 * JC]))
            dve.wait_ge(s["y0_ps"], 1)
            dve.wait_ge(s["h2t_ps"], 4)
            for i in range(4):
                v.tensor_copy(acc[:, i * 512:(i + 1) * 512], B[2 + i][:, :]).then_inc(s["y0_v"], 1)
            chain(v.memset(swt, 0.0))
            chain(v.memset(ysb, 0.0))
            v.memset(cab, 0.0).then_inc(s["cnt_v"], 1)
            slot_row = const("slot")
            settle()

            def gather_select(j):
                for t in range(NT):
                    ins = v.tensor_scalar(sgat[:, t * SLOTS:(t + 1) * SLOTS], slot_row, posj[:, bass.ds(j + t * JC, 1)], None, ALU.is_equal)
                    if t == 0:
                        chain(ins)
                ins.then_inc(s["selg"], 1)

            gather_select(0)
            J = dve.value_load(table[0:1, NE:NE + 1], min_val=NE, max_val=MAXJ)
            before_loop = done[0]
            PER = 12
            dve.sem_inc(s["gu_v"], 1)
            dve.sem_inc(s["act_v"], 2)
            dve.sem_inc(s["accd"], 4)
            with dve.Fori(0, J) as j:
                done[0] = 0

                def settle_j():
                    dve.wait_ge(s["vch"], j * PER + (before_loop + done[0]))

                def chain_j(ins):
                    done[0] += 1
                    ins.then_inc(s["vch"], 1)

                dve.wait_ge(s["gat"], j + 1)
                for t in range(NT):
                    ins = v.tensor_scalar(sgat[:, t * SLOTS:(t + 1) * SLOTS], slot_row, posj[:, bass.ds(j + (t * JC + 1), 1)], None, ALU.is_equal)
                    if t == 0:
                        chain_j(ins)
                ins.then_inc(s["selg"], 1)
                dve.wait_ge(s["ctr"], j + 1)
                for t in range(NT):
                    ins = v.tensor_scalar(swt[:, t * 192 + SLOTS:t * 192 + 2 * SLOTS], slot_row, posj[:, bass.ds(j + t * JC, 1)],
                                          posj[:, bass.ds(j + (2 + t) * JC, 1)], ALU.is_equal, ALU.mult)
                    if t == 0:
                        chain_j(ins)
                ins.then_inc(s["selw"], 1)
                dve.wait_ge(used[GU_UNITS - 1], j + 1)
                v.tensor_copy(gus[:, 512:1024], B[1][:, :]).then_inc(s["gu_v"], 1)
                bj3 = bJ.rearrange("p (c j) -> p c j", j=JC)
                for q in range(2):
                    bt = B[(2, 5)[q]][:, :].rearrange("p (c x) -> p c x", c=4)
                    gq, uq, sq = (x[:, q * 256:(q + 1) * 256] for x in (tg, tu, ts))
                    g3, u3 = (x.rearrange("p (c x) -> p c x", c=4) for x in (gq, uq))
                    dve.wait_ge(s["trn"], 2 * j + q + 1)
                    if q == 0:
                        dve.wait_ge(s["sg_rdy"], 2 * j + 2)
                    chain_j(v.tensor_tensor(g3, bt[:, :, 0:64], bj3[:, 4 * q:4 * q + 4, bass.ds(j, 1)].broadcast_to([P, 4, 64]), ALU.add))
                    chain_j(v.tensor_tensor(u3, bt[:, :, 64:128], bj3[:, 8 + 4 * q:12 + 4 * q, bass.ds(j, 1)].broadcast_to([P, 4, 64]), ALU.add))
                    settle_j()
                    v.tensor_scalar(gq, gq, LIMIT, None, ALU.min).then_inc(s["g_rdy"], 1)
                    chain_j(v.tensor_scalar(uq, uq, LIMIT, -LIMIT, ALU.min, ALU.max))
                    settle_j()
                    dve.wait_ge(s["g_rdy"], 2 * j + q + 1)
                    chain_j(v.scalar_tensor_tensor(out=uq, in0=uq, scalar=1.0, in1=gq, op0=ALU.add, op1=ALU.mult))
                    settle_j()
                    dve.wait_ge(s["sg_rdy"], 2 * j + q + 3)
                    v.tensor_tensor(actT[:, q * 256:(q + 1) * 256], uq, sq, ALU.mult).then_inc(s["act_v"], 1)
                    for i in (2 * q, 2 * q + 1):
                        dve.wait_ge(s["sc"], 4 * j + i + 1)
                        dve.wait_ge(s["accd"], 4 * j + i + 4)
                        a = acc[:, i * 512:(i + 1) * 512]
                        v.tensor_tensor(a, a, B[ROW_BANK[i]][:, :], ALU.add).then_inc(s["accd"], 1)
                for _ in range(PER - done[0]):
                    chain_j(v.engine_nop())
            for i in range(4):
                dve.wait_ge(s["sc"], 4 * J + (i + 1))
                a = acc[:, i * 512:(i + 1) * 512]
                v.tensor_tensor(a, a, B[ROW_BANK[i]][:, :], ALU.add).then_inc(s["accd"], 1)
            dve.wait_ge(s["fss"], 2)
            root_arg(ssum[:, 10:12], ssum[:, 8:10], 1.0 / D, EPS).then_inc(s["fsr"], 1)
            dve.wait_ge(s["fss"], 3)
            v.reciprocal(rsc[:, 10:12], rsc[:, 8:10]).then_inc(s["fsr"], 1)
            dve.wait_ge(s["fsr"], 2)
            for t in range(NT):
                a = slice(t * D, (t + 1) * D)
                v.scalar_tensor_tensor(out=gv[1][:, a], in0=acc[:, a], scalar=rsc[:, 10 + t:11 + t], in1=GF, op0=ALU.mult, op1=ALU.mult).then_inc(s["fsr"], 1)
                dve.wait_ge(s["fsr"], 3 + t)
                v.tensor_tensor(xs[:, a], xs[:, a], gv[1][:, a], ALU.add).then_inc(s["fo"], 1)

        @block.tensor
        def _(pe):
            def sum8(out_ap, lhs, rhs):
                for k in range(KD):
                    ins = pe.matmul(out_ap, lhs(k), rhs(k), start=(k == 0), stop=(k == KD - 1))
                return ins

            def free_bank(use):
                if use >= 2:
                    pe.wait_ge(s[reader(plan[use - 2])], read_count(use - 2))

            def unit(i, k=KD):
                pe.wait_ge(landed[i % MIX_RING], 16 * (i // MIX_RING + 1))
                return slot(i % MIX_RING).rearrange("p (k n) -> p k n", k=k)

            pe.wait_ge(s["const_in"], 16)
            pe.wait_ge(s["sq_x"], 1)
            sum8(B[7][:, 0:S], lambda k: ones, lambda k: rows[:, k * S:(k + 1) * S]).then_inc(s["ss_x"], 1)
            sil3 = silc.rearrange("p (k n) -> p k n", n=32)

            def finish_turn(ins, name):
                ins.then_inc(s["proj"], 1)
                pe.wait_ge(s["proj"], turns(name))
                pe.sem_inc(s["unit_used"], 1)

            def ada_pair(name):
                use = USE[name]
                free_bank(use)
                for n in range(2):
                    w = unit(UNIT_OF[name] + n)
                    for k in range(KD):
                        q = k % 4
                        ins = pe.matmul(B[use % 2][32 * q:32 * q + 32, n * BLK:(n + 1) * BLK], sil3[:, k, :], w[:, k, :],
                                        start=(k < 4), stop=(k >= 4), tile_position=(0, 32 * q))
                    if n == 0:
                        ins.then_inc(s["unit_used"], 1)
                finish_turn(ins, name)

            def shift_scale_columns(q):
                pe.wait_ge(s["a_read"], q + 1)
                for j in range(4 * q, 4 * q + 4):
                    ins = pe.matmul(B[6][:, j:j + 1], rows[:, j * P:(j + 1) * P], ones[:, 0:1], start=True, stop=True)
                if q == 3:
                    ins.then_inc(s["col_ps"], 1)

            pe.wait_ge(s["silu_c"], 1)
            for q in range(4):
                ada_pair(f"c{q}")
                if q:
                    shift_scale_columns(q - 1)
            shift_scale_columns(3)
            pe.wait_ge(s["wba_in"], 16)
            pe.wait_ge(s["h_ok"], 8)
            w8 = wba[:, :].rearrange("p (k n) -> p k n", k=KD)
            sum8(B[7][0:8, 0:S], lambda k: w8[:, k, :], lambda k: hTk[:, k, :]).then_inc(s["ba_ps"], 1)

            def project(name):
                use = USE[name]
                free_bank(use)
                w = unit(UNIT_OF[name])
                for c in range(2):
                    ins = sum8(B[use % 2][:, c * S:(c + 1) * S], lambda k: w[:, k, c * P:(c + 1) * P], lambda k: hTk[:, k, :])
                finish_turn(ins, name)

            def project_v(name):
                use = USE[name]
                free_bank(use)
                w = unit(UNIT_OF[name])
                for t in range(NT):
                    ins = sum8(B[use % 2][:, t * BLK:(t + 1) * BLK], lambda k: hTk[:, k, t * P:(t + 1) * P], lambda k: w[:, k, :])
                finish_turn(ins, name)

            def mod_half(i):
                use = USE[f"M{i}"]
                free_bank(use)
                r = i // 2 * 2
                pe.wait_ge(s["a_read"], read_count(USE[f"r{r + i % 2}"]))
                a = (i % 4) * 512
                pe.matmul(B[use % 2][:, :], ones, rows[:, a:a + 512], start=True, stop=True).then_inc(s["proj"], 1)

            def norm_sums(which):
                pe.wait_ge(s["sq_k"], which + 1)
                for h in range(H):
                    ins = pe.matmul(B[2 + 2 * which + h // 2][:, (h % 2) * S:(h % 2) * S + S], ones, squares[:, h * S:(h + 1) * S],
                                    start=True, stop=True)
                ins.then_inc(s["ss_ps"], 1)

            project("k0")
            pe.wait_ge(s["ba_sb"], 1)
            for t in range(NT):
                ins = pe.matmul(B[7][:, 256 + 8 * t:264 + 8 * t], baT[:, t * P:(t + 1) * P], ident[0:8, 0:8], start=True, stop=True)
            ins.then_inc(s["bat_ps"], 1)
            project("k1")
            project("q0")
            norm_sums(0)
            pe.wait_ge(s["const2_in"], 16)
            pe.wait_ge(s["g_ok"], 1)
            for i, n in enumerate(("tri", "blockones", "firsthalf", "secondhalf")):
                ins = pe.matmul(B[7][:, 8 * i:8 * i + 8], const(n), g, start=True, stop=True)
            ins.then_inc(s["cum_ps"], 1)
            project("q1")
            project("v0")
            norm_sums(1)
            project("v1")

            def token_layout(src, t, bank):
                for h in range(H):
                    ins = pe.transpose(bank[:, h * HD:(h + 1) * HD], src[:, h * S + t * P:h * S + (t + 1) * P], ident)
                ins.then_inc(s["tr_ps"], 1)

            project("z0")
            pe.wait_ge(s["qk_n"], 1)
            pe.wait_ge(s["ss_e"], 1)
            for t in range(NT):
                token_layout(kT, t, B[2 + t])
            project("z1")
            pe.wait_ge(s["ract"], 6)
            pe.wait_ge(s["ss_e"], 2)
            for t in range(NT):
                token_layout(vT, t, B[4 + t])

            def decay_rows(t):
                if t == 1:
                    pe.wait_ge(s["dt_v"], 1)
                    pe.wait_ge(s["egb_a"], 1)
                for h in range(H):
                    c = t * H + h
                    ins = pe.matmul(B[6][:, h * HD:(h + 1) * HD], g[:, c:c + 1].broadcast_to([P, P]), const("tri"), start=True, stop=True)
                ins.then_inc(s["gcb_ps"], 1)
                if t == 1:
                    pe.wait_ge(s["lt_v"], 1)
                else:
                    pe.wait_ge(s["cum_a"], 2)
                    pe.wait_ge(s["cum_v"], 1)
                for h in range(H):
                    c = t * H + h
                    ins = pe.matmul(B[7][:, h * HD:(h + 1) * HD], beta[:, c:c + 1].broadcast_to([P, P]), ident, start=True, stop=True)
                ins.then_inc(s["bb_ps"], 1)

            def products(t):
                if t == 0:
                    pe.wait_ge(s["ktok"], 2 * NT * H)
                    pe.wait_ge(s["ktv"], NT * H)
                    pe.wait_ge(s["qk_n"], 2)
                for i, x in enumerate((kT, qT)):
                    for h in range(H):
                        a = slice(h * S + t * P, h * S + (t + 1) * P)
                        ins = pe.matmul(B[2 + 2 * i + t][:, h * HD:(h + 1) * HD], kT[:, a], x[:, a], start=True, stop=True)
                ins.then_inc(s["kk_ps"], 1)

            decay_rows(0)
            project("mq0")
            products(0)
            project("mq1")
            decay_rows(1)
            products(1)
            project("mk0")
            for t in range(NT):
                pe.wait_ge(s["lt_v"], t + 1)
                for h in range(H):
                    ins = pe.transpose(B[2 + t][:, h * HD:(h + 1) * HD], head(LT, t, h), ident)
                ins.then_inc(s["l_ps"], 1)
            project("mk1")

            def double_a(l, t):
                pe.wait_ge(s["t1_v"], 2 * NT) if l == 1 else pe.wait_ge(s["tt_v"], (l - 2) * NT + t + 1)
                for h in range(H):
                    ins = pe.matmul(B[2 + t][:, h * HD:(h + 1) * HD], head(LT, t, h), head(T, t, h), start=True, stop=True)
                ins.then_inc(s["a_ps"], 1)

            def double_x(l, t):
                pe.wait_ge(s["m_v"], (l - 1) * NT + t + 1)
                if l == 1:
                    pe.wait_ge(s["qk_v"], t + 1)
                if l < 5:
                    for h in range(H):
                        pe.matmul(B[4 + t][:, h * HD:(h + 1) * HD], head(TT, t, h), head(M, t, h), start=True, stop=True)
                for h in range(H):
                    ins = pe.matmul(B[6 + t][:, h * HD:(h + 1) * HD], head(M, t, h), head(TT, t, h), start=True, stop=True)
                ins.then_inc(s["x_ps"], 1)

            def step(names):
                for name in names.split():
                    kind = name[:-1]
                    if kind == "r":
                        ada_pair(name)
                    elif kind == "M":
                        mod_half(int(name[-1]))
                    elif kind == "mv":
                        project_v(name)
                    else:
                        project(name)

            between = (("r0 r1", "mv0"), ("M0 M1 r2", "r3 mv1"), ("M2 M3 r4", "g0"), ("r5 M4 M5", "g1"), ("r6 r7", "g2"))
            for l in range(1, 6):
                for t in range(NT):
                    double_a(l, t)
                step(between[l - 1][0])
                for t in range(NT):
                    double_x(l, t)
                step(between[l - 1][1])

            for t in range(NT):
                pe.wait_ge(s["tt_v"], 4 * NT + t + 1)
                for h in range(H):
                    pe.matmul(B[2 + t][:, h * HD:(h + 1) * HD], head(TT, t, h), head(vb, t, h), start=True, stop=True)
                for h in range(H):
                    ins = pe.matmul(B[6 + t][:, h * HD:(h + 1) * HD], head(kbg, t, h), head(TT, t, h), start=True, stop=True)
                ins.then_inc(s["uw_ps"], 1)
            step("M6 M7 g3")

            for n in range(4):
                t, hf = n // 2, n % 2
                r = slice(CHUNK * hf, CHUNK * hf + CHUNK)
                at = (0, CHUNK * hf)
                vnb = vn[:, hf * TW:(hf + 1) * TW]
                if n == 0:
                    pe.wait_ge(s["uw_a"], 4)
                else:
                    pe.wait_ge(s["s_v"], n)
                    for h in range(H):
                        ins = pe.matmul(B[6][r, h * HD:(h + 1) * HD], head(wT, t, h)[:, r], state[:, h * HD:(h + 1) * HD],
                                        start=True, stop=True, tile_position=at)
                    ins.then_inc(s["ws_ps"], 1)
                if n == 0:
                    pe.wait_ge(s["rope_v"], 2)
                q0 = n * S
                free_bank(USE[f"s{n}"])
                sc = bank("s", n)
                pe.matmul(sc[:, 0:P], mq[:, q0:q0 + P], mk[:, q0:q0 + P], start=True, stop=True)
                pe.matmul(sc[:, P:3 * P], mq[:, q0 + P:q0 + 2 * P], mk[:, q0:q0 + S], start=True, stop=True).then_inc(s["sc_ps"], 1)
                project(f"g{4 + n}")
                pe.wait_ge(s["vn_v"], n + 1)
                for h in range(H):
                    o = B[2 + t][r, h * HD:(h + 1) * HD]
                    if n:
                        pe.matmul(o, head(qd, t, h)[:, r], state[:, h * HD:(h + 1) * HD], start=True, stop=False, tile_position=at)
                    ins = pe.matmul(o, head(QK, t, h)[:, r], vnb[:, h * HD:(h + 1) * HD], start=(n == 0), stop=True, tile_position=at)
                ins.then_inc(s["o_ps"], 1)
                if n < 3:
                    for h in range(H):
                        ins = pe.matmul(B[7][:, h * HD:(h + 1) * HD], head(ktl, t, h), vnb[:, h * HD:(h + 1) * HD], start=True, stop=True)
                    ins.then_inc(s["st_ps"], 1)
                p = prob[:, (n % 2) * 768:(n % 2) * 768 + 384]
                pt = prob[:, (n % 2) * 768 + 384:(n % 2) * 768 + 768]
                pe.wait_ge(s["pn_v"], 2 * n + 2)
                free_bank(USE[f"t{n}"])
                for i in range(3):
                    ins = pe.transpose(bank("t", n)[:, i * P:(i + 1) * P], p[:, i * P:(i + 1) * P], ident)
                ins.then_inc(s["pt_ps"], 1)
                pe.wait_ge(s["pt_a"], n + 1)
                free_bank(USE[f"o{n}"])
                ob = bank("o", n)
                pe.matmul(ob[:, 0:P], head(mv, 0, n), pt[:, 0:P], start=True, stop=True)
                pe.matmul(ob[:, P:S], head(mv, 0, n), pt[:, P:2 * P], start=True, stop=False)
                pe.matmul(ob[:, P:S], head(mv, 1, n), pt[:, 2 * P:3 * P], start=False, stop=True).then_inc(s["ob_ps"], 1)

            for t in range(NT):
                pe.wait_ge(s["ro_v"], 1 + H * (t + 1))
                for h in range(H):
                    ins = pe.transpose(B[4 + t][:, h * HD:(h + 1) * HD], head(otok, t, h), ident)
                ins.then_inc(s["ot_ps"], 1)
            pe.wait_ge(s["ot_ps"], 2)
            pe.sem_inc(s["scratch_dead"], 1)
            pe.wait_ge(s["oa_v"], 2)
            pe.wait_ge(s["ob_a"], H)
            pe.wait_ge(s["o_a"], 4)
            for j in range(KD):
                wa, wb = unit(BR0 + 2 * (j // 4), H), unit(BR0 + 1 + 2 * (j // 4), H)
                if j >= 2:
                    pe.wait_ge(s["ya_v"], j - 1)
                for i, (w, o) in enumerate(((wa, oaT), (wb, obT))):
                    for k in range(H):
                        ins = pe.matmul(B[2 + j % 2][:, i * S:(i + 1) * S], w[:, k, (j % 4) * P:(j % 4 + 1) * P],
                                        o[:, k * S:(k + 1) * S], start=(k == 0), stop=(k == H - 1))
                ins.then_inc(s["ya_ps"], 1)
                if j % 4 == 3:
                    pe.wait_ge(s["ya_ps"], j + 1)
                    pe.sem_inc(s["unit_used"], 2)
            pe.wait_ge(s["ya_v"], KD)
            for n in range(4):
                w = unit(O0 + n)
                if n >= 2:
                    pe.wait_ge(s["mix_a"], n - 1)
                for t in range(NT):
                    ins = sum8(B[n % 2][:, t * BLK:(t + 1) * BLK], lambda k: hTk[:, k, t * P:(t + 1) * P], lambda k: w[:, k, :])
                ins.then_inc(s["mix_ps"], 1)
                pe.wait_ge(s["mix_ps"], n + 1)
                pe.sem_inc(s["unit_used"], 1)

            pe.wait_ge(s["h2"], 2)
            pe.wait_ge(s["mix_a"], 4)
            for n in range(4):
                for kk in range(2):
                    for t in range(NT):
                        k = 2 * n + kk
                        ins = pe.transpose(B[n][:, kk * S + t * P:kk * S + (t + 1) * P], gv[0][:, t * D + k * P:t * D + (k + 1) * P], ident)
                ins.then_inc(s["h2t_ps"], 1)
            pe.wait_ge(s["h2t"], 4)
            pe.wait_ge(s["x2_in"], 64)
            w3 = wrt[:, :].rearrange("p (k n) -> p k n", k=KD)
            for t in range(NT):
                ins = sum8(B[4][:, t * NE:(t + 1) * NE], lambda k: hTk[:, k, t * P:(t + 1) * P], lambda k: w3[:, k, :])
            ins.then_inc(s["lg_ps"], 1)
            selt, posm, wts = rt[:, 128:192], rt[:, 320:384], rt[:, 384:448]
            pe.wait_ge(s["sel_v"], 1)
            pe.matmul(B[5][:, 0:NE], const("before"), selt[:, 0:NE], start=True, stop=True)
            pe.matmul(B[5][:, NE:2 * NE], const("before"), selt[:, NE:2 * NE], start=True, stop=False)
            pe.matmul(B[5][:, NE:2 * NE], ones, selt[:, 0:NE], start=False, stop=True)
            for t in range(NT):
                pe.matmul(B[5][:, 2 * NE:3 * NE], ones, selt[:, t * NE:(t + 1) * NE], start=(t == 0), stop=(t == 1))
            for t in range(NT):
                ins = pe.matmul(B[5][0:NE, 96:97], selt[:, t * NE:(t + 1) * NE], ones[:, 0:1], start=(t == 0), stop=(t == 1))
            ins.then_inc(s["pos_ps"], 1)
            pe.wait_ge(s["pos_v"], 1)
            ncol = rt[0:NE, 520:521]
            pe.matmul(B[7][0:NE, 0:1], const("ntri32")[0:NE, :], ncol, start=True, stop=True)
            pe.matmul(B[7][0:NE, 1:2], const("tri32")[0:NE, :], ncol, start=True, stop=True)
            for i, x in enumerate((posm, wts)):
                for t in range(NT):
                    ins = pe.transpose(B[6][0:NE, (2 * i + t) * P:(2 * i + t + 1) * P], x[:, t * NE:(t + 1) * NE], ident)
            ins.then_inc(s["jt_ps"], 1)
            pe.wait_ge(s["oh_v"], 1)
            pqw, oh = ffn[0:NE, 0:512], ffn[0:NE, 512:512 + JC]
            for i in range(4):
                ins = pe.matmul(B[7][:, 128 + i * JC:128 + (i + 1) * JC], pqw[:, i * P:(i + 1) * P], oh, start=True, stop=True)
            ins.then_inc(s["job_ps"], 1)
            pe.wait_ge(s["bdn_in"], 16)
            for t in range(NT):
                for n in range(2):
                    ins = pe.matmul(B[2 + 2 * t + n][:, :], pqw[:, S + t * P:S + (t + 1) * P], bdn[:, n * 512:(n + 1) * 512], start=True, stop=True)
            ins.then_inc(s["y0_ps"], 1)
            pe.wait_ge(s["expert_rows"], 16)
            for n in range(2):
                for c in range(8):
                    ins = pe.matmul(B[n][:, c * JC:(c + 1) * JC], bgu[:, (8 * n + c) * P:(8 * n + c + 1) * P], oh, start=True, stop=True)
                ins.then_inc(s["bj_ps"], 1)
            pe.wait_ge(s["y0_v"], 4)

            def gather():
                for c in range(KD):
                    for i in range(3):
                        for t in range(NT):
                            ins = pe.matmul(B[3][:, c * SLOTS:(c + 1) * SLOTS], hb[:, i, t, c * P:(c + 1) * P],
                                            sgat[:, t * SLOTS:(t + 1) * SLOTS], start=(i == 0 and t == 0), stop=(i == 2 and t == 1))
                ins.then_inc(s["gat"], 1)

            pe.wait_ge(s["hb1"], 2)
            pe.wait_ge(s["selg"], 1)
            gather()
            pe.wait_ge(s["bj_a"], 2)
            pe.wait_ge(s["cnt_v"], 1)
            pe.wait_ge(s["tab_v"], 1)
            def weights(group, r, u):
                g = r * UPE + u
                pe.wait_ge(landed[g % RING], group * (16 * LAPS) + landed_count(g))
                return slot(g % RING)

            def job(j, group, r):
                pe.wait_ge(s["xg_a"], j + 1)
                pe.wait_ge(s["gu_a"], j + 1)
                pe.wait_ge(s["gu_v"], j + 1)
                pe.wait_ge(s["accd"], 4 * j + 4)
                for u in range(GU_UNITS):
                    w = weights(group, r, u)
                    for n in range(2):
                        for half in range(2):
                            ins = pe.matmul(B[n][64 * half:64 * half + 64, :], xg[:, u * SLOTS:(u + 1) * SLOTS],
                                            w[:, half * F + n * 512:half * F + (n + 1) * 512], start=(u == 0), stop=(u == GU_UNITS - 1),
                                            tile_position=(0, 64 * half))
                    ins.then_inc(used[u], 1)
                pe.wait_ge(s["selg"], j + 2)
                pe.wait_ge(s["c_a"], j + 1)
                gather()
                for q in range(2):
                    if q == 0:
                        pe.wait_ge(s["gu_a"], j + 2)
                        pe.wait_ge(s["act_v"], 2 * j + 2)
                    else:
                        pe.wait_ge(s["gu_v"], j + 2)
                    for c in range(4):
                        ins = pe.transpose(B[(2, 5)[q]][:, c * P:(c + 1) * P], gus[:, (4 * q + c) * P:(4 * q + c + 1) * P], ident)
                    ins.then_inc(s["trn"], 1)
                pe.wait_ge(s["y_a"], j + 1)
                pe.wait_ge(s["c_a"], j + 1)
                for i in range(4):
                    pe.matmul(B[ROW_BANK[i]][:, :], cab[:, i * P:(i + 1) * P], ysb, start=True, stop=True).then_inc(s["sc"], 1)
                pe.wait_ge(s["selw"], j + 1)
                pe.wait_ge(s["xg_a"], j + 2)
                for t in range(NT):
                    for half in range(2):
                        ins = pe.transpose(B[3][:, (2 * t + half) * P:(2 * t + half + 1) * P],
                                           swt[:, t * 192 + 64 - 64 * half:t * 192 + 192 - 64 * half], ident)
                ins.then_inc(s["ctr"], 1)
                for f in range(KF):
                    u = GU_UNITS + f // 2
                    if f == 0:
                        pe.wait_ge(s["act_v"], 2 * j + 3)
                    if f == 4:
                        pe.wait_ge(s["act_v"], 2 * j + 4)
                    w = weights(group, r, u)
                    for half in range(2):
                        ins = pe.matmul(B[4][64 * half:64 * half + 64, :], actT[:, f * SLOTS:(f + 1) * SLOTS],
                                        w[:, (f % 2) * D + half * 512:(f % 2) * D + (half + 1) * 512], start=(f == 0), stop=(f == KF - 1),
                                        tile_position=(0, 64 * half))
                    if f % 2:
                        ins.then_inc(used[u], 1)

            pe.sem_inc(s["ctr"], 1)
            with pe.Fori(0, NE // GROUP) as n:
                e0 = n * GROUP
                for r in range(GROUP):
                    first = pe.value_load(table[0:1, bass.ds(e0 + r, 1)], min_val=0, max_val=MAXJ)
                    end = pe.value_load(table[0:1, bass.ds(e0 + (r + 1), 1)], min_val=1, max_val=MAXJ)
                    with pe.Fori(first, end) as j:
                        job(j, n, r)
            J = pe.value_load(table[0:1, NE:NE + 1], min_val=NE, max_val=MAXJ)
            pe.wait_ge(s["y_a"], J + 1)
            pe.wait_ge(s["c_a"], J + 1)
            pe.wait_ge(s["accd"], 4 * J + 4)
            for i in range(4):
                pe.matmul(B[ROW_BANK[i]][:, :], cab[:, i * P:(i + 1) * P], ysb, start=True, stop=True).then_inc(s["sc"], 1)


def kernel(**inputs):
    import concourse.bacc as bacc
    from concourse.bass_utils import run_bass_kernel_spmd

    def arr(n):
        return np.asarray(inputs[n])

    def columns(v, n):
        return np.ascontiguousarray(v.reshape(n, P).T)

    x = arr("x")[0]
    data = {
        "x": x, "xT": np.ascontiguousarray(x.T),
        "columns": np.concatenate([
            columns(arr("g_pre_mix")[0], KD), columns(arr("b_ada")[0][:2 * D], 2 * KD),
            arr("conv_w")[0].reshape(TAPS, 12, P).transpose(2, 1, 0).reshape(P, 12 * TAPS),
            columns(arr("g_dn_out")[0], 1), columns(arr("c")[0], KD)], 1),
        "w_ada": arr("w_ada")[0], "b_ada": arr("b_ada"), "w_in": arr("w_in")[0],
        "g_post_mix": arr("g_post_mix"), "g_pre_ffn": arr("g_pre_ffn"), "g_post_ffn": arr("g_post_ffn"),
        "a_log": arr("a_log"), "dt_bias": arr("dt_bias"),
        "w_br_a": arr("w_br_a")[0], "w_br_b": arr("w_br_b")[0], "w_o": arr("w_o")[0],
        "w_router": arr("w_router")[0], "b_router": arr("b_router"),
        "w_gu": arr("w_gu")[0], "b_gu": arr("b_gu")[0], "w_down": arr("w_down")[0], "b_down": arr("b_down")[0],
        "cst": shape_constants(),
    }
    nc = bacc.Bacc("TRN2", target_bir_lowering=False, num_devices=1)
    arrays, A = {}, {}
    for n, a in data.items():
        a = np.ascontiguousarray(a)
        arrays[f"in_{n}"] = a
        A[n] = nc.dram_tensor(f"in_{n}", a.shape, mybir.dt.from_np(a.dtype), kind="ExternalInput").ap()
    out = nc.dram_tensor("out_0", (S, D), F32, kind="ExternalOutput").ap()
    build(nc, A, out)
    r = run_bass_kernel_spmd(nc, [arrays], core_ids=[0])
    return r.results[0]["out_0"].reshape(1, S, D)
```

```python
import numpy as np
import concourse.bass as bass
from concourse import mybir
from contextlib import ExitStack

F32 = mybir.dt.float32
BF16 = mybir.dt.bfloat16
I32 = mybir.dt.int32
ALU = mybir.AluOpType
ACT = mybir.ActivationFunctionType
AX = mybir.AxisListType

P = 128
D = 1024
S = 256
NT = S // P
KD = D // P
HD = 128
H = 4
W = H * HD
CHUNK = 64
TAPS = 4
HALF_ROPE = HD // 8
NE = 32
TOPK = 4
F = 1024
KF = F // P
SLOTS = 64
MAXJ = NE + S * TOPK // SLOTS
JC = MAXJ + 1
EPS = 1e-6
LIMIT = 7.0
ALPHA = 1.702
NEG = -1e30

BLK = 256
UNIT = KD * BLK
GU_UNITS = KD
DN_UNITS = KF // 2
UPE = GU_UNITS + DN_UNITS
RING = 16
ROW_BANK = (6, 7, 0, 1)
BIAS_BANK = (2, 4, 5, 6)
GROUP = 4
LAPS = GROUP * UPE // RING
OWN = 12
MIX_RING = 6

CONST = {}
_at = 0
for _name, _n in (("ident", 128), ("ones", 128), ("tri", 128), ("blockones", 128), ("firsthalf", 128),
                  ("secondhalf", 128), ("decaymask", 128), ("strict", 128), ("level", 6 * 128), ("level1t", 128),
                  ("before", 128), ("causal", 128), ("iota", JC), ("slot", SLOTS), ("cos", S), ("sin", S),
                  ("tri32", 32), ("ntri32", 32), ("expert", 1)):
    CONST[_name] = (_at, _n)
    _at += _n
NCONST = _at


def shape_constants():
    c = np.zeros((P, NCONST), np.float32)

    def put(name, value):
        a, n = CONST[name]
        c[:value.shape[0], a:a + n] = value

    i, j = np.arange(P)[:, None], np.arange(P)[None, :]
    same = i // CHUNK == j // CHUNK
    put("ident", (i == j).astype(np.float32))
    put("ones", np.ones((P, P), np.float32))
    put("tri", ((i <= j) & same).astype(np.float32))
    put("blockones", same.astype(np.float32))
    put("firsthalf", (i + 0 * j < CHUNK).astype(np.float32))
    put("secondhalf", (i + 0 * j >= CHUNK).astype(np.float32))
    put("decaymask", np.where((i <= j) & same, 0.0, NEG).astype(np.float32))
    put("strict", ((i < j) & same).astype(np.float32))
    levels = []
    for s in (1, 2, 4, 8, 16, 32):
        m = (i // (2 * s) == j // (2 * s)) & (i // s % 2 == 1) & (j // s % 2 == 0)
        levels.append(-m.astype(np.float32))
    put("level", np.concatenate(levels, 1))
    put("level1t", levels[0].T)
    put("before", (i < j).astype(np.float32))
    put("causal", np.where(j <= i, 0.0, NEG).astype(np.float32))
    put("iota", np.broadcast_to(np.arange(JC, dtype=np.float32), (P, JC)))
    put("slot", np.broadcast_to(np.arange(SLOTS, dtype=np.float32), (P, SLOTS)))
    inv = np.float32(500000.0) ** (-np.arange(HALF_ROPE, dtype=np.float32) / np.float32(HALF_ROPE))
    ang = (np.arange(S, dtype=np.float32)[:, None] * inv[None, :]).astype(np.float32).astype(np.float64)
    cos, sin = np.cos(ang).T.astype(np.float32), np.sin(ang).T.astype(np.float32)
    put("cos", np.concatenate([cos, cos]))
    put("sin", np.concatenate([-sin, sin]))
    e = np.arange(NE)
    put("tri32", (e[:, None] <= e[None, :]).astype(np.float32))
    put("ntri32", (e[:, None] < e[None, :]).astype(np.float32))
    put("expert", e[:, None].astype(np.float32))
    return c


def build(nc, A, out):
    ctx = ExitStack()
    with ctx:
        def sb(name, shape, dt=F32):
            return ctx.enter_context(nc.sbuf_tensor(name, shape, dt))

        def sem(name):
            return ctx.enter_context(nc.semaphore(name))

        B = [ctx.enter_context(nc.psum_tensor(f"bank{i}", [P, 512], F32)) for i in range(8)]

        ring = sb("ring", [P, OWN * UNIT])
        cst = sb("cst", [P, NCONST])
        hT = sb("hT", [P, KD * S])
        qkv = sb("qkv", [P, 3 * H * S])
        zT = sb("zT", [P, H * S])
        mbx = sb("mbx", [P, 3 * H * S])
        gates = sb("gates", [P, 2 * KD * S])
        oT = sb("oT", [P, 2 * H * S])
        rows = sb("rows", [P, 2 * D])
        xs = sb("xs", [P, NT * D])
        mod = sb("mod", [P, 5 * D])
        col = sb("col", [P, 8 + 16 + 48 + 1 + 8 + 8])
        wba = sb("wba", [P, KD * 8])
        wrt = sb("wrt", [P, KD * NE])
        sm = sb("sm", [P, 640])

        def const(name):
            a, n = CONST[name]
            return cst[:, a:a + n]

        ident, ones = const("ident"), const("ones")
        gcol, bcol = col[:, 0:8], col[:, 8:24]
        convw = col[:, 24:72]
        gdn = col[:, 72:73]
        ccol = col[:, 73:81]
        hTk = hT[:, :].rearrange("p (k t) -> p k t", k=KD)
        qT, kT, vT = (qkv[:, i * H * S:(i + 1) * H * S] for i in range(3))
        gv = [gates[:, i * KD * S:(i + 1) * KD * S] for i in range(2)]
        oaT, obT = oT[:, 0:H * S], oT[:, H * S:2 * H * S]
        mq, mk, mv = (mbx[:, i * H * S:(i + 1) * H * S] for i in range(3))

        scr = MIX_RING * UNIT

        def scratch(at, n):
            return ring[:, scr + at:scr + at + n]

        TW = H * HD
        vb, kbg, ktl, DT, LT, QK, T, TT, M, qd = (scratch(1024 * i, 1024) for i in range(10))
        state = scratch(10240, TW)
        prob = scratch(10752, 1536)
        silc = prob[:, 1280:1536]
        uu, wT, vn, otok = DT, LT, T, kbg
        squares, rnorm = scratch(1024 * 6, 2048), scratch(1024 * 3, 2048)
        egb = T

        def tile(buf, t):
            return buf[:, t * TW:(t + 1) * TW]

        def head(buf, t, h):
            return buf[:, t * TW + h * HD:t * TW + (h + 1) * HD]

        def small(a, n):
            return sm[:, a:a + n]

        shG = small(0, 16)
        ba = small(16, 16)
        beta, g, gc, eg, etail, bk, t8a, t8b = (small(32 + 8 * i, 8) for i in range(8))
        dec = small(96, 16)
        alog = small(112, 4)
        dtb = small(116, 4)
        ssum = small(120, 16)
        rsc = small(136, 16)
        mx = small(152, 16)
        baT = sm[0:8, 168:168 + S]
        rmsb = small(168, S)
        eps128 = small(424, 4)
        mstat = small(428, 8)
        rbr = small(436, NE)
        silr = small(468, KD)
        table = small(480, NE + 1 + JC)[0:1, :].bitcast(I32)

        hb = qkv[:, :].bitcast(BF16).rearrange("p (s t d) -> p s t d", s=3, t=NT)
        acc = gv[0]
        ffn = gv[1]
        gus = ffn[:, 0:1024]
        ysb = ffn[:, 1024:1536]
        cab = ffn[:, 1536:2048]
        xg = oT[:, 0:512]
        actT = oT[:, 512:1024]
        tg, tu, ts = zT[:, 384:896], oT[:, 1024:1536], oT[:, 1536:2048]
        swt = zT[:, 0:2 * 192]
        bgu = mbx[:, 0:2 * F // P * NE]
        rt = zT[:, 384:1024]
        bdn = mbx[:, 2 * D:3 * D]
        lv = const("level")
        posj = lv[:, 0:2 * NT * JC]
        sgat = lv[:, 256:256 + NT * SLOTS // 2].bitcast(BF16)
        GF, GM, SH2, G2 = (mod[:, i * D:(i + 1) * D] for i in range(4))
        gpm, gpf, gqf = (mbx[:, i * D:(i + 1) * D] for i in range(3))

        names = """const_in x_in small_in col_in wba_in x2_in rows_in modb_in bdn_in silu_c zeros sq_x ss_x ssx_e rt_x col_ps h_ok
            unit_used row_v proj conv ract a_read sq_k ss_ps ss_e rtn qk_n ba_ps ba_sb bat_ps ax axe g_ok cum_ps
            cum_a cum_v tr_ps ktok gcb_ps dt_v dt_a egb_a bb_ps kk_ps lt_v qk_v l_ps t1_v a_ps m_v x_ps tt_v
            uw_ps uw_a ws_ps vn_v o_ps o_a st_ps s_v ro_a ro_v ot_ps oa_v rope_v sc_ps mx_v p_a pn_v pt_ps
            pt_a ob_ps ob_a mod_a mod_v ya_ps ya_v mix_ps mix_a mix_q xss hss hb0 xsr x1 h2 hb1 h2t_ps h2t lg_ps lg_v ex_a
            sel_v pos_ps pos_v cnt_v jt_ps oh_v job_ps tab_v y0_ps zero_b selg gat xg_a gu_a gu_v
            trn g_rdy sg_rdy act_v ctr c_a y_a sc accd fss fsr fgain fo out_d vch ach scratch_dead bgu_in
            const2_in selw ktv""".split()
        s = {n: sem(n) for n in names}
        landed = [sem(f"landed{i}") for i in range(RING)]
        used = [sem(f"used{i}") for i in range(UPE)]

        order = "c0 c1 c2 c3 k0 k1 q0 q1 v0 v1 z0 z1 mq0 r0 mq1 mk0 r1 mk1 M0 r2 mv0 M1 r3 mv1 M2 r4 g0 M3 r5 g1 M4 r6 g2"
        order += " M5 r7 g3 s0 g4 t0 o0 M6 s1 g5 t1 o1 M7 s2 g6 t2 o2 s3 g7 t3 o3"
        order = order.split()
        plan = [name for name in order if name[0] != "r"]
        USE = {name: i for i, name in enumerate(plan)}
        IN_COLS = {"q": 0, "k": 512, "v": 1024, "z": 1536, "mq": 2056, "mk": 2568, "mv": 3080, "g": 3592}
        units, UNIT_OF = [], {}
        for name in order:
            kind, n = name[:-1], int(name[-1])
            if kind in IN_COLS or kind in "cr":
                UNIT_OF[name] = len(units)
            if kind in IN_COLS:
                units.append(("in", IN_COLS[kind] + n * BLK))
            elif kind in "cr":
                first = (2 * D if kind == "r" else 0) + 2 * n * BLK
                units += [("ada" if kind == "c" else "row", first), ("ada" if kind == "c" else "row", first + BLK)]
        BR0 = len(units)
        units += [("bra", 0), ("brb", 0), ("bra", 512), ("brb", 512)]
        O0 = len(units)
        units += [("o", i * BLK) for i in range(4)]
        NU = len(units)
        assert NU % MIX_RING == 0
        ROUNDS = NU // MIX_RING

        def reader(name):
            kind = name[:-1]
            if kind in ("q", "k", "v"):
                return "conv"
            return {"M": "mod_a", "s": "mx_v", "t": "pt_a", "o": "ob_a"}.get(kind, "a_read")

        def read_count(use):
            return sum(reader(n) == reader(plan[use]) for n in plan[:use + 1])

        def slot(i):
            if i < OWN:
                return ring[:, i * UNIT:(i + 1) * UNIT]
            return (hT[:, :], rows[:, :], mod[:, D:3 * D], mod[:, 3 * D:5 * D])[i - OWN]

        def landed_count(g):
            return 16 * (g // RING + 1) + (16 * ROUNDS if g % RING < MIX_RING else 0)

        def unit_source(i):
            kind, c = units[i]
            if kind in ("bra", "brb"):
                return A["w_br_a" if kind == "bra" else "w_br_b"][:, c:c + 512].rearrange("(k p) n -> p k n", p=P)
            w = A[{"ada": "w_ada", "row": "w_ada", "in": "w_in", "o": "w_o"}[kind]]
            return w[:, c:c + BLK].rearrange("(k p) n -> p k n", p=P)

        def wait_used(engine, i):
            rows_so_far = sum(kind == "row" for kind, _ in units[:i + 1])
            if units[i][0] == "row":
                engine.wait_ge(s["row_v"], rows_so_far)
            else:
                engine.wait_ge(s["unit_used"], i + 1 - rows_so_far)

        block = ctx.enter_context(nc.Block())

        def bank(kind, n):
            return B[USE[f"{kind}{n}"] % 2][:, :]

        def turns(name):
            return sum(n[:-1] not in ("s", "t", "o") for n in plan[:USE[name] + 1])

        @block.sync
        def _(sp):
            def load(e, g):
                u, dst = g % UPE, slot(g % RING)
                if u < GU_UNITS:
                    src = A["w_gu"][bass.ds(e, 1), u * P:(u + 1) * P, :].rearrange("e p n -> p (e n)")
                else:
                    v = u - GU_UNITS
                    src = A["w_down"][bass.ds(e, 1), v * 2 * P:(v + 1) * 2 * P, :].rearrange("e (f p) n -> p (e f) n", p=P)
                    dst = dst.rearrange("p (f n) -> p f n", f=2)
                sp.dma_start(dst, src).then_inc(landed[g % RING], 16)

            for i in range(NU):
                if i == O0:
                    sp.wait_ge(s["scratch_dead"], 1)
                    for g in range(MIX_RING, OWN):
                        load(0, g)
                if i >= MIX_RING:
                    wait_used(sp, i - MIX_RING)
                v = slot(i % MIX_RING).rearrange("p (k n) -> p k n", k=4 if units[i][0][:2] == "br" else KD)
                sp.dma_start(v, unit_source(i)).then_inc(landed[i % MIX_RING], 16)
                if i == 0:
                    sp.dma_start(wba[:, :].rearrange("p (k n) -> p k n", k=KD),
                                 A["w_in"][:, 2048:2056].rearrange("(k p) n -> p k n", p=P)).then_inc(s["wba_in"], 16)

            def group(e0, g0):
                last = None
                for g in range(g0, GROUP * UPE):
                    before = g - RING
                    de, u = before // UPE, before % UPE
                    if de != last:
                        jobs = sp.value_load(table[0:1, bass.ds(e0 + (de + 1), 1)], min_val=1, max_val=MAXJ)
                        last = de
                    sp.wait_ge(used[u], jobs)
                    load(e0 + g // UPE, g)

            for g in (*range(MIX_RING), *range(OWN, RING)):
                if g < MIX_RING:
                    wait_used(sp, NU - MIX_RING + g)
                elif g == OWN:
                    sp.wait_ge(s["lg_ps"], NT)
                elif g == OWN + 1:
                    sp.wait_ge(s["x1"], NT)
                elif g == OWN + 2:
                    sp.wait_ge(s["h2"], 4)
                load(g // UPE, g)
            sp.wait_ge(s["tab_v"], 1)
            group(0, RING)
            with sp.Fori(1, NE // GROUP) as n:
                group(n * GROUP, 0)
            for i in range(2 * NT):
                t, c = i // 2, (i % 2) * 512
                sp.wait_ge(s["fo"], i + 1)
                sp.dma_start(out[t * P:(t + 1) * P, c:c + 512], xs[:, t * D + c:t * D + c + 512]).then_inc(s["out_d"], 16)
            sp.wait_ge(s["out_d"], 16 * 2 * NT)

        @block.gpsimd
        def _(pool):
            pool.memset(silc, 0.0).then_inc(s["zeros"], 1)
            pool.wait_ge(s["proj"], turns("k0"))
            pool.dma_start(cst[:, 2 * P:], A["cst"][:, 2 * P:]).then_inc(s["const2_in"], 16)
            pool.wait_ge(s["proj"], turns("v0"))
            for i, c in enumerate((2048, 3072, 4096, 5120)):
                pool.dma_start(mod[:, (i + 1) % 4 * D:((i + 1) % 4 + 1) * D], A["b_ada"][0:1, c:c + D].partition_broadcast(P)).then_inc(s["modb_in"], 16)
            for t in range(NT):
                pool.dma_start(xs[:, t * D:(t + 1) * D], A["x"][t * P:(t + 1) * P, :]).then_inc(s["x2_in"], 16)
            pool.dma_start(rbr, A["b_router"][0:1, :].partition_broadcast(P)).then_inc(s["x2_in"], 16)
            pool.dma_start(wrt[:, :].rearrange("p (k n) -> p k n", k=KD),
                           A["w_router"].rearrange("(k p) n -> p k n", p=P)).then_inc(s["x2_in"], 16)
            pool.wait_ge(s["ob_a"], H)
            for i, n in enumerate(("g_post_mix", "g_pre_ffn", "g_post_ffn")):
                pool.dma_start(mbx[:, i * D:(i + 1) * D], A[n][0:1, :].partition_broadcast(P)).then_inc(s["rows_in"], 16)
            pool.wait_ge(s["mod_v"], 4)
            pool.memset(mbx[:, 2 * D:3 * D], 0.0).then_inc(s["zero_b"], 1)
            pool.wait_ge(s["zero_b"], 1)
            pool.dma_start(bdn[0:NE, :], A["b_down"]).then_inc(s["bdn_in"], 16)
            pool.dma_start(bgu, A["b_gu"]).then_inc(s["bgu_in"], 16)

        @block.scalar
        def _(act):
            def turn_done(kind, n):
                act.wait_ge(s["proj"], turns(f"{kind}{n}"))

            act.dma_start(col[:, 0:81], A["columns"]).then_inc(s["col_in"], 16)
            act.dma_start(hTk, A["xT"].rearrange("(k p) t -> p k t", p=P)).then_inc(s["x_in"], 16)
            act.dma_start(cst[:, 0:2 * P], A["cst"][:, 0:2 * P]).then_inc(s["const_in"], 16)
            act.dma_start(alog, A["a_log"][0:1, :].partition_broadcast(P)).then_inc(s["small_in"], 16)
            act.dma_start(dtb, A["dt_bias"][0:1, :].partition_broadcast(P)).then_inc(s["small_in"], 16)
            act.wait_ge(s["col_in"], 16)
            act.wait_ge(s["zeros"], 1)
            act.activation(silc.rearrange("p (k n) -> p k n", n=32)[:, :, 0], ccol, ACT.Silu).then_inc(s["silu_c"], 1)
            act.wait_ge(s["x_in"], 16)
            act.activation(gv[0], hT[:, :], ACT.Square).then_inc(s["sq_x"], 1)
            for q in range(4):
                turn_done("c", q)
                act.activation(rows[:, q * 512:(q + 1) * 512], bank("c", q), ACT.Copy).then_inc(s["a_read"], 1)
                if q == 1:
                    act.wait_ge(s["ssx_e"], 1)
                    act.activation(rmsb, rmsb, ACT.Sqrt).then_inc(s["rt_x"], 1)
            act.wait_ge(s["small_in"], 16 * 2)
            act.activation(alog, alog, ACT.Exp).then_inc(s["ach"], 1)

            def silu_conv(n):
                dst = (kT, kT, qT, qT, vT, vT)[n][:, (n % 2) * 512:(n % 2) * 512 + 512]
                act.wait_ge(s["conv"], n + 1)
                act.activation(dst, dst, ACT.Silu).then_inc(s["ract"], 1)

            def square_norm(which):
                src = kT if which == 0 else qT
                if which == 1:
                    act.wait_ge(s["ss_ps"], 1)
                act.wait_ge(s["ract"], 2 * which + 2)
                act.activation(squares[:, 0:1024], src, ACT.Square).then_inc(s["sq_k"], 1)

            def root_norm(which):
                r = rnorm[:, which * 1024:(which + 1) * 1024]
                act.wait_ge(s["ss_e"], which + 1)
                act.activation(r, r, ACT.Sqrt).then_inc(s["rtn"], 1)

            act.wait_ge(s["ba_ps"], 1)
            act.activation(baT, B[7][0:8, 0:S], ACT.Copy).then_inc(s["ba_sb"], 1)
            silu_conv(0)
            silu_conv(1)
            square_norm(0)
            act.wait_ge(s["ax"], 1)
            act.activation(beta.rearrange("p (t h) -> p t h", t=NT),
                           B[7][:, 256:272].rearrange("p (t h) -> p t h", t=NT)[:, :, 0:H], ACT.Sigmoid).then_inc(s["ach"], 1)
            act.activation(t8b, t8b, ACT.Exp).then_inc(s["ach"], 1)
            act.wait_ge(s["ach"], 3)
            act.activation(t8b, t8b, ACT.Ln, bias=1.0).then_inc(s["axe"], 1)
            silu_conv(2)
            root_norm(0)
            silu_conv(3)
            square_norm(1)
            act.wait_ge(s["cum_v"], 1)
            act.activation(eg, B[7][:, 0:8], ACT.Exp).then_inc(s["cum_a"], 1)
            act.activation(dec, B[7][:, 16:32], ACT.Exp).then_inc(s["cum_a"], 1)
            act.activation(etail, t8a, ACT.Exp).then_inc(s["cum_a"], 1)
            silu_conv(4)
            root_norm(1)
            silu_conv(5)

            for n in range(2):
                turn_done("z", n)
                act.activation(zT[:, n * 512:(n + 1) * 512], bank("z", n), ACT.Silu).then_inc(s["a_read"], 1)

            def decay_exp(t):
                act.wait_ge(s["dt_v"], t + 1)
                if t == 0:
                    act.wait_ge(s["ss_ps"], 2)
                act.activation(tile(egb, t), B[6][:, :], ACT.Exp).then_inc(s["egb_a"], 1)
                act.activation(tile(DT, t), tile(DT, t), ACT.Exp).then_inc(s["dt_a"], 1)

            for t in range(NT):
                act.wait_ge(s["ktv"], H * (t + 1))
                act.wait_ge(s["cum_a"], 3)
                for h in range(H):
                    c = t * H + h
                    act.activation(head(ktl, t, h), B[2 + t][:, h * HD:(h + 1) * HD], ACT.Copy,
                                   scale=etail[:, c:c + 1]).then_inc(s["ktok"], 1)
            for t in range(NT):
                act.wait_ge(s["tr_ps"], NT + t + 1)
                for h in range(H):
                    c = t * H + h
                    act.activation(head(vb, t, h), B[4 + t][:, h * HD:(h + 1) * HD], ACT.Copy,
                                   scale=beta[:, c:c + 1]).then_inc(s["ktok"], 1)
            decay_exp(0)

            def copy_rotary(n):
                kind = ("mq", "mk")[n // 2]
                turn_done(kind, n % 2)
                dst = (mq, mk)[n // 2][:, (n % 2) * 512:(n % 2) * 512 + 512]
                act.activation(dst, bank(kind, n % 2), ACT.Copy).then_inc(s["a_read"], 1)

            def copy_v(n):
                turn_done("mv", n)
                for t in range(NT):
                    ins = act.activation(mv[:, t * TW + n * BLK:t * TW + (n + 1) * BLK],
                                         bank("mv", n)[:, t * BLK:(t + 1) * BLK], ACT.Copy)
                ins.then_inc(s["a_read"], 1)

            def gate_sig(n):
                turn_done("g", n)
                act.activation(gv[n // 4][:, (n % 4) * 512:(n % 4) * 512 + 512], bank("g", n),
                               ACT.Sigmoid).then_inc(s["a_read"], 1)

            copy_rotary(0)
            decay_exp(1)
            copy_rotary(1)
            copy_rotary(2)
            copy_rotary(3)

            copy_v(0)
            copy_v(1)
            for n in range(3):
                gate_sig(n)
            for t in range(NT):
                act.wait_ge(s["uw_ps"], t + 1)
                act.activation(tile(uu, t), B[2 + t][:, :], ACT.Copy).then_inc(s["uw_a"], 1)
                act.activation(tile(wT, t), B[6 + t][:, :], ACT.Copy).then_inc(s["uw_a"], 1)
            gate_sig(3)

            def softmax_exp(h):
                p = prob[:, (h % 2) * 768:(h % 2) * 768 + 384]
                act.wait_ge(s["mx_v"], h + 1)
                act.activation(p[:, 0:128], p[:, 0:128], ACT.Exp, bias=mstat[:, 0:1], scale=HD ** -0.5, accum_out=mstat[:, 2:3]).then_inc(s["p_a"], 1)
                act.activation(p[:, 128:384], p[:, 128:384], ACT.Exp, bias=mstat[:, 1:2], scale=HD ** -0.5, accum_out=mstat[:, 3:4]).then_inc(s["p_a"], 1)

            def probs_copy(h):
                pt = prob[:, (h % 2) * 768 + 384:(h % 2) * 768 + 768]
                act.wait_ge(s["pt_ps"], h + 1)
                act.activation(pt, bank("t", h)[:, 0:384], ACT.Copy).then_inc(s["pt_a"], 1)

            def head_copy(h):
                act.wait_ge(s["ob_ps"], h + 1)
                act.activation(obT[:, h * S:(h + 1) * S], bank("o", h)[:, 0:S], ACT.Copy).then_inc(s["ob_a"], 1)

            def out_copy(n):
                t, r0 = n // 2, CHUNK * (n % 2)
                act.wait_ge(s["o_ps"], n + 1)
                act.activation(tile(otok, t)[r0:r0 + CHUNK, :], B[2 + t][r0:r0 + CHUNK, :], ACT.Copy).then_inc(s["o_a"], 1)

            for n in range(4):
                softmax_exp(n)
                gate_sig(4 + n)
                probs_copy(n)
                out_copy(n)
                head_copy(n)

            for t in range(NT):
                act.wait_ge(s["o_a"], 2 * t + 2)
                act.activation(tile(qd, t), tile(otok, t), ACT.Square).then_inc(s["ro_a"], 1)
            act.wait_ge(s["ro_v"], 1)
            act.activation(rsc[:, 0:8], ssum[:, 0:8], ACT.Sqrt).then_inc(s["ro_a"], 1)

            for n in range(4):
                act.wait_ge(s["mix_ps"], n + 1)
                for t in range(NT):
                    ins = act.activation(rows[:, t * D + n * BLK:t * D + (n + 1) * BLK],
                                         B[n % 2][:, t * BLK:(t + 1) * BLK], ACT.Copy)
                ins.then_inc(s["mix_a"], 1)
                if n == 0:
                    act.wait_ge(s["ya_v"], KD)
                for t in range(NT):
                    ins = act.activation(gv[1][:, (NT * n + t) * BLK:(NT * n + t + 1) * BLK], B[n % 2][:, t * BLK:(t + 1) * BLK],
                                         ACT.Square, accum_out=ssum[:, 4 * t + n:4 * t + n + 1])
                ins.then_inc(s["mix_q"], 1)
            act.wait_ge(s["xsr"], 1)
            act.activation(rsc[:, 0:2], ssum[:, 10:12], ACT.Sqrt).then_inc(s["xss"], 1)
            for t in range(NT):
                act.wait_ge(s["x1"], t + 1)
                act.activation(hT[:, t * D:(t + 1) * D], xs[:, t * D:(t + 1) * D], ACT.Square,
                               accum_out=ssum[:, 12 + t:13 + t]).then_inc(s["hss"], 1)
                act.wait_ge(s["xsr"], t + 2)
                act.activation(rsc[:, 4 + t:5 + t], ssum[:, 14 + t:15 + t], ACT.Sqrt).then_inc(s["hss"], 1)
            for t in range(NT):
                a = slice(t * D, (t + 1) * D)
                for q in range(2):
                    act.wait_ge(s["h2t_ps"], 2 * t + q + 1)
                    act.wait_ge(s["hss"], 4)
                    act.activation(hTk[:, 4 * q:4 * q + 4, t * P:(t + 1) * P],
                                   B[2 * t + q][:, :].rearrange("p (k x) -> p k x", k=4), ACT.Copy).then_inc(s["h2t"], 1)
                act.activation(hb[:, 0, t, :], gv[0][:, a], ACT.Copy).then_inc(s["hb0"], 1)
            act.wait_ge(s["lg_v"], 1)
            for t in range(NT):
                act.activation(rt[:, 64 + t * NE:64 + (t + 1) * NE], rt[:, t * NE:(t + 1) * NE], ACT.Exp,
                               bias=mx[:, 8 * t + 1:8 * t + 2]).then_inc(s["ex_a"], 1)
            act.wait_ge(s["gat"], 1)
            act.activation(xg, B[3][:, :], ACT.Copy).then_inc(s["xg_a"], 1)
            act.wait_ge(s["tab_v"], 1)
            J = act.value_load(table[0:1, NE:NE + 1], min_val=NE, max_val=MAXJ)
            act.sem_inc(s["gu_a"], 1)
            act.sem_inc(s["c_a"], 1)
            act.sem_inc(s["y_a"], 1)
            act.sem_inc(s["sg_rdy"], 2)
            with act.Fori(0, J) as j:
                act.wait_ge(used[GU_UNITS - 1], j + 1)
                act.activation(gus[:, 0:512], B[0][:, :], ACT.Copy).then_inc(s["gu_a"], 1)
                act.wait_ge(s["gat"], j + 2)
                act.activation(xg, B[3][:, :], ACT.Copy).then_inc(s["xg_a"], 1)
                for q in range(2):
                    act.wait_ge(s["g_rdy"], 2 * j + q + 1)
                    act.activation(ts[:, q * 256:(q + 1) * 256], tg[:, q * 256:(q + 1) * 256], ACT.Sigmoid, scale=ALPHA).then_inc(s["sg_rdy"], 1)
                act.wait_ge(s["ctr"], j + 2)
                act.activation(cab, B[3][:, :], ACT.Copy).then_inc(s["c_a"], 1)
                act.wait_ge(used[UPE - 1], j + 1)
                act.activation(ysb, B[4][:, :], ACT.Copy).then_inc(s["y_a"], 1)

            act.activation(mstat[:, 0:1], const("ones")[:, 0:1], ACT.Sqrt).then_inc(s["ach"], 1)
            for t in range(NT):
                act.wait_ge(s["accd"], 4 * J + (6 + 2 * t))
                act.activation(qkv[:, t * D:(t + 1) * D], acc[:, t * D:(t + 1) * D], ACT.Square,
                               accum_out=ssum[:, 8 + t:9 + t]).then_inc(s["fss"], 1)
            act.wait_ge(s["fsr"], 1)
            act.activation(rsc[:, 8:10], ssum[:, 10:12], ACT.Sqrt).then_inc(s["fss"], 1)

        @block.vector
        def _(dve):
            v = nc.vector
            done = [0]

            def chain(ins):
                done[0] += 1
                ins.then_inc(s["vch"], 1)

            def settle():
                dve.wait_ge(s["vch"], done[0])

            def heads4(ap):
                return ap.rearrange("p (h d) -> p h d", h=H)

            def over_heads(ap):
                return ap.rearrange("p (a d) -> p a d", a=1).broadcast_to([P, H, ap.shape[1]])

            def root_arg(dst, src, scale, eps):
                return v.tensor_scalar(dst, src, scale, eps, ALU.mult, ALU.add)

            dve.wait_ge(s["ss_x"], 1)
            root_arg(rmsb, B[7][:, 0:S], 1.0 / D, EPS).then_inc(s["ssx_e"], 1)
            dve.wait_ge(s["rt_x"], 1)
            chain(v.reciprocal(rmsb, rmsb))
            settle()
            chain(v.tensor_tensor(hTk, hTk, rmsb.rearrange("p (a t) -> p a t", a=1).broadcast_to([P, KD, S]), ALU.mult))
            dve.wait_ge(s["col_ps"], 1)
            dve.wait_ge(s["col_in"], 16)
            chain(v.tensor_tensor(shG, B[6][:, 0:16], bcol, ALU.add))
            settle()
            chain(v.scalar_tensor_tensor(out=shG[:, 8:16], in0=shG[:, 8:16], scalar=1.0, in1=gcol, op0=ALU.add, op1=ALU.mult))
            settle()
            for k in range(KD):
                v.tensor_scalar(hTk[:, k, :], hTk[:, k, :], shG[:, 8 + k:9 + k], shG[:, k:k + 1], ALU.mult, ALU.add).then_inc(s["h_ok"], 1)

            def conv(n):
                base = (kT, kT, qT, qT, vT, vT)[n]
                first = (4, 6, 0, 2, 8, 10)[n]
                name = ("k0", "k1", "q0", "q1", "v0", "v1")[n]
                dve.wait_ge(s["proj"], turns(name))
                for j in range(TAPS):
                    if j:
                        settle()
                    for c in range(2):
                        x = B[USE[name] % 2][:, c * S:(c + 1) * S]
                        y = base[:, (n % 2) * 512 + c * S:(n % 2) * 512 + (c + 1) * S]
                        w = convw[:, (first + c) * TAPS + TAPS - 1 - j:(first + c) * TAPS + TAPS - j]
                        if j == 0:
                            ins = v.tensor_scalar(y, x, w, None, ALU.mult)
                        else:
                            ins = v.scalar_tensor_tensor(out=y[:, j:], in0=x[:, 0:S - j], scalar=w, in1=y[:, j:], op0=ALU.mult, op1=ALU.add)
                        if j < TAPS - 1 or c == 0:
                            chain(ins)
                        else:
                            ins.then_inc(s["conv"], 1)

            def norm_arg(which):
                dve.wait_ge(s["ss_ps"], which + 1)
                for i in range(2):
                    ins = v.tensor_scalar(rnorm[:, which * 1024 + i * 512:which * 1024 + (i + 1) * 512],
                                          B[2 + 2 * which + i][:, :], 1e-6, None, ALU.add)
                    if i == 0:
                        chain(ins)
                ins.then_inc(s["ss_e"], 1)

            def normalise(which):
                r = rnorm[:, which * 1024:(which + 1) * 1024]
                dve.wait_ge(s["rtn"], which + 1)
                chain(v.reciprocal(r, r))
                settle()
                if which == 0:
                    v.tensor_tensor(kT, kT, r, ALU.mult).then_inc(s["qk_n"], 1)
                else:
                    v.scalar_tensor_tensor(out=qT, in0=qT, scalar=HD ** -0.5, in1=r, op0=ALU.mult, op1=ALU.mult).then_inc(s["qk_n"], 1)

            conv(0)
            conv(1)
            dve.wait_ge(s["bat_ps"], 1)
            dve.wait_ge(s["small_in"], 16 * 2)
            chain(v.tensor_tensor(t8a.rearrange("p (t h) -> p t h", t=NT), B[7][:, 256:272].rearrange("p (t h) -> p t h", t=NT)[:, :, H:2 * H],
                                  dtb.rearrange("p (a h) -> p a h", a=1).broadcast_to([P, NT, H]), ALU.add))
            settle()
            chain(v.tensor_scalar(gc, t8a, -1.0, None, ALU.mult))
            settle()
            v.tensor_tensor(t8b, t8a, gc, ALU.min).then_inc(s["ax"], 1)
            conv(2)
            norm_arg(0)
            dve.wait_ge(s["axe"], 1)
            chain(v.scalar_tensor_tensor(out=g, in0=t8a, scalar=0.0, in1=t8b, op0=ALU.max, op1=ALU.add))
            settle()
            v.scalar_tensor_tensor(out=g.rearrange("p (t h) -> p t h", t=NT), in0=g.rearrange("p (t h) -> p t h", t=NT), scalar=-1.0,
                                   in1=alog.rearrange("p (a h) -> p a h", a=1).broadcast_to([P, NT, H]),
                                   op0=ALU.mult, op1=ALU.mult).then_inc(s["g_ok"], 1)
            conv(3)
            normalise(0)
            dve.wait_ge(s["cum_ps"], 1)
            chain(v.tensor_copy(gc, B[7][:, 0:8]))
            settle()
            v.tensor_tensor(t8a, B[7][:, 8:16], gc, ALU.subtract).then_inc(s["cum_v"], 1)
            dve.wait_ge(s["cum_a"], 1)
            v.tensor_tensor(bk, beta, eg, ALU.mult).then_inc(s["cum_v"], 1)
            conv(4)
            norm_arg(1)
            conv(5)
            normalise(1)
            dve.wait_ge(s["cum_v"], 2)
            for t in range(NT):
                dve.wait_ge(s["tr_ps"], t + 1)
                for h in range(H):
                    c = t * H + h
                    v.tensor_scalar(head(kbg, t, h), B[2 + t][:, h * HD:(h + 1) * HD], bk[:, c:c + 1], None, ALU.mult).then_inc(s["ktv"], 1)

            ROWS_AT = {"P0": [(0, 0)], "P1": [(0, 1)], "P2": [(1, 0)], "P3": [(1, 1)], "A1": [(2, 0)], "B1": [(2, 1)],
                       "A2": [(3, 0)], "B2": [(3, 1)], "A3": [(4, 0)], "B3": [(4, 1)], "A4": [(5, 0)], "B4": [(5, 1)],
                       "A5": [(6, 0)], "B5": [(6, 1)], "U": [(7, 0), (7, 1)]}

            def mod_row(i, part):
                first = UNIT_OF[f"r{i}"]
                if i >= 4 and part == 0:
                    dve.wait_ge(s["proj"], turns(f"M{i - 4}"))
                for k in range(4 * part, 4 * part + 4):
                    settle()
                    for n in range(2):
                        u = first + n
                        if k == 0:
                            dve.wait_ge(landed[u % MIX_RING], 16 * (u // MIX_RING + 1))
                        w = slot(u % MIX_RING).rearrange("p (k n) -> p k n", k=KD)[:, k, :]
                        a = (i % 4) * 512 + n * BLK
                        y, c = rows[:, a:a + BLK], silr[:, k:k + 1]
                        if k == 0:
                            ins = v.tensor_scalar(y, w, c, None, ALU.mult)
                        else:
                            ins = v.scalar_tensor_tensor(out=y, in0=w, scalar=c, in1=y, op0=ALU.mult, op1=ALU.add)
                        if k < KD - 1:
                            chain(ins)
                        else:
                            ins.then_inc(s["row_v"], 1)

            def mod_rows(place):
                for i, part in ROWS_AT.get(place, ()):
                    mod_row(i, part)

            chain(v.tensor_copy(silr, silc.rearrange("p (k n) -> p k n", n=32)[:, :, 0]))
            dve.wait_ge(s["const2_in"], 16)
            def decay_arg(t):
                dve.wait_ge(s["gcb_ps"], t + 1)
                for h in range(H):
                    ins = v.scalar_tensor_tensor(out=head(DT, t, h), in0=B[6][:, h * HD:(h + 1) * HD], scalar=gc[:, t * H + h:t * H + h + 1],
                                                 in1=const("decaymask"), op0=ALU.subtract, op1=ALU.add)
                    if h < H - 1:
                        chain(ins)
                ins.then_inc(s["dt_v"], 1)

            def lower(t):
                dve.wait_ge(s["dt_a"], t + 1)
                chain(v.tensor_tensor(heads4(tile(LT, t)), heads4(tile(DT, t)), over_heads(const("strict")), ALU.mult))
                dve.wait_ge(s["kk_ps"], t + 1)
                dve.wait_ge(s["bb_ps"], t + 1)
                settle()
                chain(v.tensor_tensor(tile(LT, t), tile(LT, t), B[7][:, :], ALU.mult))
                settle()
                v.tensor_tensor(tile(LT, t), tile(LT, t), B[2 + t][:, :], ALU.mult).then_inc(s["lt_v"], 1)
                v.tensor_tensor(tile(QK, t), tile(DT, t), B[4 + t][:, :], ALU.mult).then_inc(s["qk_v"], 1)
                dve.wait_ge(s["egb_a"], t + 1)
                chain(v.tensor_tensor(heads4(tile(qd, t)), heads4(qT)[:, :, t * P:(t + 1) * P], heads4(tile(egb, t)), ALU.mult))

            mod_rows("P0")
            decay_arg(0)
            mod_rows("P1")
            lower(0)
            decay_arg(1)
            mod_rows("P2")
            lower(1)
            mod_rows("P3")

            def level(l):
                a = const("level")[:, l * P:(l + 1) * P]
                return over_heads(a)

            for t in range(NT):
                dve.wait_ge(s["l_ps"], t + 1)
                settle()
                chain(v.tensor_tensor(heads4(tile(T, t)), heads4(B[2 + t][:, :]), level(0), ALU.mult))
                chain(v.tensor_tensor(heads4(tile(TT, t)), heads4(tile(LT, t)), over_heads(const("level1t")), ALU.mult))
                settle()
                v.tensor_tensor(heads4(tile(T, t)), heads4(tile(T, t)), over_heads(ident), ALU.add).then_inc(s["t1_v"], 1)
                v.tensor_tensor(heads4(tile(TT, t)), heads4(tile(TT, t)), over_heads(ident), ALU.add).then_inc(s["t1_v"], 1)
            def rotary(i):
                swap = [(c + HALF_ROPE) % (2 * HALF_ROPE) for c in range(2 * HALF_ROPE)]
                R = 2 * HALF_ROPE
                m = (mq, mk)[i]
                tmp = prob[0:R, 0:H * S]
                rows32 = m[0:R, :].rearrange("p (h t) -> p h t", h=H)
                c4 = const("cos")[0:R, :].rearrange("p (a t) -> p a t", a=1).broadcast_to([R, H, S])
                s4 = const("sin")[0:R, :].rearrange("p (a t) -> p a t", a=1).broadcast_to([R, H, S])
                dve.wait_ge(s["a_read"], read_count(USE["mk1"]))
                settle()
                chain(v.stream_shuffle(tmp, m[0:R, :], swap))
                settle()
                chain(v.tensor_tensor(tmp.rearrange("p (h t) -> p h t", h=H), tmp.rearrange("p (h t) -> p h t", h=H), s4, ALU.mult))
                chain(v.tensor_tensor(rows32, rows32, c4, ALU.mult))
                settle()
                v.tensor_tensor(m[0:R, :], m[0:R, :], tmp, ALU.add).then_inc(s["rope_v"], 1)
                dve.wait_ge(s["rope_v"], i + 1)

            def mod_sum(i):
                dve.wait_ge(s["proj"], turns(f"M{i}"))
                dve.wait_ge(s["modb_in"], 64)
                row = (i // 2 + 1) % 4 * D + i % 2 * 512
                v.tensor_tensor(mod[:, row:row + 512], mod[:, row:row + 512], bank("M", i), ALU.add).then_inc(s["mod_a"], 1)

            ROT = (1, 4)
            for l in range(1, 6):
                for t in range(NT):
                    i = (l - 1) * NT + t
                    dve.wait_ge(s["a_ps"], i + 1)
                    v.tensor_tensor(heads4(tile(M, t)), heads4(B[2 + t][:, :]), level(l), ALU.mult).then_inc(s["m_v"], 1)
                if l in ROT:
                    rotary(ROT.index(l))
                mod_sum(l - 1)
                mod_rows(f"A{l}")
                for t in range(NT):
                    i = (l - 1) * NT + t
                    dve.wait_ge(s["x_ps"], i + 1)
                    if l < 5:
                        chain(v.tensor_tensor(tile(T, t), tile(T, t), B[4 + t][:, :], ALU.add))
                    v.tensor_tensor(tile(TT, t), tile(TT, t), B[6 + t][:, :], ALU.add).then_inc(s["tt_v"], 1)
                mod_rows(f"B{l}")
            settle()
            chain(v.memset(vn, 0.0))
            mod_sum(5)
            mod_rows("U")

            for n in range(4):
                t, hf = n // 2, n % 2
                r = slice(CHUNK * hf, CHUNK * hf + CHUNK)
                vnb = vn[:, hf * TW:(hf + 1) * TW]
                if n in (1, 2):
                    mod_sum(5 + n)
                dve.wait_ge(s["uw_a"], 2 * t + 1)
                settle()
                if n == 0:
                    v.tensor_copy(vnb[r, :], tile(uu, t)[r, :]).then_inc(s["vn_v"], 1)
                else:
                    dve.wait_ge(s["ws_ps"], n)
                    v.tensor_tensor(vnb[r, :], tile(uu, t)[r, :], B[6][r, :], ALU.subtract).then_inc(s["vn_v"], 1)
                p = prob[:, (n % 2) * 768:(n % 2) * 768 + 384]
                dve.wait_ge(s["sc_ps"], n + 1)
                if n:
                    dve.wait_ge(s["pn_v"], 2 * n)
                if n >= 2:
                    dve.wait_ge(s["pt_ps"], n - 1)
                chain(v.tensor_tensor(p[:, 0:128], bank("s", n)[:, 0:128], const("causal"), ALU.add))
                chain(v.tensor_copy(p[:, 128:256], bank("s", n)[:, 128:256]))
                chain(v.tensor_tensor(p[:, 256:384], bank("s", n)[:, 256:384], const("causal"), ALU.add))
                settle()
                chain(v.tensor_reduce(mstat[:, 0:1], p[:, 0:128], AX.X, ALU.max))
                chain(v.tensor_reduce(mstat[:, 1:2], p[:, 128:384], AX.X, ALU.max))
                settle()
                v.tensor_scalar(mstat[:, 0:2], mstat[:, 0:2], -HD ** -0.5, None, ALU.mult).then_inc(s["mx_v"], 1)
                dve.wait_ge(s["p_a"], 2 * n + 2)
                chain(v.reciprocal(mstat[:, 4:6], mstat[:, 2:4]))
                settle()
                v.tensor_scalar(p[:, 0:128], p[:, 0:128], mstat[:, 4:5], None, ALU.mult).then_inc(s["pn_v"], 1)
                v.tensor_scalar(p[:, 128:384], p[:, 128:384], mstat[:, 5:6], None, ALU.mult).then_inc(s["pn_v"], 1)
                if n < 3:
                    dve.wait_ge(s["st_ps"], n + 1)
                    if n == 0:
                        v.tensor_copy(state, B[7][:, :]).then_inc(s["s_v"], 1)
                    else:
                        for h in range(H):
                            c = hf * 8 + t * H + h
                            st = state[:, h * HD:(h + 1) * HD]
                            ins = v.scalar_tensor_tensor(out=st, in0=st, scalar=dec[:, c:c + 1], in1=B[7][:, h * HD:(h + 1) * HD],
                                                         op0=ALU.mult, op1=ALU.add)
                            if h < H - 1:
                                chain(ins)
                        ins.then_inc(s["s_v"], 1)
                    dve.wait_ge(s["s_v"], n + 1)

            for t in range(NT):
                dve.wait_ge(s["ro_a"], t + 1)
                chain(v.tensor_reduce(ssum[:, t * H:(t + 1) * H], heads4(tile(qd, t)), AX.X, ALU.add))
            settle()
            root_arg(ssum[:, 0:8], ssum[:, 0:8], 1.0 / HD, EPS).then_inc(s["ro_v"], 1)
            dve.wait_ge(s["ro_a"], 3)
            chain(v.reciprocal(rsc[:, 0:8], rsc[:, 0:8]))
            settle()
            for t in range(NT):
                for h in range(H):
                    v.tensor_scalar(head(otok, t, h), head(otok, t, h), rsc[:, t * H + h:t * H + h + 1], None, ALU.mult).then_inc(s["ro_v"], 1)
            for t in range(NT):
                dve.wait_ge(s["ot_ps"], t + 1)
                v.scalar_tensor_tensor(out=heads4(oaT)[:, :, t * P:(t + 1) * P], in0=heads4(B[4 + t][:, :]), scalar=gdn,
                                       in1=heads4(zT)[:, :, t * P:(t + 1) * P], op0=ALU.mult, op1=ALU.mult).then_inc(s["oa_v"], 1)
            for j in range(KD):
                b = B[2 + j % 2]
                ga, gb = (gv[i][:, j * S:(j + 1) * S] for i in range(2))
                dve.wait_ge(s["ya_ps"], j + 1)
                if j == 0:
                    dve.wait_ge(s["a_read"], read_count(USE["g7"]))
                chain(v.tensor_tensor(ga, ga, b[:, 0:S], ALU.mult))
                chain(v.tensor_tensor(gb, gb, b[:, S:2 * S], ALU.mult))
                settle()
                v.tensor_tensor(hTk[:, j, :], ga, gb, ALU.add).then_inc(s["ya_v"], 1)
            dve.wait_ge(s["rows_in"], 48)
            dve.wait_ge(s["mod_a"], 8)
            v.tensor_tensor(GM, GM, gpm, ALU.mult).then_inc(s["mod_v"], 1)
            v.scalar_tensor_tensor(out=G2, in0=G2, scalar=1.0, in1=gpf, op0=ALU.add, op1=ALU.mult).then_inc(s["mod_v"], 1)
            v.tensor_tensor(GF, GF, gqf, ALU.mult).then_inc(s["mod_v"], 2)

            dve.wait_ge(s["mod_v"], 4)
            for n in range(4):
                dve.wait_ge(s["mix_a"], n + 1)
                for t in range(NT):
                    a = slice(t * D + n * BLK, t * D + (n + 1) * BLK)
                    chain(v.tensor_tensor(gv[0][:, a], rows[:, a], GM[:, n * BLK:(n + 1) * BLK], ALU.mult))
            dve.wait_ge(s["mix_q"], 4)
            chain(v.tensor_reduce(ssum[:, 8:10], ssum[:, 0:8].rearrange("p (t n) -> p t n", t=NT), AX.X, ALU.add))
            settle()
            root_arg(ssum[:, 10:12], ssum[:, 8:10], 1.0 / D, EPS).then_inc(s["xsr"], 1)
            dve.wait_ge(s["xss"], 1)
            chain(v.reciprocal(rsc[:, 2:4], rsc[:, 0:2]))
            settle()
            dve.wait_ge(s["x2_in"], 64)
            for t in range(NT):
                a = slice(t * D, (t + 1) * D)
                v.scalar_tensor_tensor(out=xs[:, a], in0=gv[0][:, a], scalar=rsc[:, 2 + t:3 + t], in1=xs[:, a], op0=ALU.mult, op1=ALU.add).then_inc(s["x1"], 1)
            for t in range(NT):
                a = slice(t * D, (t + 1) * D)
                dve.wait_ge(s["x1"], t + 1)
                chain(v.tensor_tensor(gv[1][:, a], xs[:, a], G2, ALU.mult))
                dve.wait_ge(s["hss"], 2 * t + 1)
                root_arg(ssum[:, 14 + t:15 + t], ssum[:, 12 + t:13 + t], 1.0 / D, EPS).then_inc(s["xsr"], 1)
                dve.wait_ge(s["hss"], 2 * t + 2)
                chain(v.reciprocal(rsc[:, 6 + t:7 + t], rsc[:, 4 + t:5 + t]))
                settle()
                for q in range(2):
                    a = slice(t * D + q * 512, t * D + (q + 1) * 512)
                    v.scalar_tensor_tensor(out=gv[0][:, a], in0=gv[1][:, a], scalar=rsc[:, 6 + t:7 + t], in1=SH2[:, q * 512:(q + 1) * 512],
                                           op0=ALU.mult, op1=ALU.add).then_inc(s["h2"], 1)

            def rest_1(t):
                a = slice(t * D, (t + 1) * D)
                dve.wait_ge(s["hb0"], t + 1)
                dve.wait_ge(s["h2"], 2 * t + 2)
                chain(v.tensor_tensor(gv[1][:, a], gv[0][:, a], hb[:, 0, t, :], ALU.subtract))

            def part_2(t):
                settle()
                chain(v.tensor_copy(hb[:, 1, t, :], gv[1][:, t * D:(t + 1) * D]))

            def part_3(t):
                settle()
                v.tensor_tensor(hb[:, 2, t, :], gv[1][:, t * D:(t + 1) * D], hb[:, 1, t, :], ALU.subtract).then_inc(s["hb1"], 1)

            rest_1(0)
            part_2(0)
            part_3(0)

            rt_ = rt
            lgt, ex, selt, eqt, tmp, posm, wts = (rt_[:, i * 64:(i + 1) * 64] for i in range(7))
            cum, misc = rt_[:, 448:512], rt_[:, 512:640]
            dve.wait_ge(s["lg_ps"], NT)
            for t in range(NT):
                chain(v.tensor_tensor(lgt[:, t * NE:(t + 1) * NE], B[4 + t][:, 0:NE], rbr, ALU.add))
            settle()
            for t in range(NT):
                chain(v.max(mx[:, t * 8:(t + 1) * 8], lgt[:, t * NE:(t + 1) * NE]))
            settle()
            for t in range(NT):
                e = slice(t * NE, (t + 1) * NE)
                chain(v.tensor_scalar(selt[:, e], lgt[:, e], mx[:, 8 * t + TOPK - 1:8 * t + TOPK], None, ALU.is_gt))
                chain(v.tensor_scalar(eqt[:, e], lgt[:, e], mx[:, 8 * t + TOPK - 1:8 * t + TOPK], None, ALU.is_equal))
                ins = v.tensor_scalar(mx[:, 8 * t + 1:8 * t + 2], mx[:, 8 * t:8 * t + 1], -1.0, None, ALU.mult)
                if t == 0:
                    chain(ins)
                else:
                    ins.then_inc(s["lg_v"], 1)
            settle()
            for t in range(NT):
                e = slice(t * NE, (t + 1) * NE)
                chain(v.tensor_reduce(misc[:, t:t + 1], selt[:, e], AX.X, ALU.add))
                chain(v.tensor_tensor_scan(cum[:, e], ones[:, 0:NE], eqt[:, e], 0.0, ALU.mult, ALU.add))
            settle()
            chain(v.tensor_scalar(misc[:, 0:2], misc[:, 0:2], -1.0, float(TOPK), ALU.mult, ALU.add))
            settle()
            for t in range(NT):
                e = slice(t * NE, (t + 1) * NE)
                chain(v.scalar_tensor_tensor(out=tmp[:, e], in0=cum[:, e], scalar=misc[:, t:t + 1], in1=eqt[:, e], op0=ALU.is_le, op1=ALU.mult))
            settle()
            v.tensor_tensor(selt, selt, tmp, ALU.add).then_inc(s["sel_v"], 1)
            dve.wait_ge(s["sel_v"], 1)
            dve.wait_ge(s["ex_a"], 2)
            chain(v.tensor_tensor(ex, ex, selt, ALU.mult))
            settle()
            chain(v.tensor_reduce(misc[:, 2:4], ex.rearrange("p (t e) -> p t e", t=NT), AX.X, ALU.add))
            settle()
            chain(v.reciprocal(misc[:, 2:4], misc[:, 2:4]))
            settle()
            for t in range(NT):
                e = slice(t * NE, (t + 1) * NE)
                chain(v.tensor_scalar(wts[:, e], ex[:, e], misc[:, 2 + t:3 + t], None, ALU.mult))
            rest_1(1)
            dve.wait_ge(s["pos_ps"], 1)
            chain(v.scalar_tensor_tensor(out=posm, in0=B[5][:, 0:2 * NE], scalar=1.0, in1=selt, op0=ALU.add, op1=ALU.mult))
            nrow, jend, ncol = misc[:, 32:64], misc[:, 64:96], misc[0:NE, 8:9]
            chain(v.tensor_scalar(nrow, B[5][:, 64:64 + NE], float(SLOTS), 1.0, ALU.is_gt, ALU.add))
            chain(v.tensor_scalar(ncol, B[5][0:NE, 96:97], float(SLOTS), 1.0, ALU.is_gt, ALU.add))
            settle()
            chain(v.tensor_scalar(posm, posm, -1.0, None, ALU.add))
            for m in range(2, S // SLOTS):
                chain(v.scalar_tensor_tensor(out=nrow, in0=B[5][:, 64:64 + NE], scalar=float(SLOTS * m), in1=nrow, op0=ALU.is_gt, op1=ALU.add))
                chain(v.scalar_tensor_tensor(out=ncol, in0=B[5][0:NE, 96:97], scalar=float(SLOTS * m), in1=ncol, op0=ALU.is_gt, op1=ALU.add))
                settle()
            v.tensor_copy(misc[0:1, 16:17], ones[0:1, 0:1]).then_inc(s["pos_v"], 1)
            chain(v.memset(ffn[:, S:2 * S], 0.0))
            chain(v.tensor_tensor_scan(jend, ones[:, 0:NE], nrow, 0.0, ALU.mult, ALU.add))
            settle()
            chain(v.tensor_tensor(nrow, jend, nrow, ALU.subtract))
            settle()
            chain(v.tensor_copy(table[0:1, 0:NE], nrow[0:1, :]))
            v.tensor_copy(table[0:1, NE:NE + 1], jend[0:1, NE - 1:NE]).then_inc(s["tab_v"], 1)
            jst, jen, jst64 = misc[0:NE, 9:10], misc[0:NE, 10:11], misc[0:NE, 11:12]
            pqw = ffn[0:NE, 0:512]
            oh, oh1 = ffn[0:NE, 512:512 + JC], ffn[0:NE, 576:576 + JC]
            part_2(1)
            dve.wait_ge(s["jt_ps"], 1)
            settle()
            chain(v.tensor_copy(misc[0:NE, 9:11], B[7][0:NE, 0:2]))
            settle()
            chain(v.tensor_scalar(jst64, jst, float(SLOTS), None, ALU.mult))
            chain(v.tensor_scalar(oh1, const("iota")[0:NE, :], jst, None, ALU.is_ge))
            settle()
            dve.wait_ge(s["hb1"], 1)
            chain(v.scalar_tensor_tensor(out=oh, in0=const("iota")[0:NE, :], scalar=jen, in1=oh1, op0=ALU.is_lt, op1=ALU.mult))
            chain(v.tensor_scalar(pqw[:, 0:S], B[6][0:NE, 0:S], jst64, None, ALU.add))
            v.tensor_copy(pqw[:, S:2 * S], B[6][0:NE, S:2 * S]).then_inc(s["oh_v"], 1)
            part_3(1)
            dve.wait_ge(s["job_ps"], 1)
            for t in range(NT):
                chain(v.scalar_tensor_tensor(out=posj[:, t * JC:(t + 1) * JC], in0=const("iota"), scalar=-float(SLOTS),
                                             in1=B[7][:, 128 + t * JC:128 + (t + 1) * JC], op0=ALU.mult, op1=ALU.add))
            slot_row = const("slot")
            settle()

            def gather_select(j):
                for t in range(NT):
                    ins = v.tensor_scalar(sgat[:, t * SLOTS:(t + 1) * SLOTS], slot_row, posj[:, bass.ds(j + t * JC, 1)], None, ALU.is_equal)
                    if t == 0:
                        chain(ins)
                ins.then_inc(s["selg"], 1)

            gather_select(0)
            v.tensor_copy(table[0:1, NE + 1:], B[7][0:1, 128 + 4 * JC:128 + 5 * JC]).then_inc(s["tab_v"], 1)
            chain(v.tensor_copy(posj[:, 2 * JC:4 * JC], B[7][:, 128 + 2 * JC:128 + 4 * JC]))
            dve.sem_inc(s["gu_v"], 1)
            dve.sem_inc(s["act_v"], 2)
            dve.sem_inc(s["accd"], 4)
            chain(v.memset(swt, 0.0))
            chain(v.memset(ysb, 0.0))
            v.memset(cab, 0.0).then_inc(s["cnt_v"], 1)
            dve.wait_ge(s["y0_ps"], 1)
            dve.wait_ge(s["h2t_ps"], 4)
            for i in range(4):
                chain(v.tensor_copy(acc[:, i * 512:(i + 1) * 512], B[BIAS_BANK[i]][:, :]))
            dve.wait_ge(s["tab_v"], 1)
            J = dve.value_load(table[0:1, NE:NE + 1], min_val=NE, max_val=MAXJ)
            dve.wait_ge(s["bgu_in"], 16)
            settle()
            before_loop = done[0]
            PER = 12
            with dve.Fori(0, J) as j:
                done[0] = 0

                def settle_j():
                    dve.wait_ge(s["vch"], j * PER + (before_loop + done[0]))

                def chain_j(ins):
                    done[0] += 1
                    ins.then_inc(s["vch"], 1)

                e = dve.value_load(table[0:1, bass.ds(j + (NE + 1), 1)], min_val=0, max_val=NE - 1)
                dve.wait_ge(s["gat"], j + 1)
                for t in range(NT):
                    ins = v.tensor_scalar(sgat[:, t * SLOTS:(t + 1) * SLOTS], slot_row, posj[:, bass.ds(j + (t * JC + 1), 1)], None, ALU.is_equal)
                    if t == 0:
                        chain_j(ins)
                ins.then_inc(s["selg"], 1)
                dve.wait_ge(s["ctr"], j + 1)
                for t in range(NT):
                    ins = v.tensor_scalar(swt[:, t * 192 + SLOTS:t * 192 + 2 * SLOTS], slot_row, posj[:, bass.ds(j + t * JC, 1)],
                                          posj[:, bass.ds(j + (2 + t) * JC, 1)], ALU.is_equal, ALU.mult)
                    if t == 0:
                        chain_j(ins)
                ins.then_inc(s["selw"], 1)
                dve.wait_ge(used[GU_UNITS - 1], j + 1)
                v.tensor_copy(gus[:, 512:1024], B[1][:, :]).then_inc(s["gu_v"], 1)
                bias = bgu.rearrange("p (c e) -> p c e", e=NE)
                for q in range(2):
                    bt = B[(2, 5)[q]][:, :].rearrange("p (c x) -> p c x", c=4)
                    gq, uq, sq = (x[:, q * 256:(q + 1) * 256] for x in (tg, tu, ts))
                    g3, u3 = (x.rearrange("p (c x) -> p c x", c=4) for x in (gq, uq))
                    dve.wait_ge(s["trn"], 2 * j + q + 1)
                    if q == 0:
                        dve.wait_ge(s["sg_rdy"], 2 * j + 2)
                    chain_j(v.tensor_tensor(g3, bt[:, :, 0:64], bias[:, 4 * q:4 * q + 4, bass.ds(e, 1)].broadcast_to([P, 4, 64]), ALU.add))
                    chain_j(v.tensor_tensor(u3, bt[:, :, 64:128], bias[:, 8 + 4 * q:12 + 4 * q, bass.ds(e, 1)].broadcast_to([P, 4, 64]), ALU.add))
                    settle_j()
                    v.tensor_scalar(gq, gq, LIMIT, None, ALU.min).then_inc(s["g_rdy"], 1)
                    chain_j(v.tensor_scalar(uq, uq, LIMIT, -LIMIT, ALU.min, ALU.max))
                    settle_j()
                    dve.wait_ge(s["g_rdy"], 2 * j + q + 1)
                    chain_j(v.scalar_tensor_tensor(out=uq, in0=uq, scalar=1.0, in1=gq, op0=ALU.add, op1=ALU.mult))
                    settle_j()
                    dve.wait_ge(s["sg_rdy"], 2 * j + q + 3)
                    v.tensor_tensor(actT[:, q * 256:(q + 1) * 256], uq, sq, ALU.mult).then_inc(s["act_v"], 1)
                    for i in (2 * q, 2 * q + 1):
                        dve.wait_ge(s["sc"], 4 * j + i + 1)
                        dve.wait_ge(s["accd"], 4 * j + i + 4)
                        a = acc[:, i * 512:(i + 1) * 512]
                        v.tensor_tensor(a, a, B[ROW_BANK[i]][:, :], ALU.add).then_inc(s["accd"], 1)
                for _ in range(PER - done[0]):
                    chain_j(v.engine_nop())
            for t in range(NT):
                for i in (2 * t, 2 * t + 1):
                    dve.wait_ge(s["sc"], 4 * J + (i + 1))
                    a = acc[:, i * 512:(i + 1) * 512]
                    v.tensor_tensor(a, a, B[ROW_BANK[i]][:, :], ALU.add).then_inc(s["accd"], 1)
                a = slice(t * D, (t + 1) * D)
                dve.wait_ge(s["accd"], 4 * J + (6 + 2 * t))
                v.tensor_tensor(ffn[:, a], acc[:, a], GF, ALU.mult).then_inc(s["fgain"], 1)
            dve.wait_ge(s["fss"], 2)
            root_arg(ssum[:, 10:12], ssum[:, 8:10], 1.0 / D, EPS).then_inc(s["fsr"], 1)
            dve.wait_ge(s["fss"], 3)
            v.reciprocal(rsc[:, 10:12], rsc[:, 8:10]).then_inc(s["fsr"], 1)
            dve.wait_ge(s["fsr"], 2)
            dve.wait_ge(s["fgain"], NT)
            for t in range(NT):
                for q in range(2):
                    a = slice(t * D + q * 512, t * D + (q + 1) * 512)
                    v.scalar_tensor_tensor(out=xs[:, a], in0=ffn[:, a], scalar=rsc[:, 10 + t:11 + t], in1=xs[:, a],
                                           op0=ALU.mult, op1=ALU.add).then_inc(s["fo"], 1)

        @block.tensor
        def _(pe):
            def sum8(out_ap, lhs, rhs):
                for k in range(KD):
                    ins = pe.matmul(out_ap, lhs(k), rhs(k), start=(k == 0), stop=(k == KD - 1))
                return ins

            def free_bank(use):
                if use >= 2:
                    pe.wait_ge(s[reader(plan[use - 2])], read_count(use - 2))

            def unit(i, k=KD):
                pe.wait_ge(landed[i % MIX_RING], 16 * (i // MIX_RING + 1))
                return slot(i % MIX_RING).rearrange("p (k n) -> p k n", k=k)

            sil3 = silc.rearrange("p (k n) -> p k n", n=32)

            def finish_turn(ins, name):
                ins.then_inc(s["proj"], 1)
                pe.wait_ge(s["proj"], turns(name))
                pe.sem_inc(s["unit_used"], 1)

            def ada_pair(name):
                use = USE[name]
                free_bank(use)
                for n in range(2):
                    w = unit(UNIT_OF[name] + n)
                    for k in range(KD):
                        q = k % 4
                        ins = pe.matmul(B[use % 2][32 * q:32 * q + 32, n * BLK:(n + 1) * BLK], sil3[:, k, :], w[:, k, :],
                                        start=(k < 4), stop=(k >= 4), tile_position=(0, 32 * q))
                    if n == 0:
                        ins.then_inc(s["unit_used"], 1)
                finish_turn(ins, name)

            def shift_scale_columns(q):
                pe.wait_ge(s["a_read"], q + 1)
                for j in range(4 * q, 4 * q + 4):
                    ins = pe.matmul(B[6][:, j:j + 1], rows[:, j * P:(j + 1) * P], ones[:, 0:1], start=True, stop=True)
                if q == 3:
                    ins.then_inc(s["col_ps"], 1)

            pe.wait_ge(s["silu_c"], 1)
            for q in range(4):
                ada_pair(f"c{q}")
                if q == 0:
                    pe.wait_ge(s["const_in"], 16)
                    pe.wait_ge(s["sq_x"], 1)
                    sum8(B[7][:, 0:S], lambda k: ones, lambda k: gv[0][:, k * S:(k + 1) * S]).then_inc(s["ss_x"], 1)
                if q:
                    shift_scale_columns(q - 1)
            shift_scale_columns(3)
            pe.wait_ge(s["wba_in"], 16)
            w8 = wba[:, :].rearrange("p (k n) -> p k n", k=KD)
            for k in range(KD):
                pe.wait_ge(s["h_ok"], k + 1)
                ins = pe.matmul(B[7][0:8, 0:S], w8[:, k, :], hTk[:, k, :], start=(k == 0), stop=(k == KD - 1))
            ins.then_inc(s["ba_ps"], 1)

            def project(name, halves=(0, 1)):
                use = USE[name]
                if halves[0] == 0:
                    free_bank(use)
                w = unit(UNIT_OF[name])
                for c in halves:
                    ins = sum8(B[use % 2][:, c * S:(c + 1) * S], lambda k: w[:, k, c * P:(c + 1) * P], lambda k: hTk[:, k, :])
                if halves[-1] == 1:
                    finish_turn(ins, name)

            def project_v(name, halves=(0, 1)):
                use = USE[name]
                if halves[0] == 0:
                    free_bank(use)
                w = unit(UNIT_OF[name])
                for t in halves:
                    ins = sum8(B[use % 2][:, t * BLK:(t + 1) * BLK], lambda k: hTk[:, k, t * P:(t + 1) * P], lambda k: w[:, k, :])
                if halves[-1] == 1:
                    finish_turn(ins, name)

            def mod_half(i):
                use = USE[f"M{i}"]
                free_bank(use)
                pe.wait_ge(s["row_v"], 2 * (i + 1))
                a = (i % 4) * 512
                pe.matmul(B[use % 2][:, :], ones, rows[:, a:a + 512], start=True, stop=True).then_inc(s["proj"], 1)

            def norm_sums(which):
                pe.wait_ge(s["sq_k"], which + 1)
                for h in range(H):
                    ins = pe.matmul(B[2 + 2 * which + h // 2][:, (h % 2) * S:(h % 2) * S + S], ones, squares[:, h * S:(h + 1) * S],
                                    start=True, stop=True)
                ins.then_inc(s["ss_ps"], 1)

            project("k0")
            pe.wait_ge(s["ba_sb"], 1)
            for t in range(NT):
                ins = pe.matmul(B[7][:, 256 + 8 * t:264 + 8 * t], baT[:, t * P:(t + 1) * P], ident[0:8, 0:8], start=True, stop=True)
            ins.then_inc(s["bat_ps"], 1)
            project("k1")
            project("q0")
            norm_sums(0)
            project("q1")
            pe.wait_ge(s["const2_in"], 16)
            pe.wait_ge(s["g_ok"], 1)
            for i, n in enumerate(("tri", "blockones", "firsthalf", "secondhalf")):
                ins = pe.matmul(B[7][:, 8 * i:8 * i + 8], const(n), g, start=True, stop=True)
            ins.then_inc(s["cum_ps"], 1)
            project("v0")
            norm_sums(1)
            project("v1")

            def token_layout(src, t, bank):
                for h in range(H):
                    ins = pe.transpose(bank[:, h * HD:(h + 1) * HD], src[:, h * S + t * P:h * S + (t + 1) * P], ident)
                ins.then_inc(s["tr_ps"], 1)

            project("z0")
            pe.wait_ge(s["qk_n"], 1)
            pe.wait_ge(s["ss_e"], 1)
            for t in range(NT):
                token_layout(kT, t, B[2 + t])
            project("z1")
            pe.wait_ge(s["ract"], 6)
            pe.wait_ge(s["ss_e"], 2)
            for t in range(NT):
                token_layout(vT, t, B[4 + t])

            def decay_rows(t):
                if t == 1:
                    pe.wait_ge(s["dt_v"], 1)
                    pe.wait_ge(s["egb_a"], 1)
                for h in range(H):
                    c = t * H + h
                    ins = pe.matmul(B[6][:, h * HD:(h + 1) * HD], g[:, c:c + 1].broadcast_to([P, P]), const("tri"), start=True, stop=True)
                ins.then_inc(s["gcb_ps"], 1)
                if t == 1:
                    pe.wait_ge(s["lt_v"], 1)
                else:
                    pe.wait_ge(s["cum_a"], 2)
                    pe.wait_ge(s["cum_v"], 1)
                for h in range(H):
                    c = t * H + h
                    ins = pe.matmul(B[7][:, h * HD:(h + 1) * HD], beta[:, c:c + 1].broadcast_to([P, P]), ident, start=True, stop=True)
                ins.then_inc(s["bb_ps"], 1)

            def products(t):
                if t == 0:
                    pe.wait_ge(s["ktok"], 2 * NT * H)
                    pe.wait_ge(s["ktv"], NT * H)
                    pe.wait_ge(s["qk_n"], 2)
                for i, x in enumerate((kT, qT)):
                    for h in range(H):
                        a = slice(h * S + t * P, h * S + (t + 1) * P)
                        ins = pe.matmul(B[2 + 2 * i + t][:, h * HD:(h + 1) * HD], kT[:, a], x[:, a], start=True, stop=True)
                ins.then_inc(s["kk_ps"], 1)

            decay_rows(0)
            project("mq0")
            products(0)
            project("mq1")
            decay_rows(1)
            products(1)
            project("mk0")
            for t in range(NT):
                pe.wait_ge(s["lt_v"], t + 1)
                for h in range(H):
                    ins = pe.transpose(B[2 + t][:, h * HD:(h + 1) * HD], head(LT, t, h), ident)
                ins.then_inc(s["l_ps"], 1)
            project("mk1")

            def double_a(l, t):
                pe.wait_ge(s["t1_v"], 2 * NT) if l == 1 else pe.wait_ge(s["tt_v"], (l - 2) * NT + t + 1)
                for h in range(H):
                    ins = pe.matmul(B[2 + t][:, h * HD:(h + 1) * HD], head(LT, t, h), head(T, t, h), start=True, stop=True)
                ins.then_inc(s["a_ps"], 1)

            def double_x(l, t):
                pe.wait_ge(s["m_v"], (l - 1) * NT + t + 1)
                if l == 1:
                    pe.wait_ge(s["qk_v"], t + 1)
                if l < 5:
                    for h in range(H):
                        pe.matmul(B[4 + t][:, h * HD:(h + 1) * HD], head(TT, t, h), head(M, t, h), start=True, stop=True)
                for h in range(H):
                    ins = pe.matmul(B[6 + t][:, h * HD:(h + 1) * HD], head(M, t, h), head(TT, t, h), start=True, stop=True)
                ins.then_inc(s["x_ps"], 1)

            def step(names):
                for name in names.split():
                    halves = {"a": (0,), "b": (1,)}.get(name[-1], (0, 1))
                    name = name.rstrip("ab")
                    if name[0] == "M":
                        mod_half(int(name[-1]))
                    elif name[:2] == "mv":
                        project_v(name, halves)
                    else:
                        project(name, halves)

            between = (("M0 mv0a", "mv0b"), ("M1 mv1a", "mv1b"), ("M2 g0a", "g0b"), ("M3 g1a", "g1b"), ("M4 g2a", "g2b"))
            for l in range(1, 6):
                for t in range(NT):
                    double_a(l, t)
                step(between[l - 1][0])
                for t in range(NT):
                    double_x(l, t)
                step(between[l - 1][1])

            for t in range(NT):
                pe.wait_ge(s["tt_v"], 4 * NT + t + 1)
                for h in range(H):
                    pe.matmul(B[2 + t][:, h * HD:(h + 1) * HD], head(TT, t, h), head(vb, t, h), start=True, stop=True)
                for h in range(H):
                    ins = pe.matmul(B[6 + t][:, h * HD:(h + 1) * HD], head(kbg, t, h), head(TT, t, h), start=True, stop=True)
                ins.then_inc(s["uw_ps"], 1)
            step("M5 g3")

            for n in range(4):
                t, hf = n // 2, n % 2
                r = slice(CHUNK * hf, CHUNK * hf + CHUNK)
                at = (0, CHUNK * hf)
                vnb = vn[:, hf * TW:(hf + 1) * TW]
                if n in (1, 2):
                    step(f"M{5 + n}")
                if n == 0:
                    pe.wait_ge(s["rope_v"], 2)
                q0 = n * S
                free_bank(USE[f"s{n}"])
                sc = bank("s", n)
                pe.matmul(sc[:, 0:P], mq[:, q0:q0 + P], mk[:, q0:q0 + P], start=True, stop=True)
                pe.matmul(sc[:, P:3 * P], mq[:, q0 + P:q0 + 2 * P], mk[:, q0:q0 + S], start=True, stop=True).then_inc(s["sc_ps"], 1)
                if n == 0:
                    pe.wait_ge(s["uw_a"], 4)
                else:
                    pe.wait_ge(s["s_v"], n)
                    for h in range(H):
                        ins = pe.matmul(B[6][r, h * HD:(h + 1) * HD], head(wT, t, h)[:, r], state[:, h * HD:(h + 1) * HD],
                                        start=True, stop=True, tile_position=at)
                    ins.then_inc(s["ws_ps"], 1)
                project(f"g{4 + n}")
                p = prob[:, (n % 2) * 768:(n % 2) * 768 + 384]
                pt = prob[:, (n % 2) * 768 + 384:(n % 2) * 768 + 768]
                pe.wait_ge(s["pn_v"], 2 * n + 2)
                free_bank(USE[f"t{n}"])
                for i in range(3):
                    ins = pe.transpose(bank("t", n)[:, i * P:(i + 1) * P], p[:, i * P:(i + 1) * P], ident)
                ins.then_inc(s["pt_ps"], 1)
                pe.wait_ge(s["vn_v"], n + 1)
                for h in range(H):
                    o = B[2 + t][r, h * HD:(h + 1) * HD]
                    if n:
                        pe.matmul(o, head(qd, t, h)[:, r], state[:, h * HD:(h + 1) * HD], start=True, stop=False, tile_position=at)
                    ins = pe.matmul(o, head(QK, t, h)[:, r], vnb[:, h * HD:(h + 1) * HD], start=(n == 0), stop=True, tile_position=at)
                ins.then_inc(s["o_ps"], 1)
                if n < 3:
                    for h in range(H):
                        ins = pe.matmul(B[7][:, h * HD:(h + 1) * HD], head(ktl, t, h), vnb[:, h * HD:(h + 1) * HD], start=True, stop=True)
                    ins.then_inc(s["st_ps"], 1)
                pe.wait_ge(s["pt_a"], n + 1)
                free_bank(USE[f"o{n}"])
                ob = bank("o", n)
                pe.matmul(ob[:, 0:P], head(mv, 0, n), pt[:, 0:P], start=True, stop=True)
                pe.matmul(ob[:, P:S], head(mv, 0, n), pt[:, P:2 * P], start=True, stop=False)
                pe.matmul(ob[:, P:S], head(mv, 1, n), pt[:, 2 * P:3 * P], start=False, stop=True).then_inc(s["ob_ps"], 1)

            def branch(i, j):
                w, o = unit(BR0 + i + 2 * (j // 4), H), (oaT, obT)[i]
                for k in range(H):
                    ins = pe.matmul(B[2 + j % 2][:, i * S:(i + 1) * S], w[:, k, (j % 4) * P:(j % 4 + 1) * P],
                                    o[:, k * S:(k + 1) * S], start=(k == 0), stop=(k == H - 1))
                return ins

            pe.wait_ge(s["ob_a"], H)
            pe.wait_ge(s["o_a"], 4)
            branch(1, 0)
            branch(1, 1)
            for t in range(NT):
                pe.wait_ge(s["ro_v"], 1 + H * (t + 1))
                for h in range(H):
                    ins = pe.transpose(B[4 + t][:, h * HD:(h + 1) * HD], head(otok, t, h), ident)
                ins.then_inc(s["ot_ps"], 1)
            pe.wait_ge(s["ot_ps"], 2)
            pe.sem_inc(s["scratch_dead"], 1)
            pe.wait_ge(s["oa_v"], 2)
            for j in range(KD):
                if j >= 2:
                    pe.wait_ge(s["ya_v"], j - 1)
                    branch(1, j)
                branch(0, j).then_inc(s["ya_ps"], 1)
                if j % 4 == 3:
                    pe.wait_ge(s["ya_ps"], j + 1)
                    pe.sem_inc(s["unit_used"], 2)
            for n in range(4):
                w = unit(O0 + n)
                if n >= 2:
                    pe.wait_ge(s["mix_q"], n - 1)
                for t in range(NT):
                    for k in range(KD):
                        if n == 0 and t == 0:
                            pe.wait_ge(s["ya_v"], k + 1)
                        ins = pe.matmul(B[n % 2][:, t * BLK:(t + 1) * BLK], hTk[:, k, t * P:(t + 1) * P], w[:, k, :],
                                        start=(k == 0), stop=(k == KD - 1))
                ins.then_inc(s["mix_ps"], 1)
                pe.wait_ge(s["mix_ps"], n + 1)
                pe.sem_inc(s["unit_used"], 1)

            def keep_busy(n, b=6):
                for _ in range(n):
                    pe.matmul(B[b][:, :P], ident, ident, start=True, stop=True)

            keep_busy(34)
            pe.wait_ge(s["mix_q"], 4)
            pe.wait_ge(s["x2_in"], 64)
            w3 = wrt[:, :].rearrange("p (k n) -> p k n", k=KD)
            for t in range(NT):
                for q in range(2):
                    pe.wait_ge(s["h2"], 2 * t + q + 1)
                    for k in range(4 * q, 4 * q + 4):
                        ins = pe.transpose(B[2 * t + q][:, (k % 4) * P:(k % 4 + 1) * P], gv[0][:, t * D + k * P:t * D + (k + 1) * P], ident)
                    ins.then_inc(s["h2t_ps"], 1)
                for q in range(2):
                    pe.wait_ge(s["h2t"], 2 * t + q + 1)
                    for k in range(4 * q, 4 * q + 4):
                        ins = pe.matmul(B[4 + t][:, 0:NE], hTk[:, k, t * P:(t + 1) * P], w3[:, k, :], start=(k == 0), stop=(k == KD - 1))
                ins.then_inc(s["lg_ps"], 1)
            selt, posm, wts = rt[:, 128:192], rt[:, 320:384], rt[:, 384:448]
            keep_busy(14)
            pe.wait_ge(s["sel_v"], 1)
            pe.matmul(B[5][:, 0:NE], const("before"), selt[:, 0:NE], start=True, stop=True)
            pe.matmul(B[5][:, NE:2 * NE], const("before"), selt[:, NE:2 * NE], start=True, stop=False)
            pe.matmul(B[5][:, NE:2 * NE], ones, selt[:, 0:NE], start=False, stop=True)
            for t in range(NT):
                pe.matmul(B[5][:, 2 * NE:3 * NE], ones, selt[:, t * NE:(t + 1) * NE], start=(t == 0), stop=(t == 1))
            for t in range(NT):
                ins = pe.matmul(B[5][0:NE, 96:97], selt[:, t * NE:(t + 1) * NE], ones[:, 0:1], start=(t == 0), stop=(t == 1))
            ins.then_inc(s["pos_ps"], 1)
            keep_busy(4)
            pe.wait_ge(s["pos_v"], 1)
            ncol = rt[0:NE, 520:521]
            pe.matmul(B[7][0:NE, 0:1], const("ntri32")[0:NE, :], ncol, start=True, stop=True)
            pe.matmul(B[7][0:NE, 1:2], const("tri32")[0:NE, :], ncol, start=True, stop=True)
            for i, x in enumerate((posm, wts)):
                for t in range(NT):
                    ins = pe.transpose(B[6][0:NE, (2 * i + t) * P:(2 * i + t + 1) * P], x[:, t * NE:(t + 1) * NE], ident)
            ins.then_inc(s["jt_ps"], 1)
            keep_busy(8, 4)
            pe.wait_ge(s["oh_v"], 1)
            pqw, oh = ffn[0:NE, 0:512], ffn[0:NE, 512:512 + JC]
            for i in range(4):
                pe.matmul(B[7][:, 128 + i * JC:128 + (i + 1) * JC], pqw[:, i * P:(i + 1) * P], oh, start=True, stop=True)
            pe.matmul(B[7][0:1, 128 + 4 * JC:128 + 5 * JC], const("expert")[0:NE, :], oh, start=True, stop=True).then_inc(s["job_ps"], 1)
            pe.wait_ge(s["bdn_in"], 16)

            def bias_rows(t):
                for n in range(2):
                    ins = pe.matmul(B[BIAS_BANK[2 * t + n]][:, :], ffn[:, S + t * P:S + (t + 1) * P], bdn[:, n * 512:(n + 1) * 512], start=True, stop=True)
                return ins

            def gather():
                for c in range(KD):
                    for i in range(3):
                        for t in range(NT):
                            ins = pe.matmul(B[3][:, c * SLOTS:(c + 1) * SLOTS], hb[:, i, t, c * P:(c + 1) * P],
                                            sgat[:, t * SLOTS:(t + 1) * SLOTS], start=(i == 0 and t == 0), stop=(i == 2 and t == 1))
                ins.then_inc(s["gat"], 1)

            bias_rows(0)
            pe.wait_ge(s["hb1"], 2)
            pe.wait_ge(s["selg"], 1)
            gather()
            bias_rows(1).then_inc(s["y0_ps"], 1)
            pe.wait_ge(s["cnt_v"], 1)
            pe.wait_ge(s["tab_v"], 1)
            def weights(group, r, u):
                g = r * UPE + u
                pe.wait_ge(landed[g % RING], group * (16 * LAPS) + landed_count(g))
                return slot(g % RING)

            def job(j, group, r):
                pe.wait_ge(s["xg_a"], j + 1)
                pe.wait_ge(s["gu_a"], j + 1)
                pe.wait_ge(s["gu_v"], j + 1)
                pe.wait_ge(s["accd"], 4 * j + 4)
                for u in range(GU_UNITS):
                    w = weights(group, r, u)
                    for n in range(2):
                        for half in range(2):
                            ins = pe.matmul(B[n][64 * half:64 * half + 64, :], xg[:, u * SLOTS:(u + 1) * SLOTS],
                                            w[:, half * F + n * 512:half * F + (n + 1) * 512], start=(u == 0), stop=(u == GU_UNITS - 1),
                                            tile_position=(0, 64 * half))
                    ins.then_inc(used[u], 1)
                pe.wait_ge(s["selg"], j + 2)
                pe.wait_ge(s["c_a"], j + 1)
                gather()
                for q in range(2):
                    if q == 0:
                        pe.wait_ge(s["gu_a"], j + 2)
                        pe.wait_ge(s["act_v"], 2 * j + 2)
                    else:
                        pe.wait_ge(s["gu_v"], j + 2)
                    for c in range(4):
                        ins = pe.transpose(B[(2, 5)[q]][:, c * P:(c + 1) * P], gus[:, (4 * q + c) * P:(4 * q + c + 1) * P], ident)
                    ins.then_inc(s["trn"], 1)
                pe.wait_ge(s["y_a"], j + 1)
                pe.wait_ge(s["c_a"], j + 1)
                for i in range(4):
                    pe.matmul(B[ROW_BANK[i]][:, :], cab[:, i * P:(i + 1) * P], ysb, start=True, stop=True).then_inc(s["sc"], 1)
                pe.wait_ge(s["selw"], j + 1)
                pe.wait_ge(s["xg_a"], j + 2)
                for t in range(NT):
                    for half in range(2):
                        ins = pe.transpose(B[3][:, (2 * t + half) * P:(2 * t + half + 1) * P],
                                           swt[:, t * 192 + 64 - 64 * half:t * 192 + 192 - 64 * half], ident)
                ins.then_inc(s["ctr"], 1)
                for f in range(KF):
                    u = GU_UNITS + f // 2
                    if f == 0:
                        pe.wait_ge(s["act_v"], 2 * j + 3)
                    if f == 4:
                        pe.wait_ge(s["act_v"], 2 * j + 4)
                    w = weights(group, r, u)
                    for half in range(2):
                        ins = pe.matmul(B[4][64 * half:64 * half + 64, :], actT[:, f * SLOTS:(f + 1) * SLOTS],
                                        w[:, (f % 2) * D + half * 512:(f % 2) * D + (half + 1) * 512], start=(f == 0), stop=(f == KF - 1),
                                        tile_position=(0, 64 * half))
                    if f % 2:
                        ins.then_inc(used[u], 1)

            pe.sem_inc(s["ctr"], 1)
            with pe.Fori(0, NE // GROUP) as n:
                e0 = n * GROUP
                for r in range(GROUP):
                    first = pe.value_load(table[0:1, bass.ds(e0 + r, 1)], min_val=0, max_val=MAXJ)
                    end = pe.value_load(table[0:1, bass.ds(e0 + (r + 1), 1)], min_val=1, max_val=MAXJ)
                    with pe.Fori(first, end) as j:
                        job(j, n, r)
            J = pe.value_load(table[0:1, NE:NE + 1], min_val=NE, max_val=MAXJ)
            pe.wait_ge(s["y_a"], J + 1)
            pe.wait_ge(s["c_a"], J + 1)
            pe.wait_ge(s["accd"], 4 * J + 4)
            for i in range(4):
                pe.matmul(B[ROW_BANK[i]][:, :], cab[:, i * P:(i + 1) * P], ysb, start=True, stop=True).then_inc(s["sc"], 1)


def kernel(**inputs):
    import concourse.bacc as bacc
    from concourse.bass_utils import run_bass_kernel_spmd

    def arr(n):
        return np.asarray(inputs[n])

    def columns(v, n):
        return np.ascontiguousarray(v.reshape(n, P).T)

    x = arr("x")[0]
    data = {
        "x": x, "xT": np.ascontiguousarray(x.T),
        "columns": np.concatenate([
            columns(arr("g_pre_mix")[0], KD), columns(arr("b_ada")[0][:2 * D], 2 * KD),
            arr("conv_w")[0].reshape(TAPS, 12, P).transpose(2, 1, 0).reshape(P, 12 * TAPS),
            columns(arr("g_dn_out")[0], 1), columns(arr("c")[0], KD)], 1),
        "w_ada": arr("w_ada")[0], "b_ada": arr("b_ada"), "w_in": arr("w_in")[0],
        "g_post_mix": arr("g_post_mix"), "g_pre_ffn": arr("g_pre_ffn"), "g_post_ffn": arr("g_post_ffn"),
        "a_log": arr("a_log"), "dt_bias": arr("dt_bias"),
        "w_br_a": arr("w_br_a")[0], "w_br_b": arr("w_br_b")[0], "w_o": arr("w_o")[0],
        "w_router": arr("w_router")[0], "b_router": arr("b_router"),
        "w_gu": arr("w_gu")[0], "b_gu": arr("b_gu")[0].reshape(NE, 2 * F // P, P).transpose(2, 1, 0).reshape(P, -1), "w_down": arr("w_down")[0], "b_down": arr("b_down")[0],
        "cst": shape_constants(),
    }
    nc = bacc.Bacc("TRN2", target_bir_lowering=False, num_devices=1)
    arrays, A = {}, {}
    for n, a in data.items():
        a = np.ascontiguousarray(a)
        arrays[f"in_{n}"] = a
        A[n] = nc.dram_tensor(f"in_{n}", a.shape, mybir.dt.from_np(a.dtype), kind="ExternalInput").ap()
    out = nc.dram_tensor("out_0", (S, D), F32, kind="ExternalOutput").ap()
    build(nc, A, out)
    r = run_bass_kernel_spmd(nc, [arrays], core_ids=[0])
    return r.results[0]["out_0"].reshape(1, S, D)
```
